# Optimizing a Trainium2 kernel written in Bass

```python
import math
import jax, jax.numpy as jnp
from jax import lax
import numpy as np

D_MODEL = 1024
BATCH = 1
SEQ = 512
DEPTH = 1

SB_HEADS = 8
SB_HEAD_DIM = 64
SB_WIDTH = SB_HEADS * SB_HEAD_DIM
MLA_HEADS = 8
MLA_NOPE_DIM = 64
MLA_ROPE_DIM = 32
MLA_V_DIM = 64
MLA_Q_RANK = 384
MLA_KV_RANK = 256
MLA_WIDTH = MLA_HEADS * MLA_V_DIM
MLA_QK_DIM = MLA_NOPE_DIM + MLA_ROPE_DIM

Q_BLOCK = 128
ROPE_BASE = 10000.0
EPS = 1e-6

SPLITS = (SB_WIDTH, SB_WIDTH, SB_WIDTH, SB_WIDTH,
          MLA_Q_RANK, MLA_KV_RANK, MLA_ROPE_DIM, MLA_WIDTH,
          D_MODEL, D_MODEL)
IN_WIDTH = int(sum(SPLITS))
SPLIT_POINTS = tuple(int(v) for v in np.cumsum(SPLITS)[:-1])


def rmsnorm(x, g):
    xf = x.astype(jnp.float32)
    y = xf * lax.rsqrt(jnp.mean(xf * xf, axis=-1, keepdims=True) + EPS)
    return (y * g.astype(jnp.float32)).astype(x.dtype)

def rope(x, positions):
    r = x.shape[-1]
    inv_freq = ROPE_BASE ** (-jnp.arange(0, r, 2, dtype=jnp.float32) / r)
    ang = positions.astype(jnp.float32)[:, :, None, None] * inv_freq
    cos, sin = jnp.cos(ang), jnp.sin(ang)
    xf = x.astype(jnp.float32)
    x1, x2 = xf[..., : r // 2], xf[..., r // 2:]
    return jnp.concatenate([x1 * cos - x2 * sin, x1 * sin + x2 * cos], axis=-1)

def to_blocks(t):
    b, h, s, d = t.shape
    return t.reshape(b, h, s // Q_BLOCK, Q_BLOCK, d).transpose(2, 0, 1, 3, 4)

def from_blocks(t):
    n, b, h, q, d = t.shape
    return t.transpose(1, 2, 0, 3, 4).reshape(b, h, n * q, d)

def stick_breaking_attention(q, k, v):
    s_len = k.shape[2]
    scale = 1.0 / math.sqrt(q.shape[-1])
    key_idx = jnp.arange(s_len)

    def block(args):
        qb, i = args
        z = jnp.einsum('bhqd,bhkd->bhqk', qb, k) * scale
        q_idx = i * Q_BLOCK + jnp.arange(Q_BLOCK)
        strict = key_idx[None, :] < q_idx[:, None]
        log_one_minus = jnp.where(strict, jax.nn.log_sigmoid(-z), 0.0)
        suffix = lax.cumsum(log_one_minus, axis=3, reverse=True) - log_one_minus
        w = jnp.where(strict, jnp.exp(jax.nn.log_sigmoid(z) + suffix), 0.0)
        return jnp.einsum('bhqk,bhkd->bhqd', w, v)

    n_blk = s_len // Q_BLOCK
    out = lax.map(block, (to_blocks(q), jnp.arange(n_blk)))
    return from_blocks(out)

def latent_attention(q_nope, q_pe, k_nope, k_pe, v):
    s_len = k_nope.shape[2]
    scale = 1.0 / math.sqrt(MLA_QK_DIM)
    key_idx = jnp.arange(s_len)

    def block(args):
        qn, qp, i = args
        sc = (jnp.einsum('bhqd,bhkd->bhqk', qn, k_nope)
              + jnp.einsum('bhqr,bkr->bhqk', qp, k_pe)) * scale
        q_idx = i * Q_BLOCK + jnp.arange(Q_BLOCK)
        causal = key_idx[None, :] <= q_idx[:, None]
        p = jax.nn.softmax(jnp.where(causal, sc, -jnp.inf), axis=-1)
        return jnp.einsum('bhqk,bhkd->bhqd', p, v)

    n_blk = s_len // Q_BLOCK
    out = lax.map(block, (to_blocks(q_nope), to_blocks(q_pe), jnp.arange(n_blk)))
    return from_blocks(out)

def split_heads(t, h):
    b, s, w = t.shape
    return t.reshape(b, s, h, w // h).transpose(0, 2, 1, 3)

def merge_heads(t):
    b, h, s, d = t.shape
    return t.transpose(0, 2, 1, 3).reshape(b, s, h * d)

def first_inputs(seed: int = 0) -> dict:
    key = jax.random.key(seed)
    ks = jax.random.split(key, 16)
    f32 = jnp.float32

    def nrm(k, shape, fan_in, mult=1.0):
        return jax.random.normal(k, shape, f32) * (mult * fan_in ** -0.5)

    x = jax.random.normal(ks[0], (BATCH, SEQ, D_MODEL), f32)
    c = jax.random.normal(ks[1], (BATCH, D_MODEL), f32)
    positions = jnp.broadcast_to(jnp.arange(SEQ, dtype=jnp.int32), (BATCH, SEQ))
    w_ada = nrm(ks[2], (DEPTH, D_MODEL, 3 * D_MODEL), D_MODEL, 0.2)
    b_ada = jax.random.normal(ks[3], (DEPTH, 3 * D_MODEL), f32) * 0.02
    norm_gain = 1.0 + 0.02 * jax.random.normal(ks[4], (DEPTH, D_MODEL), f32)
    w_in = nrm(ks[5], (DEPTH, D_MODEL, IN_WIDTH), D_MODEL)
    q_norm_gain = 1.0 + 0.02 * jax.random.normal(ks[6], (DEPTH, MLA_Q_RANK), f32)
    w_uq = nrm(ks[7], (DEPTH, MLA_Q_RANK, MLA_HEADS * MLA_QK_DIM), MLA_Q_RANK)
    kv_norm_gain = 1.0 + 0.02 * jax.random.normal(ks[8], (DEPTH, MLA_KV_RANK), f32)
    w_ukv = nrm(ks[9], (DEPTH, MLA_KV_RANK, MLA_HEADS * (MLA_NOPE_DIM + MLA_V_DIM)), MLA_KV_RANK)
    w_branch_a = nrm(ks[10], (DEPTH, SB_WIDTH, D_MODEL), SB_WIDTH)
    w_branch_b = nrm(ks[11], (DEPTH, MLA_WIDTH, D_MODEL), MLA_WIDTH)
    w_out = nrm(ks[12], (DEPTH, D_MODEL, D_MODEL), D_MODEL)
    final_norm_gain = 1.0 + 0.02 * jax.random.normal(ks[13], (D_MODEL,), f32)
    return {"x": x, "c": c, "positions": positions, "w_ada": w_ada, "b_ada": b_ada,
            "norm_gain": norm_gain, "w_in": w_in, "q_norm_gain": q_norm_gain, "w_uq": w_uq,
            "kv_norm_gain": kv_norm_gain, "w_ukv": w_ukv, "w_branch_a": w_branch_a,
            "w_branch_b": w_branch_b, "w_out": w_out, "final_norm_gain": final_norm_gain}

def first_block(x, c, positions, w_ada, b_ada, norm_gain, w_in, q_norm_gain, w_uq,
              kv_norm_gain, w_ukv, w_branch_a, w_branch_b, w_out, final_norm_gain):
    b, s, _ = x.shape
    f32 = jnp.float32
    for l in range(DEPTH):
        mod = c @ w_ada[l] + b_ada[l]
        shift, scale, gate = jnp.split(mod, 3, axis=-1)
        h = rmsnorm(x, norm_gain[l]) * (1.0 + scale[:, None, :]) + shift[:, None, :]

        proj = h @ w_in[l]
        (sb_q, sb_k, sb_v, sb_z, c_q, c_kv, k_rot, mla_z, g_a, g_b) = jnp.split(proj, SPLIT_POINTS, axis=-1)

        o_a = stick_breaking_attention(split_heads(sb_q, SB_HEADS).astype(f32),
                                       split_heads(sb_k, SB_HEADS).astype(f32),
                                       split_heads(sb_v, SB_HEADS).astype(f32))
        o_a = merge_heads(o_a).astype(x.dtype)
        y_a = (o_a * jax.nn.silu(sb_z)) @ w_branch_a[l]

        q = (rmsnorm(c_q, q_norm_gain[l]) @ w_uq[l]).reshape(b, s, MLA_HEADS, MLA_QK_DIM)
        q_nope = q[..., :MLA_NOPE_DIM].astype(f32)
        q_pe = rope(q[..., MLA_NOPE_DIM:], positions)
        kv = (rmsnorm(c_kv, kv_norm_gain[l]) @ w_ukv[l]).reshape(b, s, MLA_HEADS, MLA_NOPE_DIM + MLA_V_DIM)
        k_nope = kv[..., :MLA_NOPE_DIM].astype(f32)
        v_b = kv[..., MLA_NOPE_DIM:].astype(f32)
        k_pe = rope(k_rot[:, :, None, :], positions)[:, :, 0, :]
        o_b = latent_attention(q_nope.transpose(0, 2, 1, 3), q_pe.transpose(0, 2, 1, 3),
                               k_nope.transpose(0, 2, 1, 3), k_pe, v_b.transpose(0, 2, 1, 3))
        o_b = merge_heads(o_b).astype(x.dtype)
        y_b = (o_b * jax.nn.silu(mla_z)) @ w_branch_b[l]

        merged = jax.nn.sigmoid(g_a) * y_a + jax.nn.sigmoid(g_b) * y_b
        x = x + gate[:, None, :] * (merged @ w_out[l])
    return rmsnorm(x, final_norm_gain)


PLE_DIM = 256
MIX_WIDTH = D_MODEL
GDN_WIDTH = D_MODEL // 2
GDN_HEAD_DIM = 128
GDN_HEADS = GDN_WIDTH // GDN_HEAD_DIM
FOX_WIDTH = MIX_WIDTH - GDN_WIDTH
FOX_HEAD_DIM = 64
FOX_HEADS = FOX_WIDTH // FOX_HEAD_DIM
CONV_WIDTH = 4
CHUNK = 64
D_FF = -(-8 * D_MODEL // (3 * 256)) * 256

IN_SIZES = [3 * GDN_WIDTH, GDN_WIDTH, GDN_HEADS, GDN_HEADS, 3 * FOX_WIDTH, FOX_HEADS]
D_IN = sum(IN_SIZES)
IN_SPLITS = [sum(IN_SIZES[:i + 1]) for i in range(len(IN_SIZES) - 1)]


def rmsnorm_2(x, w):
    xf = x.astype(jnp.float32)
    y = xf * lax.rsqrt(jnp.mean(xf * xf, axis=-1, keepdims=True) + EPS)
    return (y * w.astype(jnp.float32)).astype(x.dtype)

def l2norm(x):
    return x * lax.rsqrt(jnp.sum(x * x, axis=-1, keepdims=True) + EPS)

def causal_depthwise_conv(x, w):
    c = x.shape[-1]
    return lax.conv_general_dilated(
        x, w.astype(x.dtype)[:, None, :], window_strides=(1,),
        padding=[(CONV_WIDTH - 1, 0)], dimension_numbers=('NWC', 'WIO', 'NWC'),
        feature_group_count=c)

def gated_delta_rule(q, k, v, g, beta):
    b, s, h, dk = q.shape
    dv = v.shape[-1]
    n = s // CHUNK

    def chunk(t):
        return jnp.moveaxis(t.reshape((b, n, CHUNK, h) + t.shape[3:]), 3, 2)

    q = chunk(q * (dk ** -0.5))
    k, v, g, beta = chunk(k), chunk(v), chunk(g), chunk(beta)
    gc = jnp.cumsum(g, axis=-1)
    lower = jnp.tril(jnp.ones((CHUNK, CHUNK), bool))
    strict = jnp.tril(jnp.ones((CHUNK, CHUNK), bool), -1)
    diff = gc[..., :, None] - gc[..., None, :]
    decay = jnp.where(lower, jnp.exp(jnp.where(lower, diff, 0.0)), 0.0)
    kb = k * beta[..., None]
    vb = v * beta[..., None]
    kk = jnp.einsum('bnhid,bnhjd->bnhij', kb, k) * decay
    a_mat = jnp.where(strict, kk, 0.0) + jnp.eye(CHUNK, dtype=kk.dtype)
    rhs = jnp.concatenate([vb, kb * jnp.exp(gc)[..., None]], axis=-1)
    sol = lax.linalg.triangular_solve(a_mat, rhs, left_side=True, lower=True, unit_diagonal=True)
    u, w = sol[..., :dv], sol[..., dv:]
    qk = jnp.where(lower, jnp.einsum('bnhid,bnhjd->bnhij', q, k) * decay, 0.0)

    def step(state, xs):
        q_c, k_c, u_c, w_c, gc_c, qk_c = xs
        v_new = u_c - jnp.einsum('bhcd,bhde->bhce', w_c, state)
        o = (jnp.einsum('bhcd,bhde->bhce', q_c * jnp.exp(gc_c)[..., None], state)
             + jnp.einsum('bhij,bhje->bhie', qk_c, v_new))
        g_last = gc_c[..., -1]
        k_dec = k_c * jnp.exp(g_last[..., None] - gc_c)[..., None]
        state = state * jnp.exp(g_last)[..., None, None] + jnp.einsum('bhcd,bhce->bhde', k_dec, v_new)
        return state, o

    xs = tuple(jnp.moveaxis(t, 1, 0) for t in (q, k, u, w, gc, qk))
    state0 = jnp.zeros((b, h, dk, dv), jnp.float32)
    _, o = lax.scan(step, state0, xs)
    o = jnp.moveaxis(jnp.moveaxis(o, 0, 1), 2, 3)
    return o.reshape(b, s, h, dv)

def forgetting_attention(q, k, v, log_f):
    b, s, h, d = q.shape
    scale = d ** -0.5
    c = jnp.cumsum(log_f.astype(jnp.float32), axis=1).transpose(0, 2, 1)
    q, k, v = (t.transpose(0, 2, 1, 3) for t in (q, k, v))
    outs = []
    for blk in range(s // Q_BLOCK):
        q0, q1 = blk * Q_BLOCK, (blk + 1) * Q_BLOCK
        logits = jnp.einsum('bhqd,bhkd->bhqk', q[:, :, q0:q1], k[:, :, :q1],
                            preferred_element_type=jnp.float32) * scale
        logits = logits + c[:, :, q0:q1, None] - c[:, :, None, :q1]
        causal = jnp.arange(q0, q1)[:, None] >= jnp.arange(q1)[None, :]
        logits = jnp.where(causal, logits, -jnp.inf)
        prob = jax.nn.softmax(logits, axis=-1)
        outs.append(jnp.einsum('bhqk,bhkd->bhqd', prob.astype(v.dtype), v[:, :, :q1]))
    o = jnp.concatenate(outs, axis=2)
    return o.transpose(0, 2, 1, 3)

def second_inputs(seed: int = 0) -> dict:
    key = jax.random.key(seed)
    ks = jax.random.split(key, 20)
    f32 = jnp.float32
    nrm = lambda k, shape, s: jax.random.normal(k, shape, f32) * s
    gain = lambda k, shape: 1.0 + 0.1 * jax.random.normal(k, shape, f32)
    dt = jnp.exp(jax.random.uniform(ks[5], (DEPTH, GDN_HEADS), f32) * (np.log(0.1) - np.log(0.001)) + np.log(0.001))
    dt_bias = dt + jnp.log(-jnp.expm1(-dt))
    return {
        'x': nrm(ks[0], (BATCH, SEQ, D_MODEL), 1.0),
        'p': nrm(ks[1], (DEPTH, BATCH, SEQ, PLE_DIM), 1.0),
        'attn_norm_w': gain(ks[2], (DEPTH, D_MODEL)),
        'w_in': nrm(ks[3], (DEPTH, D_MODEL, D_IN), D_MODEL ** -0.5),
        'conv_w': nrm(ks[4], (DEPTH, CONV_WIDTH, 3 * GDN_WIDTH), CONV_WIDTH ** -0.5),
        'a_log': jnp.log(jax.random.uniform(ks[6], (DEPTH, GDN_HEADS), f32, 1.0, 16.0)),
        'dt_bias': dt_bias,
        'gdn_norm_w': gain(ks[7], (DEPTH, GDN_HEAD_DIM)),
        'fox_f_bias': 3.0 + 0.5 * jax.random.normal(ks[8], (DEPTH, FOX_HEADS), f32),
        'w_out': nrm(ks[9], (DEPTH, MIX_WIDTH, D_MODEL), MIX_WIDTH ** -0.5),
        'ffn_norm_w': gain(ks[10], (DEPTH, D_MODEL)),
        'w_gate_up': nrm(ks[11], (DEPTH, D_MODEL, 2 * D_FF), D_MODEL ** -0.5),
        'w_down': nrm(ks[12], (DEPTH, D_FF, D_MODEL), D_FF ** -0.5),
        'ple_norm_w': gain(ks[13], (DEPTH, D_MODEL)),
        'w_ple_gate': nrm(ks[14], (DEPTH, D_MODEL, D_MODEL), D_MODEL ** -0.5),
        'w_ple_proj': nrm(ks[15], (DEPTH, PLE_DIM, D_MODEL), PLE_DIM ** -0.5),
        'final_norm_w': gain(ks[16], (D_MODEL,)),
    }

def second_block(x, p, attn_norm_w, w_in, conv_w, a_log, dt_bias, gdn_norm_w, fox_f_bias, w_out,
              ffn_norm_w, w_gate_up, w_down, ple_norm_w, w_ple_gate, w_ple_proj, final_norm_w):
    b, s, _ = x.shape
    f32 = jnp.float32
    h = x
    for i in range(DEPTH):
        xn = rmsnorm_2(h, attn_norm_w[i])
        proj = xn @ w_in[i]
        g_qkv, g_z, g_a, g_b, f_qkv, f_f = jnp.split(proj, IN_SPLITS, axis=-1)

        g_qkv = jax.nn.silu(causal_depthwise_conv(g_qkv, conv_w[i])).astype(f32)
        gq, gk, gv = jnp.split(g_qkv.reshape(b, s, 3 * GDN_HEADS, GDN_HEAD_DIM), 3, axis=2)
        gq, gk = l2norm(gq), l2norm(gk)
        beta = jax.nn.sigmoid(g_b.astype(f32))
        g_decay = -jnp.exp(a_log[i].astype(f32)) * jax.nn.softplus(g_a.astype(f32) + dt_bias[i].astype(f32))
        o_g = gated_delta_rule(gq, gk, gv, g_decay, beta)
        o_g = o_g * lax.rsqrt(jnp.mean(o_g * o_g, axis=-1, keepdims=True) + EPS) * gdn_norm_w[i].astype(f32)
        o_g = o_g * jax.nn.silu(g_z.astype(f32)).reshape(b, s, GDN_HEADS, GDN_HEAD_DIM)
        o_g = o_g.reshape(b, s, GDN_WIDTH).astype(h.dtype)

        fq, fk, fv = jnp.split(f_qkv.reshape(b, s, 3 * FOX_HEADS, FOX_HEAD_DIM), 3, axis=2)
        log_f = jax.nn.log_sigmoid(f_f.astype(f32) + fox_f_bias[i].astype(f32))
        o_f = forgetting_attention(fq, fk, fv, log_f).reshape(b, s, FOX_WIDTH).astype(h.dtype)

        h = h + jnp.concatenate([o_g, o_f], axis=-1) @ w_out[i]

        hn = rmsnorm_2(h, ffn_norm_w[i])
        gate, up = jnp.split(hn @ w_gate_up[i], 2, axis=-1)
        h = h + (jax.nn.silu(gate) * up) @ w_down[i]

        ple_gate = jax.nn.sigmoid(rmsnorm_2(h, ple_norm_w[i]) @ w_ple_gate[i])
        h = h + ple_gate * (p[i] @ w_ple_proj[i])
    return rmsnorm_2(h, final_norm_w)


def setup_inputs(seed=0):
    out = dict(first_inputs(seed))
    for name, value in second_inputs(seed + 1).items():
        if name != "x":
            out[name + "_2"] = value
    return out


def reference(
    x, c, positions, w_ada, b_ada, norm_gain, w_in, q_norm_gain, w_uq, kv_norm_gain, w_ukv,
    w_branch_a, w_branch_b, w_out, final_norm_gain, p_2, attn_norm_w_2, w_in_2, conv_w_2,
    a_log_2, dt_bias_2, gdn_norm_w_2, fox_f_bias_2, w_out_2, ffn_norm_w_2, w_gate_up_2,
    w_down_2, ple_norm_w_2, w_ple_gate_2, w_ple_proj_2, final_norm_w_2,
):
    x = first_block(
        x, c, positions, w_ada, b_ada, norm_gain, w_in, q_norm_gain, w_uq, kv_norm_gain, w_ukv,
        w_branch_a, w_branch_b, w_out, final_norm_gain,
    )
    return second_block(
        x, p_2, attn_norm_w_2, w_in_2, conv_w_2, a_log_2, dt_bias_2, gdn_norm_w_2, fox_f_bias_2,
        w_out_2, ffn_norm_w_2, w_gate_up_2, w_down_2, ple_norm_w_2, w_ple_gate_2, w_ple_proj_2,
        final_norm_w_2,
    )


_drawn_inputs = setup_inputs


def setup_inputs(seed=0):
    import zlib

    import numpy as np

    out = dict(_drawn_inputs(seed))
    spreads = {}
    factors = {'b_ada': 7.882,
     'norm_gain': 8.0,
     'q_norm_gain': 8.0,
     'w_uq': 5.191,
     'kv_norm_gain': 8.0,
     'ple_norm_w_2': 3.625}
    for name, (base, spread) in spreads.items():
        noise = np.random.default_rng([zlib.crc32(name.encode()), seed]).standard_normal(out[name].shape)
        drawn = base * np.exp(spread * noise) if base else spread * noise
        out[name] = __import__('jax').numpy.asarray(drawn.astype(out[name].dtype))
    for name, factor in factors.items():
        out[name] = (out[name] * factor).astype(out[name].dtype)
    return out
```

```python
import math
from contextlib import ExitStack

import concourse.bass as bass
import numpy as np
from concourse import mybir

F32 = mybir.dt.float32
F32R = mybir.dt.float32r
I32 = mybir.dt.int32
ALU = mybir.AluOpType
ACT = mybir.ActivationFunctionType
AX = mybir.AxisListType

S = 512
D = 1024
NB = D // 128
EPS = 1e-6
NEG = -float(2 ** 100)
FFB = 22
EXPLN = "natural_log_exp_and_others"
SILU = "silu_and_others"

O_IDENT, O_NIDENT, O_ONES, O_COL = 0, 128, 256, 384
NCST = 392
R_NONES, R_MC, R_MS, R_MG, R_TRI = (128 * i for i in range(5))
NRC = 640
G_LM, G_RM = 0, 768
NGC = 1280

V_NG, V_BA, V_AN, V_FN, V_PN, V_LN = 0, 8, 32, 40, 48, 56
V_QN, V_KN, V_GN, V_CV = 64, 67, 69, 70
V_DT, V_FB, V_AL, V_N1 = 118, 119, 120, 121
NVEC = 129


def chunks():
    out = [("ada", i, 8, 128) for i in range(16)]
    out += [("sbq", i, 8, 128) for i in range(4)] + [("sbk", i, 8, 128) for i in range(4)]
    out += [("sbv", i, 2, 512) for i in range(4)]
    out += [("sz", i, 8, 128) for i in range(4)] + [("mz", i, 8, 128) for i in range(4)]
    out += [("ga", i, 8, 128) for i in range(8)]
    out += [("cq", i, 8, 128) for i in range(3)] + [("ckv", i, 8, 128) for i in range(2)] + [("kr", 0, 8, 96)]
    out += [("gb", i, 8, 128) for i in range(8)]
    out += [("uq", 0, 3, 288), ("uq", 1, 3, 288), ("uq", 2, 3, 192), ("uk", 0, 2, 512), ("uv", 0, 2, 512)]
    out += [("wa", i, 4, 256) for i in range(4)] + [("ada", i, 8, 128) for i in range(16, 24)]
    out += [("wb", i, 4, 256) for i in range(4)]
    out += [("wo", i, 8, 128) for i in range(8)]
    out += [("small", 0, 8, 96)]
    out += [("fq", i, 8, 128) for i in range(4)] + [("fk", i, 8, 128) for i in range(4)]
    out += [("fv", i, 2, 512) for i in range(4)]
    out += [("gqkv", i, 8, 128) for i in range(12)] + [("gz", i, 8, 128) for i in range(4)]
    out += [("wo2", i, 8, 128) for i in range(8)]
    for j in range(FFB):
        out += [("gt", j, 8, 128), ("up", j, 8, 128)]
    for m in range(NB):
        out += [("dn", 3 * m, 8, 128), ("dn", 3 * m + 1, 8, 128), ("dn", 3 * m + 2, 6, 128)]
    out += [("pp", 0, 2, 512), ("pp", 1, 2, 512)] + [("pg", i, 8, 128) for i in range(8)]
    return out


def build(nc, w_all, cst_d, rc_d, gc_d, vec_d, x_d, c_d, pos_d, p_d, out_d):
    PLAN = chunks()
    OFF, at = [], 0
    for _, _, kb, n in PLAN:
        OFF.append(at)
        at += 128 * kb * n

    top = ExitStack()
    with top:
        def sem(n):
            return top.enter_context(nc.semaphore(n))

        queue = {e: [] for e in "SGATV"}
        done = {e: sem("s_" + n) for e, n in zip("GATV", ("pool", "act", "pe", "dve"))}
        count = {e: 0 for e in "GATV"}

        def op(e, fn, *waits, inc=True):
            queue[e].append((waits, fn, inc))
            if inc:
                count[e] += 1
                return (done[e], count[e])
            return None

        def V(fn, *w): return op("V", fn, *w)
        def A(fn, *w): return op("A", fn, *w)
        def G(fn, *w): return op("G", fn, *w)
        def T(fn, *w, inc=False): return op("T", fn, *w, inc=inc)

        dsem = {}

        def DMA(name, dst, src, *w):
            if name not in dsem:
                dsem[name] = [sem("d_" + name), 0]
            d = dsem[name]
            d[1] += 16
            s = d[0]
            queue["S"].append((w, lambda e: e.dma_start(dst, src).then_inc(s, 16), False))
            return (s, d[1])

        def emit(t_out):
            def run(name):
                def body(eng):
                    seen = {}
                    for waits, fn, inc in queue[name]:
                        for s, v in waits:
                            if seen.get(id(s), 0) < v:
                                seen[id(s)] = v
                                eng.wait_ge(s, v)
                        ins = fn(eng)
                        if inc:
                            ins.then_inc(done[name], 1)
                    if name == "S":
                        for s, v in t_out:
                            eng.wait_ge(s, v)
                return body

            with nc.Block() as block:
                block.sync(run("S"))
                block.gpsimd(run("G"))
                block.scalar(run("A"))
                block.vector(run("V"))
                block.tensor(run("T"))

        def sb(stack, name, shape, dt=F32):
            return stack.enter_context(nc.sbuf_tensor(name, shape, dt))

        PB = [top.enter_context(nc.psum_tensor(f"pb{i}", [128, 512], F32)) for i in range(8)]
        free = [[] for _ in range(8)]

        cst = sb(top, "cst", [128, NCST])
        vec = sb(top, "vec", [128, NVEC])
        xT = sb(top, "xT", [128, NB, S])
        NRAW, NHL, LOOK = 4, 4, 2
        raw = sb(top, "raw", [128, NRAW, 1024])
        whi = sb(top, "whi", [128, NHL, 1024], F32R)
        wlo = sb(top, "wlo", [128, NHL, 1024], F32R)
        rcst = sb(top, "rcst", [128, 6, 128], F32R)
        sq = sb(top, "sq", [128, 2, S])
        ssq = sb(top, "ssq", [128, S])
        rsb = sb(top, "rsb", [128, S])
        tmpf = sb(top, "tmpf", [128, 2, S])
        mod = sb(top, "mod", [128, 24])
        sc8 = sb(top, "sc8", [128, 16])
        epsc = sb(top, "epsc", [128, 4])

        t_cst = DMA("cst", cst[:, :], cst_d)
        t_vec = DMA("vec", vec[:, :], vec_d)
        ident = cst[:, O_IDENT:O_IDENT + 128]
        ones = cst[:, O_ONES:O_ONES + 128]

        def cb(o):
            return cst[:, o:o + 128]

        def fr(ap):
            return ap.bitcast(F32)

        def vc(i, p0=0, p1=128):
            return vec[p0:p1, i:i + 1]

        with ExitStack() as tmp:
            rcf = sb(tmp, "rcf", [128, NRC])
            t_rcf = DMA("rcf", rcf[:, :], rc_d)
            V(lambda e: e.tensor_copy(rcst[:, 0, :], cb(O_IDENT)), t_cst)
            for i in range(5):
                t_rc = V(lambda e, i=i: e.tensor_copy(rcst[:, i + 1, :], rcf[:, 128 * i:128 * i + 128]), t_rcf)
        identR, nonesR, mcR, msR, mgR, triR = (rcst[:, i, :] for i in range(6))

        class Stream:
            def __init__(self):
                self.dma, self.cv, self.next = 0, 0, 0
                self.tok, self.conv = {}, {}
                self.rawfree = [[] for _ in range(NRAW)]
                self.hlfree = [[] for _ in range(NHL)]
                self.hl = 0

            def load(self, upto):
                while self.dma < min(upto, len(PLAN)):
                    i = self.dma
                    _, _, kb, n = PLAN[i]
                    r = i % NRAW
                    src = w_all[OFF[i]:OFF[i] + 128 * kb * n].rearrange("(p n) -> p n", p=128)
                    self.tok[i] = DMA(f"raw{r}", raw[:, r, 0:kb * n], src, *self.rawfree[r])
                    self.dma += 1

            def convert(self, upto):
                while self.cv < min(upto, len(PLAN)):
                    i = self.cv
                    name, _, kb, n = PLAN[i]
                    self.load(i + 1)
                    if name == "ada":
                        if i >= self.next:
                            return
                        self.cv += 1
                        continue
                    r, h, w = i % NRAW, self.hl % NHL, kb * n
                    self.hl += 1
                    src = raw[:, r, 0:w]
                    hi, lo = whi[:, h, 0:w], wlo[:, h, 0:w]
                    th = A(lambda e, a=hi, b=src: e.activation(a, b, ACT.Copy), self.tok[i], *self.hlfree[h])
                    tl = V(lambda e, a=lo, b=src, c=fr(hi): e.tensor_tensor(a, b, c, ALU.subtract),
                           th, *self.hlfree[h])
                    self.rawfree[r] = [th, tl]
                    self.conv[i] = (h, tl, hi.rearrange("p (k n) -> p k n", k=kb),
                                    lo.rearrange("p (k n) -> p k n", k=kb))
                    self.cv += 1

            def get(self, name, idx):
                i = self.next
                assert PLAN[i][:2] == (name, idx), (PLAN[i], name, idx)
                self.next += 1
                self.convert(i + 1 + LOOK)
                h, tl, hi, lo = self.conv.pop(i)
                return hi, lo, tl, h

            def get_raw(self, name, idx):
                i = self.next
                assert PLAN[i][:2] == (name, idx), (PLAN[i], name, idx)
                self.next += 1
                self.load(i + 3)
                return raw[:, i % NRAW, :], self.tok[i], i % NRAW

        st = Stream()

        def mm3(out, lh, ll, rh, rl, start, stop, *w):
            T(lambda e: e.matmul(out, lh, rl, start=start, stop=False, skip_group_check=True), *w)
            T(lambda e: e.matmul(out, ll, rh, start=False, stop=False, skip_group_check=True))
            return T(lambda e: e.matmul(out, lh, rh, start=False, stop=stop, skip_group_check=True), inc=True)

        def project(name, idx, m, bank, act, n0=0, kbs=None, start=True, stop=True, chunk=None):
            hi, lo, tw, slot = chunk or st.get(name, idx)
            ah, al, at_ = act
            kbs = kbs or range(hi.shape[1])
            for q, k in enumerate(kbs):
                w = [at_[k]]
                if q == 0:
                    w += [tw] + (free[bank] if start else [])
                t = mm3(PB[bank][0:m, :], hi[:, q, n0:n0 + m], lo[:, q, n0:n0 + m], ah[:, k, :], al[:, k, :],
                        start and q == 0, stop and q == len(kbs) - 1, *w)
            st.hlfree[slot] = [t]
            return t

        def project_nat(name, count_, kper, banks, act):
            ah, al, at_ = act
            last = count_ * kper - 1
            for c in range(count_):
                hi, lo, tw, slot = st.get(name, c)
                for q in range(kper):
                    k = c * kper + q
                    for t in range(4):
                        cs = slice(128 * t, 128 * t + 128)
                        w = [at_[k], tw] + (free[banks[t]] if k == 0 else [])
                        tok = mm3(PB[banks[t]][:, :], ah[:, k, cs], al[:, k, cs], hi[:, q, :], lo[:, q, :],
                                  k == 0, k == last, *w)
                st.hlfree[slot] = [tok]
            return tok

        def split(f, hi, lo, tf, *w):
            th = A(lambda e: e.activation(hi, f, ACT.Copy), tf, *w)
            return V(lambda e: e.tensor_tensor(lo, f, fr(hi), ALU.subtract), th, tf, *w)

        sqfree = [[], []]
        sqn = [0]

        def square_in(src, first, tsrc, *w):
            i = sqn[0] % 2
            sqn[0] += 1
            dst = ssq[:, :] if first else sq[:, i, :]
            ts = A(lambda e: e.activation(dst, src, ACT.Square), tsrc, *w, *([] if first else sqfree[i]))
            if not first:
                prev = square_in.tok
                ts = V(lambda e: e.tensor_tensor(ssq[:, :], ssq[:, :], dst, ALU.add), ts, prev)
                sqfree[i] = [ts]
            square_in.tok = ts
            return ts

        ssq_read = [[]]

        def rsqrt_rows(bank, n, eps_n, dst, tsrc, bias=0.0, src=None, *w):
            src = ssq[:, :] if src is None else src
            tm = T(lambda e: e.matmul(PB[bank][:, :], ones, src, start=True, stop=True), tsrc, *free[bank], inc=True)
            tl = A(lambda e: e.activation(dst, PB[bank][:, :], ACT.Ln, bias=eps_n, scale=1.0 / n), tm, *w)
            free[bank] = [tl]
            te = A(lambda e: e.activation(dst, dst, ACT.Exp, scale=-0.5, bias=bias), tl)
            return te, tm

        def fence():
            return [(done[e], count[e]) for e in "GATV" if count[e]]

        def norm_split(gcol, tsq, tok_x, hhi, hlo, hfree):
            te, tm = rsqrt_rows(7, D, epsc[:, 0:1], rsb[:, :], tsq, 0.0, None, *hfree)
            toks = []
            fb = [[], []]
            for b in range(NB):
                t = tmpf[:, b % 2, :]
                tf = V(lambda e, t=t, b=b: e.scalar_tensor_tensor(t, xT[:, b, :], gcol(b), rsb[:, :], ALU.mult, ALU.mult),
                       te, tok_x[b], *fb[b % 2], *hfree)
                tl = split(t, hhi[:, b, :], hlo[:, b, :], tf, *hfree)
                fb[b % 2] = [tl]
                toks.append(tl)
            return toks, tm, tl

        V(lambda e: e.memset(epsc[:, 0:1], EPS))
        V(lambda e: e.memset(epsc[:, 1:2], 1.0))
        V(lambda e: e.memset(epsc[:, 2:3], math.log(128 ** -0.5)))
        t_eps = V(lambda e: e.memset(epsc[:, 3:4], math.pi / 2))
        eps_c, one_c, dk_c, hpi_c = (epsc[:, i:i + 1] for i in range(4))

        def preload(name, *w):
            queue["A"].append((w, lambda e: e.preload_act_table_set(name), False))

        one = ExitStack()
        with one:
            cosk, sink = (sb(one, n, [128, S]) for n in ("cosk", "sink"))
            zs = sb(one, "zs", [128, 8, S])
            hhi = sb(one, "hhi", [128, NB, S], F32R)
            hlo = sb(one, "hlo", [128, NB, S], F32R)
            with ExitStack() as pre:
                cbt = sb(pre, "cbt", [128, D])
                junk = sb(pre, "junk", [128, D])
                posi = sb(pre, "posi", [128, S], I32)
                ang = sb(pre, "ang", [128, S])
                rn = sb(pre, "rn", [128, S])
                t_c = DMA("c", cbt[:, :], c_d.to_broadcast([128, D]), t_rc)
                t_pos = DMA("pos", posi[:, :], pos_d.to_broadcast([128, S]), t_rc)
                t_x = [DMA(f"x{b}", xT[:, b, :], x_d[b * 128:b * 128 + 128, :]) for b in range(NB)]

                t = V(lambda e: e.tensor_copy(ang[:, :], posi[:, :]), t_pos, t_rc)
                t = V(lambda e: e.tensor_scalar(ang[:, :], ang[:, :], cst[:, O_COL:O_COL + 1], None, ALU.mult), t, t_cst)
                parts, rest = [], 2 * math.pi
                for _ in range(4):
                    q = 2.0 ** (math.floor(math.log2(rest)) - 11)
                    parts.append(math.floor(rest / q) * q)
                    rest -= parts[-1]
                for step in (2048.0, 1.0):
                    t = V(lambda e, s_=step: e.tensor_scalar(rn[:, :], ang[:, :], 1 / (2 * math.pi * s_), 12582912.0,
                                                             ALU.mult, ALU.add), t)
                    t = V(lambda e: e.tensor_scalar(rn[:, :], rn[:, :], 12582912.0, None, ALU.subtract), t)
                    for pt in parts:
                        t = V(lambda e, k=-step * pt: e.scalar_tensor_tensor(
                            ang[:, :], rn[:, :], k, ang[:, :], ALU.mult, ALU.add), t)
                lim = float(np.float32(3.1415925))
                t = V(lambda e: e.tensor_scalar(ang[:, :], ang[:, :], lim, -lim, ALU.min, ALU.max), t)
                preload(SILU)
                ts = A(lambda e: e.activation(sink[:, :], ang[:, :], ACT.Sin), t)
                tc = A(lambda e: e.activation(rn[:, :], ang[:, :], ACT.Abs), t)
                tc = A(lambda e: e.activation(cosk[:, :], rn[:, :], ACT.Sin, scale=-1.0, bias=hpi_c), tc, t_eps)
                qs = 96 ** -0.5
                t_rope = V(lambda e: e.tensor_scalar(sink[:, :], sink[:, :], cst[:, O_COL + 1:O_COL + 2], None, ALU.mult), ts)
                preload(EXPLN)

                for b in range(NB):
                    tq = square_in(xT[:, b, :], b == 0, t_x[b])
                te, tm = rsqrt_rows(7, D, eps_c, rsb[:, :], tq)
                ssq_read = [tm]

                def ada(i, *w):
                    rw, tr, slot = st.get_raw("ada", i)
                    t1 = V(lambda e: e.tensor_tensor_reduce(out=junk[:, :], in0=rw, in1=cbt[:, :], scale=1.0, scalar=0.0,
                                                            op0=ALU.mult, op1=ALU.add, accum_out=mod[:, i:i + 1]),
                           tr, t_c, *w)
                    st.rawfree[slot] = [t1]
                    return t1
                t = None
                for i in range(16):
                    t = ada(i, *([t] if t else []))
                t = V(lambda e: e.tensor_tensor(mod[:, 0:16], mod[:, 0:16], vec[:, V_BA:V_BA + 16], ALU.add), t, t_vec)
                t = V(lambda e: e.scalar_tensor_tensor(sc8[:, 0:8], mod[:, 8:16], 1.0, vec[:, V_NG:V_NG + 8],
                                                       ALU.add, ALU.mult), t)
                th = []
                fb = [[], []]
                for b in range(NB):
                    y = tmpf[:, b % 2, :]
                    tf = V(lambda e, y=y, b=b: e.tensor_tensor(y, xT[:, b, :], rsb[:, :], ALU.mult), te, *fb[b % 2])
                    tf = V(lambda e, y=y, b=b: e.tensor_scalar(y, y, sc8[:, b:b + 1], mod[:, b:b + 1], ALU.mult, ALU.add),
                           tf, t)
                    tl = split(y, hhi[:, b, :], hlo[:, b, :], tf)
                    fb[b % 2] = [tl]
                    th.append(tl)
                f_pre = fence()
            h1 = (hhi, hlo, th)

            gax = xT
            ring = [0]

            def nextbank(n=4):
                b = ring[0] % n
                ring[0] += 1
                return b

            def drain(g):
                for _ in g:
                    pass

            def step(g, n=1):
                for _ in range(n):
                    next(g, None)

            def filler_t(items, bank):
                for name, m, ev in items:
                    tp = project(name, m, 128, bank, h1)
                    free[bank] = [ev(PB[bank][:, :], tp)]
                    yield

            tga, tgb, tzs = [None] * 8, [None] * 8, [None] * 8

            def keep(dst, toks, i):
                def ev(ps, tp):
                    toks[i] = V(lambda e: e.tensor_copy(dst, ps), tp, *f_pre)
                    return toks[i]
                return ev

            fa = filler_t([("sz", m, keep(zs[:, m, :], tzs, m)) for m in range(4)]
                          + [("mz", m, keep(zs[:, 4 + m, :], tzs, 4 + m)) for m in range(4)]
                          + [("ga", m, keep(gax[:, m, :], tga, m)) for m in range(8)], 7)

            LEN = [512, 384, 256, 128]
            BK = [0, 1, 2, 1]
            BO = [0, 0, 0, 384]
            SO = [0, 512, 1024, 896]
            THIRDS = ((0, 512), (1, 512), (2, 256))

            t_oa = []
            with ExitStack() as s1:
                sbp = sb(s1, "sbp", [128, 8, S])
                sbv = sb(s1, "sbv", [128, 4, S])
                sp = sb(s1, "sp", [128, 2, 1280])
                sph = sb(s1, "sph", [128, 1280], F32R)
                spl = sb(s1, "spl", [128, 1280], F32R)
                tsq_ = []
                for m in range(8):
                    b = nextbank()
                    tp = project(*(("sbq", m) if m < 4 else ("sbk", m - 4)), 128, b, h1)
                    te = A(lambda e, b=b, m=m: e.activation(sbp[:, m, :], PB[b][:, :], ACT.Copy,
                                                            scale=0.125 if m < 4 else 1.0), tp, *f_pre)
                    free[b] = [te]
                    tsq_.append(te)
                tp = project_nat("sbv", 4, 2, [4, 5, 6, 7], h1)
                for t_ in range(4):
                    te = A(lambda e, t_=t_: e.activation(sbv[:, t_, :], PB[4 + t_][:, :], ACT.Copy), tp, *f_pre)
                    free[4 + t_] = [te]
                t_sbv = te
                use = [f_pre, f_pre]
                useh = [f_pre]
                tqk, tmx, tsp = {}, {}, {}

                def sb_qk(h):
                    r0, pr, z = 64 * (h % 2), h // 2, 3 * (h % 2)
                    for kb in (0, 1, 3, 2):
                        n, o = LEN[kb], BO[kb]
                        out = PB[z + BK[kb]][:, o:o + n]
                        T(lambda e, out=out, kb=kb, first=kb != 3: e.matmul(
                            out, sbp[r0:r0 + 64, 4 + pr, 128 * kb:128 * kb + 128], sbp[r0:r0 + 64, pr, 128 * kb:512],
                            start=first, stop=False, skip_group_check=True), tsq_[pr], tsq_[4 + pr], *free[z + BK[kb]])
                        tqk[h] = T(lambda e, out=out: e.matmul(out[:, 0:128], identR, msR, start=False, stop=False,
                                                               skip_group_check=True), t_rc, inc=True)

                def sb_pre(h):
                    z, i = 3 * (h % 2), h % 2
                    for b, n in THIRDS:
                        t1 = V(lambda e, b=b, n=n: e.tensor_scalar(sp[:, i, 512 * b:512 * b + n], PB[z + b][:, 0:n], 40.0,
                                                                   None, ALU.min), tqk[h], *use[i])
                    t1 = A(lambda e: e.activation(sp[:, i, :], sp[:, i, :], ACT.Exp), t1)
                    t1 = A(lambda e: e.activation(sp[:, i, :], sp[:, i, :], ACT.Ln, bias=one_c), t1)
                    for b, n in THIRDS:
                        v = sp[:, i, 512 * b:512 * b + n]
                        t2 = V(lambda e, b=b, n=n, v=v: e.tensor_tensor(v, PB[z + b][:, 0:n], v, ALU.max), t1)
                    tmx[h] = t2
                    t3 = G(lambda e: e.tensor_copy(sph[:, :], sp[:, i, :]), t2, *useh[0])
                    tsp[h] = G(lambda e: e.tensor_tensor(spl[:, :], sp[:, i, :], fr(sph[:, :]), ALU.subtract), t3)

                def sb_suffix(h):
                    z, i = 3 * (h % 2), h % 2
                    for kb in range(4):
                        for jb in range(kb, 4):
                            o = BO[kb] + 128 * (jb - kb)
                            out = PB[z + BK[kb]][:, o:o + LEN[jb]]
                            w = triR if jb == kb else nonesR
                            for src in (sph, spl):
                                v = src[:, SO[jb]:SO[jb] + LEN[jb]]
                                tk = T(lambda e, out=out, w=w, v=v: e.matmul(out, w, v, start=False, stop=False,
                                                                             skip_group_check=True),
                                       tsp[h], tmx[h], inc=True)
                    useh[0] = [tk]
                    for b, n in THIRDS:
                        te = A(lambda e, b=b, n=n: e.activation(sp[:, i, 512 * b:512 * b + n], PB[z + b][:, 0:n], ACT.Exp),
                               tk, tsp[h])
                        free[z + b] = [te]
                    return te

                def sb_pv(h, tw):
                    r0, pr, i = 64 * (h % 2), h // 2, h % 2
                    for kb in range(4):
                        tk = T(lambda e, kb=kb: e.matmul(
                            PB[6][r0:r0 + 64, 128 * kb:512], sbv[:, kb, 64 * h:64 * h + 64],
                            sp[:, i, SO[kb]:SO[kb] + LEN[kb]], start=kb == 0, stop=kb == 3, skip_group_check=True),
                            tw, t_sbv, *free[6], inc=True)
                    use[i] = [tk]
                    if h % 2:
                        te = V(lambda e: e.tensor_copy(sbp[:, pr, :], PB[6][:, :]), tk)
                        free[6] = [te]
                        t_oa.append(te)

                sb_qk(0)
                sb_pre(0)
                for h in range(8):
                    if h < 7:
                        sb_qk(h + 1)
                    step(fa)
                    tw = sb_suffix(h)
                    if h < 7:
                        sb_pre(h + 1)
                    step(fa)
                    sb_pv(h, tw)
                drain(fa)
                preload(SILU)
                for m in range(8):
                    tzs[m] = A(lambda e, m=m: e.activation(zs[:, m, :], zs[:, m, :], ACT.Silu), tzs[m])
                for m in range(8):
                    tga[m] = A(lambda e, m=m: e.activation(gax[:, m, :], gax[:, m, :], ACT.Tanh, scale=0.5), tga[m])
                for m in range(4):
                    tzs[m] = V(lambda e, m=m: e.tensor_tensor(zs[:, m, :], zs[:, m, :], sbp[:, m, :], ALU.mult),
                               tzs[m], t_oa[m])
                for m in range(8):
                    tga[m] = V(lambda e, m=m: e.tensor_scalar(gax[:, m, :], gax[:, m, :], 0.5, 0.5, ALU.mult, ALU.add), tga[m])
                f1 = fence()

            s4 = ExitStack()
            gbt = sb(s4, "gbt", [128, NB, S])
            s2 = ExitStack()
            qc = sb(s2, "qc", [128, 8, S])
            kc = sb(s2, "kc", [128, 8, S])
            vb = sb(s2, "vb", [128, 4, S])
            krs = sb(s2, "krs", [96, S])
            cqf = kc[:, 0:5, :]
            qs = 96 ** -0.5
            SWAP = [(i + 16) % 32 for i in range(32)]
            rope_free = list(f1)

            def rope(bank, dst, tp, *w):
                x, r0, r1 = PB[bank][64:96, :], tmpf[64:96, 0, :], tmpf[64:96, 1, :]
                t1 = V(lambda e: e.stream_shuffle(r0, x, SWAP), tp, *rope_free)
                t2 = V(lambda e: e.tensor_tensor(r1, x, cosk[64:96, :], ALU.mult), tp)
                t1 = V(lambda e: e.tensor_tensor(r0, r0, sink[64:96, :], ALU.mult), t1)
                t3 = V(lambda e: e.tensor_tensor(dst, r0, r1, ALU.add), t1, t2, *w)
                rope_free[:] = [t3]
                return t2, t3

            tcq = []
            for m in range(5):
                b = nextbank()
                tp = project(*(("cq", m) if m < 3 else ("ckv", m - 3)), 128, b, h1)
                te = A(lambda e, b=b, m=m: e.activation(cqf[:, m, :], PB[b][:, :], ACT.Copy), tp, *f1)
                free[b] = [te]
                tcq.append(te)
            b = nextbank()
            tp = project("kr", 0, 96, b, h1)
            t2, t_kr = rope(b, krs[64:96, :], tp)
            free[b] = [t2]
            preload(EXPLN)
            for lo_, n_, g_, rk in ((0, 3, V_QN, 384), (3, 2, V_KN, 256)):
                for m in range(n_):
                    tq = square_in(cqf[:, lo_ + m, :], m == 0, tcq[lo_ + m], *(ssq_read if m == 0 else []))
                te, tm = rsqrt_rows(7, rk, eps_c, rsb[:, :], tq, 0.0, None, *f1, *tcq[:lo_])
                ssq_read = [tm]
                for m in range(n_):
                    k = lo_ + m
                    tcq[k] = V(lambda e, k=k, g=g_ + m: e.scalar_tensor_tensor(
                        cqf[:, k, :], cqf[:, k, :], vc(g), rsb[:, :], ALU.mult, ALU.mult), te)
            preload(SILU)
            for m in range(8):
                b = nextbank()
                tp = project("gb", m, 128, b, h1)
                te = A(lambda e, b=b, m=m: e.activation(gbt[:, m, :], PB[b][:, :], ACT.Tanh, scale=0.5), tp, *f1)
                free[b] = [te]
                tgb[m] = V(lambda e, m=m: e.tensor_scalar(gbt[:, m, :], gbt[:, m, :], 0.5, 0.5, ALU.mult, ALU.add), te)
            t_h1 = tp
            preload(EXPLN)
            tcl = [split(cqf[:, k, :], hhi[:, k, :], hlo[:, k, :], tcq[k], t_h1) for k in range(5)]
            cact = (hhi, hlo, tcl)
            tqc, tkc = [], []
            for h in range(8):
                if h in (0, 3, 6):
                    ch = st.get("uq", h // 3)
                b = nextbank()
                tp = project(None, None, 96, b, cact, n0=96 * (h % 3), chunk=ch)
                te = A(lambda e, h=h, b=b: e.activation(qc[0:64, h, :], PB[b][0:64, :], ACT.Copy), tp, *f1)
                t2, t3 = rope(b, qc[64:96, h, :], tp, *f1)
                free[b] = [te, t2]
                tqc.append((te, t3))
            t_kc = [G(lambda e, h=h: e.tensor_scalar(kc[64:96, h, :], krs[64:96, :], qs, None, ALU.mult), t_kr, tcl[-1])
                    for h in range(8)][-1]
            ch = st.get("uk", 0)
            for p_ in range(4):
                b = nextbank()
                tp = project(None, None, 128, b, cact, n0=128 * p_, chunk=ch, kbs=range(3, 5))
                t1 = A(lambda e, p_=p_, b=b: e.activation(kc[0:64, 2 * p_, :], PB[b][0:64, :], ACT.Copy, scale=qs), tp, tcl[-1])
                t2 = V(lambda e, p_=p_, b=b: e.tensor_scalar(kc[0:64, 2 * p_ + 1, :], PB[b][64:128, :], qs, None, ALU.mult),
                       tp, tcl[-1])
                free[b] = [t1, t2]
                tkc.append((t1, t2))
            hi, lo, tw, slot = st.get("uv", 0)
            for t_ in range(4):
                cs = slice(128 * t_, 128 * t_ + 128)
                b = nextbank()
                for k in range(2):
                    tok = mm3(PB[b][:, :], hhi[:, 3 + k, cs], hlo[:, 3 + k, cs], hi[:, k, :], lo[:, k, :],
                              k == 0, k == 1, tw, tcl[3 + k], *free[b])
                t_vb = A(lambda e, t_=t_, b=b: e.activation(vb[:, t_, :], PB[b][:, :], ACT.Copy), tok, *f1)
                free[b] = [t_vb]
            st.hlfree[slot] = [tok]
            t_oh = [split(zs[:, m, :], hhi[:, m, :], hlo[:, m, :], tzs[m], tok) for m in range(4)]

            def filler_w():
                for i in range(4):
                    ch = st.get("wa", i)
                    for q in range(2):
                        m, b = 2 * i + q, 6 + q
                        tp = project(None, None, 128, b, (hhi, hlo, t_oh), n0=128 * q, chunk=ch)
                        tga[m] = V(lambda e, m=m, b=b: e.tensor_tensor(gax[:, m, :], gax[:, m, :], PB[b][:, :], ALU.mult),
                                   tp, tga[m])
                        free[b] = [tga[m]]
                        yield

            QB, QO = [1, 2, 1, 0], [384, 0, 0, 0]
            QN = [128, 256, 384, 512]
            PO = [896, 1024, 512, 0]

            def softmax_attention(pfx, scr, f0, q_of, k_of, tq_of, v_all, tv, combine, fill, nfill, cbias=None):
                P = sb(scr, pfx + "P", [128, 1280])
                PT = sb(scr, pfx + "PT", [128, 1280])
                On = sb(scr, pfx + "On", [128, 4, 128])
                nm = sb(scr, pfx + "nm", [128, 2, 4])
                rs = sb(scr, pfx + "rs", [128, 2, 4])
                state = {"P": f0, "PT": f0, "On": f0}
                texp = {}

                def qk(h):
                    for qi in (3, 2, 0, 1):
                        o, n, b = QO[qi], QN[qi], QB[qi]
                        out = PB[b][:, o:o + n]
                        T(lambda e, out=out, q_=q_of(h, qi), k_=k_of(h, n), qi=qi: e.matmul(
                            out, q_, k_, start=qi != 0, stop=False, skip_group_check=True), *tq_of(h), *free[b])
                        tk = T(lambda e, out=out, n=n, qi=qi: e.matmul(
                            out[:, n - 128:n], identR, mcR, start=False, stop=qi != 2, skip_group_check=True), inc=True)
                    i = h % 2
                    src = {qi: PB[QB[qi]][:, QO[qi]:QO[qi] + QN[qi]] for qi in range(4)}
                    cb_, tcb = cbias(h) if cbias else (None, None)
                    for qi in (3, 2, 0, 1):
                        d = P[:, PO[qi]:PO[qi] + QN[qi]]
                        if cbias:
                            tm = V(lambda e, s_=src[qi], qi=qi, d=d: e.tensor_tensor_reduce(
                                out=d, in0=s_, in1=cb_[:, 0:QN[qi]], scale=1.0, scalar=-3.0e38, op0=ALU.add, op1=ALU.max,
                                accum_out=nm[:, i, qi:qi + 1]), tk, tcb, *state["P"])
                        else:
                            tm = V(lambda e, s_=src[qi], qi=qi: e.tensor_reduce(nm[:, i, qi:qi + 1], s_, AX.X, ALU.max),
                                   tk, *state["P"])
                    if cbias:
                        cbias_used[h % 2] = [tm]
                    tm2 = V(lambda e: e.tensor_scalar(nm[:, i, :], nm[:, i, :], -1.0, None, ALU.mult), tm)
                    for qi in (3, 2, 0, 1):
                        d = P[:, PO[qi]:PO[qi] + QN[qi]]
                        te = A(lambda e, s_=d if cbias else src[qi], qi=qi, d=d: e.activation(
                            d, s_, ACT.Exp, bias=nm[:, i, qi:qi + 1], accum_out=rs[:, i, qi:qi + 1]), tm2, *state["P"])
                    for b in range(3):
                        free[b] = [tm] if cbias else [te]
                    texp[h] = te

                def turn(h):
                    toks = []
                    for kb, b, o in ((0, 3, 0), (1, 4, 0), (3, 4, 384), (2, 3, 0)):
                        for qi in range(kb, 4):
                            src = P[:, PO[qi] + 128 * kb:PO[qi] + 128 * kb + 128]
                            dst = PB[b][:, o + 128 * (qi - kb):o + 128 * (qi - kb) + 128]
                            tk = T(lambda e, src=src, dst=dst: e.transpose(dst, src, ident), texp[h], *free[b], inc=True)
                        if kb == 1:
                            continue
                        n, d0 = {0: (512, 0), 3: (512, 512), 2: (256, 1024)}[kb]
                        dd, ss = PT[:, d0:d0 + n], PB[b][:, 0:n]
                        if kb == 3:
                            te = A(lambda e, dd=dd, ss=ss: e.activation(dd, ss, ACT.Copy), tk, *state["PT"])
                        else:
                            te = V(lambda e, dd=dd, ss=ss: e.tensor_copy(dd, ss), tk, *state["PT"])
                        free[b] = [te]
                        toks.append(te)
                    state["P"] = [tk]
                    return toks

                def pv(h, toks):
                    i = h % 2
                    for qi in range(4):
                        for kb in range(qi + 1):
                            l_ = PT[:, SO[kb] + 128 * (qi - kb):SO[kb] + 128 * (qi - kb) + 128]
                            tk = T(lambda e, l_=l_, kb=kb, qi=qi: e.matmul(
                                PB[5][:, 64 * qi:64 * qi + 64], l_, v_all[:, kb, 64 * h:64 * h + 64],
                                start=kb == 0, stop=kb == qi, skip_group_check=True), *toks, *tv, *free[5], inc=True)
                    state["PT"] = [tk]
                    tr = V(lambda e: e.reciprocal(rs[:, i, :], rs[:, i, :]), texp[h])
                    te = V(lambda e: e.tensor_tensor(
                        On[:, :, 64 * i:64 * i + 64], PB[5][:, 0:256].rearrange("p (a b) -> p a b", a=4),
                        rs[:, i, :].rearrange("p (a b) -> p a b", b=1).to_broadcast([128, 4, 64]), ALU.mult),
                        tk, tr, *state["On"])
                    free[5] = [te]
                    if i:
                        for qi in range(4):
                            tk = T(lambda e, qi=qi: e.transpose(PB[5][:, 128 * qi:128 * qi + 128], On[:, qi, :], ident),
                                   te, inc=True)
                        state["On"] = [tk]
                        free[5] = [combine(h // 2, 5, tk)]

                qk(0)
                step(fill, nfill)
                for h in range(8):
                    toks = turn(h)
                    if h < 7:
                        qk(h + 1)
                    step(fill, nfill)
                    pv(h, toks)
                    yield

            def comb(pr, bank, tk):
                tzs[4 + pr] = V(lambda e: e.tensor_tensor(zs[:, 4 + pr, :], zs[:, 4 + pr, :], PB[bank][:, :], ALU.mult),
                                tk, tzs[4 + pr])
                return tzs[4 + pr]

            fw = filler_w()
            drain(softmax_attention(
                "m", s2, f1, lambda h, qi: qc[0:96, h, 128 * qi:128 * qi + 128], lambda h, n: kc[0:96, h, 0:n],
                lambda h: (*tqc[h], *tkc[h // 2], t_kc), vb, [t_vb], comb, fw, 1))
            drain(fw)
            f2 = fence()
            s2.close()

            t_oh += [split(zs[:, m, :], hhi[:, m, :], hlo[:, m, :], tzs[m], *f2) for m in range(4, 8)]
            s5 = ExitStack()
            mhi = sb(s5, "mhi", [128, NB, S], F32R)
            mlo = sb(s5, "mlo", [128, NB, S], F32R)
            cb2 = sb(s5, "cb2", [128, D])
            jk2 = sb(s5, "jk2", [128, D])
            t_c2 = DMA("c2", cb2[:, :], c_d.to_broadcast([128, D]), *f2)
            tg = t_c2
            for i in range(16, 24):
                rw, tr, slot = st.get_raw("ada", i)
                tg = V(lambda e, rw=rw, i=i: e.tensor_tensor_reduce(
                    out=jk2[:, :], in0=rw, in1=cb2[:, :], scale=1.0, scalar=0.0, op0=ALU.mult, op1=ALU.add,
                    accum_out=mod[:, i:i + 1]), tr, t_c2, tg, *f2)
                st.rawfree[slot] = [tg]
            t_gate = V(lambda e: e.tensor_tensor(mod[:, 16:24], mod[:, 16:24], vec[:, V_BA + 16:V_BA + 24], ALU.add), tg)
            tmg = []
            for i in range(4):
                ch = st.get("wb", i)
                for q in range(2):
                    m, b = 2 * i + q, nextbank()
                    tp = project(None, None, 128, b, (hhi[:, 4:8, :], hlo[:, 4:8, :], t_oh[4:8]), n0=128 * q, chunk=ch)
                    t1 = V(lambda e, m=m, b=b: e.tensor_tensor(gbt[:, m, :], gbt[:, m, :], PB[b][:, :], ALU.mult), tp, tgb[m])
                    free[b] = [t1]
                    t1 = V(lambda e, m=m: e.tensor_tensor(gbt[:, m, :], gbt[:, m, :], gax[:, m, :], ALU.add), t1, tga[m])
                    tmg.append(split(gbt[:, m, :], mhi[:, m, :], mlo[:, m, :], t1, *f2))
            t_x = [DMA(f"x{b}", xT[:, b, :], x_d[b * 128:b * 128 + 128, :], *tmg) for b in range(NB)]
            tx1 = []
            for m in range(8):
                b = nextbank()
                tp = project("wo", m, 128, b, (mhi, mlo, tmg))
                tx = V(lambda e, m=m, b=b: e.scalar_tensor_tensor(
                    xT[:, m, :], PB[b][:, :], mod[:, 16 + m:17 + m], xT[:, m, :], ALU.mult, ALU.add), tp, t_x[m], t_gate)
                free[b] = [tx]
                tx1.append(tx)
                tq = square_in(xT[:, m, :], m == 0, tx, *(ssq_read if m == 0 else []))
            te, tm = rsqrt_rows(7, D, eps_c, rsb[:, :], tq)
            ssq_read = [tm]
            for m in range(8):
                tx1[m] = V(lambda e, m=m: e.scalar_tensor_tensor(
                    xT[:, m, :], xT[:, m, :], vc(V_N1 + m), rsb[:, :], ALU.mult, ALU.mult), te, tx1[m])
                tq = square_in(xT[:, m, :], m == 0, tx1[m], *(ssq_read if m == 0 else []))
            f3 = fence()
            s5.close()
            s4.close()

        k2 = ExitStack()
        fqo = sb(k2, "fqo", [128, 4, S])
        gzs = sb(k2, "gzs", [128, 4, S])
        gq = sb(k2, "gq", [128, 12, S])
        rowt = sb(k2, "rowt", [128, S])
        gcst = sb(k2, "gcst", [128, NGC])
        t_gc = DMA("gcst", gcst[:, :], gc_d, *f3)
        hs = ExitStack()
        hhi = sb(hs, "hhi2", [128, NB, S], F32R)
        hlo = sb(hs, "hlo2", [128, NB, S], F32R)
        th, tm, _ = norm_split(lambda b: vc(V_AN + b), tq, tx1, hhi, hlo, f3)
        ssq_read = [tm]
        h2 = (hhi, hlo, th)
        fk = sb(hs, "fk", [128, 4, S])
        fv = sb(hs, "fv", [128, 4, S])
        lg = sb(hs, "lg", [96, S])
        pr_ = sb(hs, "pr_", [96, 2])

        tp = project("small", 0, 96, 3, h2)
        s1c = cst[0:96, O_COL + 2:O_COL + 3]
        t1 = V(lambda e: e.tensor_tensor(pr_[:, 0:1], vc(V_DT, 0, 96), vc(V_FB, 0, 96), ALU.add), t_vec, *f3)
        ta = A(lambda e: e.activation(pr_[:, 1:2], vc(V_AL, 0, 96), ACT.Exp), *f3)
        ta = V(lambda e: e.tensor_scalar(pr_[:, 1:2], pr_[:, 1:2], -1.0, None, ALU.mult), ta)
        t1 = V(lambda e: e.tensor_scalar(rowt[0:96, :], PB[3][0:96, :], pr_[:, 0:1], s1c, ALU.add, ALU.mult), t1, tp, *f3)
        free[3] = [t1]
        t2 = V(lambda e: e.tensor_scalar(lg[:, :], rowt[0:96, :], 40.0, None, ALU.min), t1)
        t2 = A(lambda e: e.activation(lg[:, :], lg[:, :], ACT.Exp), t2)
        t2 = A(lambda e: e.activation(lg[:, :], lg[:, :], ACT.Ln, bias=one_c[0:96, :]), t2)
        t2 = V(lambda e: e.tensor_tensor(lg[:, :], lg[:, :], rowt[0:96, :], ALU.max), t2)
        t2 = V(lambda e: e.tensor_scalar(lg[:, :], lg[:, :], pr_[:, 1:2], None, ALU.mult), t2, ta)
        t3 = V(lambda e: e.tensor_tensor_scan(rowt[0:96, :], gcst[0:96, G_RM:G_RM + 512], lg[:, :], 0.0, ALU.mult, ALU.add),
               t2, t_gc)
        c3 = rowt[0:32, :].rearrange("p (c j) -> p c j", j=64)
        t4 = V(lambda e: e.tensor_tensor(rowt[96:128, :].rearrange("p (c j) -> p c j", j=64),
                                         c3[:, :, 63:64].to_broadcast([32, 8, 64]), c3, ALU.subtract), t3)
        t_row = V(lambda e: e.tensor_copy(rowt[32:64, :], lg[32:64, :]), t3)

        tf_ = []
        for m in range(8):
            b = nextbank(3)
            tp = project(*(("fq", m) if m < 4 else ("fk", m - 4)), 128, b, h2)
            d = fqo[:, m, :] if m < 4 else fk[:, m - 4, :]
            te = A(lambda e, b=b, d=d, m=m: e.activation(d, PB[b][:, :], ACT.Copy, scale=0.125 if m < 4 else 1.0), tp, *f3)
            free[b] = [te]
            tf_.append(te)
        tp = project_nat("fv", 4, 2, [4, 5, 6, 7], h2)
        for t_ in range(4):
            te = A(lambda e, t_=t_: e.activation(fv[:, t_, :], PB[4 + t_][:, :], ACT.Copy), tp, *f3)
            free[4 + t_] = [te]
        t_fv = te

        cbuf = sb(hs, "cbuf", [128, 2, S + 3])
        cbt2 = sb(hs, "cbt2", [128, 2, S])
        tz = V(lambda e: e.memset(cbuf[:, :, 0:3], 0.0), *f3)
        tgq, tgz = [None] * 12, [None] * 4
        cfree = [[tz], [tz]]

        def filler_q():
            for m in range(12):
                b = 6 + m % 2
                tp = project("gqkv", m, 128, b, h2)
                i = m % 2
                x = cbuf[:, i, :]
                te = A(lambda e, b=b, x=x: e.activation(x[:, 3:S + 3], PB[b][:, :], ACT.Copy), tp, *cfree[i], *f3)
                free[b] = [te]
                y = gq[:, m, :]
                t = V(lambda e, x=x, y=y, m=m: e.tensor_scalar(y, x[:, 3:S + 3], vc(V_CV + 4 * m + 3), None, ALU.mult), te, tz)
                for j in range(3):
                    t = V(lambda e, x=x, y=y, m=m, j=j: e.scalar_tensor_tensor(
                        y, x[:, j:S + j], vc(V_CV + 4 * m + j), y, ALU.mult, ALU.add), t)
                cfree[i] = [t]
                tgq[m] = t
                yield
            for m in range(4):
                b = 6 + m % 2
                tp = project("gz", m, 128, b, h2)
                te = V(lambda e, b=b, m=m: e.tensor_copy(gzs[:, m, :], PB[b][:, :]), tp, *f3)
                free[b] = [te]
                tgz[m] = te
                yield

        cbias_used = [list(f3), list(f3)]
        cbtok = {}

        def make_cb(h):
            b = 7
            tk = T(lambda e: e.matmul(PB[b][:, :], ident[:, 64 + h:65 + h].to_broadcast([128, 128]), rowt[:, :],
                                      start=True, stop=True), t_row, t4, *free[b], inc=True)
            te = A(lambda e: e.activation(cbt2[:, h % 2, :], PB[b][:, :], ACT.Copy, scale=-1.0), tk, *cbias_used[h % 2])
            free[b] = [te]
            cbtok[h] = te

        def cbias(h):
            if h == 0:
                make_cb(0)
            tcb = cbtok[h]
            if h < 7:
                make_cb(h + 1)
            return cbt2[:, h % 2, :], tcb

        tfo = []

        def comb2(pr, bank, tk):
            te = A(lambda e: e.activation(fqo[:, pr, :], PB[bank][:, :], ACT.Copy), tk)
            tfo.append(te)
            return te

        fq_ = filler_q()
        drain(softmax_attention(
            "f", hs, f3, lambda h, qi: fqo[64 * (h % 2):64 * (h % 2) + 64, h // 2, 128 * qi:128 * qi + 128],
            lambda h, n: fk[64 * (h % 2):64 * (h % 2) + 64, h // 2, 0:n],
            lambda h: (tf_[h // 2], tf_[4 + h // 2]), fv, [t_fv], comb2, fq_, 2, cbias))
        drain(fq_)
        f4 = fence()
        hs.close()

        gd = ExitStack()
        NT, X, Y, QKT, KBG, KDEC, VBN, EGB = (sb(gd, n, [128, 4, S]) for n in
                                              ("NT", "X", "Y", "QKT", "KBG", "KDEC", "VBN", "EGB"))
        nat = sb(gd, "nat", [128, 4, 128])
        cols = sb(gd, "cols", [128, 3, 4, 4])
        dts = sb(gd, "dts", [128, 2, S])
        pp_ = sb(gd, "pp_", [128, 2, S])
        st2 = sb(gd, "st2", [128, 2, S])
        vnw, sg_ = tmpf[:, 0, :], tmpf[:, 1, :]

        preload(SILU)
        for m in range(12):
            tgq[m] = A(lambda e, m=m: e.activation(gq[:, m, :], gq[:, m, :], ACT.Silu), tgq[m])
        for m in range(4):
            tgz[m] = A(lambda e, m=m: e.activation(gzs[:, m, :], gzs[:, m, :], ACT.Silu), tgz[m])
        preload(EXPLN)
        for t_ in range(4):
            tk = T(lambda e, t_=t_: e.transpose(PB[0][:, 128 * t_:128 * t_ + 128], rowt[:, 128 * t_:128 * t_ + 128], ident),
                   t_row, t4, *free[0], inc=True)
        te = V(lambda e: e.tensor_copy(nat[:, :, :], PB[0][:, :].rearrange("p (a b) -> p a b", a=4)), tk, *f4)
        free[0] = [te]
        t1 = V(lambda e: e.tensor_tensor(cols[:, 1, :, :], nat[:, :, 0:4], nat[:, :, 32:36], ALU.add), te, *f4)
        ta = A(lambda e: e.activation(cols[:, 0, :, :], nat[:, :, 32:36], ACT.Exp), te, *f4)
        ta = A(lambda e: e.activation(cols[:, 2, :, :], nat[:, :, 96:100], ACT.Exp), te)
        ta = A(lambda e: e.activation(cols[:, 1, :, :], cols[:, 1, :, :], ACT.Exp), t1)
        t_cols = ta

        lfree = [[*f4], [*f4]]
        for m in range(8):
            i, b = m % 2, nextbank(3)
            ts = A(lambda e, m=m, i=i: e.activation(sq[:, i, :], gq[:, m, :], ACT.Square), tgq[m], *sqfree[i], *f4)
            te, tm = rsqrt_rows(b, 1, eps_c, dts[:, i, :], ts, dk_c if m < 4 else 0.0, sq[:, i, :], *lfree[i])
            sqfree[i] = [tm]
            tgq[m] = V(lambda e, m=m, i=i: e.tensor_tensor(gq[:, m, :], gq[:, m, :], dts[:, i, :], ALU.mult), te)
            lfree[i] = [tgq[m]]

        def hh(x, h, t_):
            return x[:, h, 128 * t_:128 * t_ + 128]

        def bc4(i, h):
            return cols[:, i, :, h:h + 1].to_broadcast([128, 4, 128])

        def v3(x):
            return x.rearrange("p (a b) -> p a b", a=4)

        tkb, tkd, tvn, tnt, tqk2, teg, tqg = ({} for _ in range(7))
        dfree = {0: lfree[0] + lfree[1], 1: lfree[0] + lfree[1]}
        for h in range(4):
            b = 3 + h % 2
            for t_ in range(4):
                tk = T(lambda e, t_=t_, b=b: e.transpose(PB[b][:, 128 * t_:128 * t_ + 128], hh(gq, 4 + h, t_), ident),
                       tgq[4 + h], *free[b], inc=True) if False else T(
                    lambda e, t_=t_, b=b, h=h: e.transpose(PB[b][:, 128 * t_:128 * t_ + 128], hh(gq, 4 + h, t_), ident),
                    tgq[4 + h], *free[b], inc=True)
            tkb[h] = V(lambda e, h=h, b=b: e.tensor_tensor(v3(KBG[:, h, :]), v3(PB[b][:, :]), bc4(1, h), ALU.mult),
                       tk, t_cols, *f4)
            tkd[h] = V(lambda e, h=h, b=b: e.tensor_tensor(v3(KDEC[:, h, :]), v3(PB[b][:, :]), bc4(2, h), ALU.mult),
                       tk, t_cols, *f4)
            free[b] = [tkd[h]]
            b = 5
            for t_ in range(4):
                tk = T(lambda e, t_=t_, b=b, h=h: e.transpose(PB[b][:, 128 * t_:128 * t_ + 128], hh(gq, 8 + h, t_), ident),
                       tgq[8 + h], *free[b], inc=True)
            tvn[h] = V(lambda e, h=h, b=b: e.tensor_tensor(v3(VBN[:, h, :]), v3(PB[b][:, :]), bc4(0, h), ALU.mult),
                       tk, t_cols, *f4)
            free[b] = [tvn[h]]
            b = 6 + h % 2
            B = PB[b]
            tk = T(lambda e, h=h, B=B: e.matmul(B[:, :], ident[:, h:h + 1].to_broadcast([128, 128]), rowt[:, :],
                                                start=True, stop=False, skip_group_check=True), t_row, t4, *free[b], inc=True)
            teg[h] = A(lambda e, h=h, B=B: e.activation(EGB[:, h, :], B[:, :], ACT.Exp), tk, *f4)
            for t_ in range(4):
                c = slice(128 * t_, 128 * t_ + 128)
                T(lambda e, h=h, B=B, c=c: e.matmul(B[:, c], rowt[:, c], cst[:, O_NIDENT + h:O_NIDENT + h + 1]
                                                    .to_broadcast([128, 128]), start=False, stop=False,
                                                    skip_group_check=True), teg[h])
                tk = T(lambda e, B=B, c=c: e.matmul(B[:, c], identR, mgR, start=False, stop=False, skip_group_check=True),
                       inc=True)
            td = A(lambda e, B=B: e.activation(dts[:, 0, :], B[:, :], ACT.Exp), tk, *dfree[0], *f4)
            tk = T(lambda e, h=h, B=B: e.matmul(B[:, :], ident[:, 32 + h:33 + h].to_broadcast([128, 128]), rowt[:, :],
                                                start=False, stop=True, skip_group_check=True), td, inc=True)
            tdb = A(lambda e, B=B: e.activation(dts[:, 1, :], B[:, :], ACT.Exp), tk, *dfree[1], *f4)
            free[b] = [tdb]
            for t_ in range(4):
                tk = T(lambda e, t_=t_, h=h: e.matmul(PB[0][:, 128 * t_:128 * t_ + 128], hh(gq, 4 + h, t_), hh(gq, 4 + h, t_),
                                                      start=True, stop=True, skip_group_check=True), tgq[4 + h], *free[0], inc=True)
            tnt[h] = V(lambda e, h=h: e.tensor_tensor(NT[:, h, :], PB[0][:, :], dts[:, 1, :], ALU.mult), tk, tdb, *f4)
            free[0] = [tnt[h]]
            for t_ in range(4):
                tk = T(lambda e, t_=t_, h=h: e.matmul(PB[1][:, 128 * t_:128 * t_ + 128], hh(gq, 4 + h, t_), hh(gq, h, t_),
                                                      start=True, stop=True, skip_group_check=True),
                       tgq[4 + h], tgq[h], *free[1], inc=True)
            tqk2[h] = V(lambda e, h=h: e.tensor_tensor(QKT[:, h, :], PB[1][:, :], dts[:, 0, :], ALU.mult), tk, td, *f4)
            free[1] = [tqk2[h]]
            dfree = {0: [tqk2[h]], 1: [tnt[h]]}
            tqg[h] = V(lambda e, h=h: e.tensor_tensor(gq[:, h, :], gq[:, h, :], EGB[:, h, :], ALU.mult), teg[h], tqk2[h])

        tX, tY = {}, {}
        for h in range(4):
            tX[h] = G(lambda e, h=h: e.tensor_copy(v3(X[:, h, :]), cst[:, 0:128].rearrange("p (a b) -> p a b", a=1)
                                                   .to_broadcast([128, 4, 128])), *f4)
            tY[h] = G(lambda e, h=h: e.tensor_copy(v3(Y[:, h, :]), cst[:, 0:128].rearrange("p (a b) -> p a b", a=1)
                                                   .to_broadcast([128, 4, 128])), *f4)
        pfree = [[*f4], [*f4]]
        for lv in range(6):
            mask = gcst[:, G_LM + 128 * lv:G_LM + 128 * lv + 128].rearrange("p (a b) -> p a b", a=1).to_broadcast([128, 4, 128])
            tP = {}

            def level_p(h):
                b = h % 2
                for t_ in range(4):
                    tk = T(lambda e, t_=t_, b=b: e.matmul(PB[b][:, 128 * t_:128 * t_ + 128], hh(NT, h, t_), hh(X, h, t_),
                                                     start=True, stop=True, skip_group_check=True),
                           tnt[h], tX[h], *free[b], inc=True)
                tP[h] = (V(lambda e, mask=mask: e.tensor_tensor(v3(pp_[:, h % 2, :]), v3(PB[b][:, :]), mask, ALU.mult),
                           tk, t_gc, *pfree[h % 2]), tk)
                free[b] = [tP[h][0]]

            def level_u(h):
                i = h % 2
                tpp, tkx = tP[h]
                if lv < 5:
                    b = 2 + i
                    for t_ in range(4):
                        tk = T(lambda e, t_=t_, b=b: e.matmul(PB[b][:, 128 * t_:128 * t_ + 128], hh(Y, h, t_), hh(pp_, i, t_),
                                                         start=True, stop=True, skip_group_check=True),
                               tpp, tY[h], *free[b], inc=True)
                    tX[h] = V(lambda e, b=b: e.tensor_tensor(X[:, h, :], X[:, h, :], PB[b][:, :], ALU.subtract), tk, tkx, tX[h])
                    free[b] = [tX[h]]
                b = 4 + i
                for t_ in range(4):
                    tk = T(lambda e, t_=t_, b=b: e.matmul(PB[b][:, 128 * t_:128 * t_ + 128], hh(pp_, i, t_), hh(Y, h, t_),
                                                     start=True, stop=True, skip_group_check=True),
                           tpp, tY[h], *free[b], inc=True)
                pfree[i] = [tk]
                tY[h] = V(lambda e, b=b: e.tensor_tensor(Y[:, h, :], Y[:, h, :], PB[b][:, :], ALU.subtract), tk, tY[h])
                free[b] = [tY[h]]

            level_p(0)
            for h in range(4):
                if h < 3:
                    level_p(h + 1)
                level_u(h)

        U, W = X, NT
        tW, tU = {}, {}
        for h in range(4):
            b = h % 2
            for t_ in range(4):
                tk = T(lambda e, t_=t_, h=h, b=b: e.matmul(PB[b][:, 128 * t_:128 * t_ + 128], hh(KBG, h, t_), hh(Y, h, t_),
                                                           start=True, stop=True, skip_group_check=True),
                       tkb[h], tY[h], *free[b], inc=True)
            tW[h] = V(lambda e, h=h, b=b: e.tensor_copy(W[:, h, :], PB[b][:, :]), tk, tP[h][1])
            free[b] = [tW[h]]
        for t_ in range(4):
            b = 2 + t_ % 2
            for h in range(4):
                tk = T(lambda e, t_=t_, h=h, b=b: e.matmul(PB[b][:, 128 * h:128 * h + 128], hh(Y, h, t_), hh(VBN, h, t_),
                                                           start=True, stop=True, skip_group_check=True),
                       tvn[h], tY[h], *free[b], inc=True)
            tU[t_] = A(lambda e, t_=t_, b=b: e.activation(U[:, t_, :], PB[b][:, :], ACT.Copy), tk, *(x[1] for x in tP.values()),
                       *tX.values())
            free[b] = [tU[t_]]

        og = gq[:, 8:12, :]
        tS = V(lambda e: e.memset(st2[:, 0, :], 0.0), *f4)
        tfree_S = [[], []]
        tog = None
        t_vu = []
        t_sg = []
        for c in range(8):
            t_, p0, cur, nx = c // 2, 64 * (c % 2), c % 2, (c + 1) % 2
            cs = slice(64 * c, 64 * c + 64)
            for h in range(4):
                tk = T(lambda e, h=h, p0=p0, cs=cs, cur=cur: e.matmul(
                    PB[6][p0:p0 + 64, 128 * h:128 * h + 128], W[:, h, cs], st2[:, cur, 128 * h:128 * h + 128],
                    start=True, stop=True, skip_group_check=True), tW[h], tS, *free[6], inc=True)
            tv_ = V(lambda e, t_=t_, p0=p0: e.tensor_tensor(vnw[p0:p0 + 64, :], U[p0:p0 + 64, t_, :], PB[6][p0:p0 + 64, :],
                                                           ALU.subtract), tk, tU[t_], *t_vu, *f4)
            free[6] = [tv_]
            ob = 2 + c % 2
            for h in range(4):
                T(lambda e, h=h, cs=cs, cur=cur, ob=ob: e.matmul(
                    PB[ob][:, 64 * h:64 * h + 64], st2[:, cur, 128 * h:128 * h + 128], gq[:, h, cs],
                    start=h == 0, stop=False, skip_group_check=True), tqg[h], tS, *free[ob])
            tsg = V(lambda e, c=c, cur=cur: e.tensor_tensor(v3(sg_[:, :]), v3(st2[:, cur, :]),
                                                           EGB[:, :, 64 * c + 63:64 * c + 64].to_broadcast([128, 4, 128]),
                                                           ALU.mult), tS, *teg.values(), *t_sg, *f4)
            if c < 7:
                for h in range(4):
                    tk = T(lambda e, h=h, p0=p0, t_=t_: e.matmul(
                        PB[7][:, 128 * h:128 * h + 128], KDEC[p0:p0 + 64, h, 128 * t_:128 * t_ + 128],
                        vnw[p0:p0 + 64, 128 * h:128 * h + 128], start=True, stop=True, skip_group_check=True),
                        tv_, tkd[h], *free[7], inc=True)
                tS = V(lambda e, nx=nx: e.tensor_tensor(st2[:, nx, :], sg_[:, :], PB[7][:, :], ALU.add), tk, tsg, *tfree_S[nx])
                free[7] = [tS]
                t_sg = [tS]
            for h in range(4):
                tk = T(lambda e, h=h, p0=p0, t_=t_, ob=ob: e.matmul(
                    PB[ob][:, 64 * h:64 * h + 64], vnw[p0:p0 + 64, 128 * h:128 * h + 128],
                    QKT[p0:p0 + 64, h, 128 * t_ + p0:128 * t_ + p0 + 64], start=False, stop=True, skip_group_check=True),
                    tv_, tqk2[h], inc=True)
            t_vu = [tk]
            tfree_S[cur] = [tk]
            tog = A(lambda e, cs=cs, ob=ob: e.activation(og[:, :, cs], PB[ob][:, 0:256].rearrange("p (a b) -> p a b", a=4),
                                                         ACT.Copy), tk, *tvn.values())
            free[ob] = [tog]
        t_og = []
        lfree = [[*dfree[0], *dfree[1]], [*dfree[0], *dfree[1]]]
        for h in range(4):
            i, b = h % 2, h % 2
            ts = A(lambda e, h=h, i=i: e.activation(sq[:, i, :], og[:, h, :], ACT.Square), tog, *sqfree[i])
            te, tm = rsqrt_rows(b, 128, eps_c, dts[:, i, :], ts, 0.0, sq[:, i, :], *lfree[i])
            sqfree[i] = [tm]
            t1 = V(lambda e, h=h, i=i: e.scalar_tensor_tensor(og[:, h, :], og[:, h, :], vc(V_GN), dts[:, i, :],
                                                              ALU.mult, ALU.mult), te)
            lfree[i] = [t1]
            t_og.append(V(lambda e, h=h: e.tensor_tensor(og[:, h, :], og[:, h, :], gzs[:, h, :], ALU.mult), t1, tgz[h]))
        f5 = fence()
        gd.close()

        hs = ExitStack()
        hhi = sb(hs, "hhi3", [128, NB, S], F32R)
        hlo = sb(hs, "hlo3", [128, NB, S], F32R)
        tm_ = [None] * 8
        for m in (4, 5, 6, 7, 0, 1, 2, 3):
            src = og[:, m, :] if m < 4 else fqo[:, m - 4, :]
            tm_[m] = split(src, hhi[:, m, :], hlo[:, m, :], t_og[m] if m < 4 else tfo[m - 4], *f5)

        def residual(bank, m, tp, txs):
            tx = V(lambda e: e.tensor_tensor(xT[:, m, :], xT[:, m, :], PB[bank][:, :], ALU.add), tp, txs[m])
            free[bank] = [tx]
            return tx, square_in(xT[:, m, :], m == 0, tx, *(ssq_read if m == 0 else []))

        tx2 = []
        for m in range(8):
            b = nextbank()
            tp = project("wo2", m, 128, b, (hhi, hlo, tm_))
            tx, tq = residual(b, m, tp, tx1)
            tx2.append(tx)
        f6 = fence()
        hs.close()
        k2.close()

        ff = ExitStack()
        ahi = sb(ff, "ahi", [128, FFB, S], F32R)
        alo = sb(ff, "alo", [128, FFB, S], F32R)
        hs = ExitStack()
        hhi = sb(hs, "hhi4", [128, NB, S], F32R)
        hlo = sb(hs, "hlo4", [128, NB, S], F32R)
        th, tm, _ = norm_split(lambda b: vc(V_FN + b), tq, tx2, hhi, hlo, f6)
        ssq_read = [tm]
        h3 = (hhi, hlo, th)
        preload(SILU)
        sfree = [[th[-1]], [th[-1]]]
        tact = []
        for j in range(FFB):
            i = j % 2
            b0, b1 = 2 * i, 2 * i + 1
            tp = project("gt", j, 128, b0, h3)
            s_ = tmpf[:, i, :]
            ts = A(lambda e, s_=s_, b0=b0: e.activation(s_, PB[b0][:, :], ACT.Silu), tp, *sfree[i])
            free[b0] = [ts]
            tp = project("up", j, 128, b1, h3)
            t1 = V(lambda e, s_=s_, b1=b1: e.tensor_tensor(s_, s_, PB[b1][:, :], ALU.mult), ts, tp)
            free[b1] = [t1]
            tl = split(s_, ahi[:, j, :], alo[:, j, :], t1, *f6)
            sfree[i] = [tl]
            tact.append(tl)
        hs.close()
        tx3 = []
        for m in range(8):
            b = 4 + m % 2
            for q in range(3):
                tp = project("dn", 3 * m + q, 128, b, (ahi, alo, tact), kbs=range(8 * q, min(8 * q + 8, FFB)),
                             start=q == 0, stop=q == 2)
            if m == 0:
                preload(EXPLN)
            tx, tq = residual(b, m, tp, tx2)
            tx3.append(tx)
        f7 = fence()
        ff.close()

        pl = ExitStack()
        pf = sb(pl, "pf", [128, 2, S])
        phi = sb(pl, "phi", [128, 2, S], F32R)
        plo = sb(pl, "plo", [128, 2, S], F32R)
        PL = sb(pl, "PL", [128, NB, S])
        hhi = sb(pl, "hhi5", [128, NB, S], F32R)
        hlo = sb(pl, "hlo5", [128, NB, S], F32R)
        t_p = DMA("p", pf[:, :, :], p_d.rearrange("(a p) n -> p a n", p=128), *f7)
        tpl = [split(pf[:, k, :], phi[:, k, :], plo[:, k, :], t_p, *f7) for k in range(2)]
        tPL = []
        for i in range(2):
            ch = st.get("pp", i)
            for q in range(4):
                m, b = 4 * i + q, nextbank()
                tp = project(None, None, 128, b, (phi, plo, tpl), n0=128 * q, chunk=ch)
                te = A(lambda e, m=m, b=b: e.activation(PL[:, m, :], PB[b][:, :], ACT.Copy, scale=0.5), tp, *f7)
                free[b] = [te]
                tPL.append(te)
        th, tm, _ = norm_split(lambda b: vc(V_PN + b), tq, tx3, hhi, hlo, f7)
        ssq_read = [tm]
        preload(SILU)
        tx4 = []
        sfree = [[th[-1]], [th[-1]]]
        for m in range(8):
            b, i = nextbank(), m % 2
            tp = project("pg", m, 128, b, (hhi, hlo, th))
            s_ = tmpf[:, i, :]
            t1 = A(lambda e, s_=s_, b=b: e.activation(s_, PB[b][:, :], ACT.Tanh, scale=0.5), tp, *sfree[i])
            free[b] = [t1]
            t1 = V(lambda e, s_=s_, m=m: e.scalar_tensor_tensor(s_, s_, 1.0, PL[:, m, :], ALU.add, ALU.mult), t1, tPL[m])
            tx = V(lambda e, s_=s_, m=m: e.tensor_tensor(xT[:, m, :], xT[:, m, :], s_, ALU.add), t1, tx3[m])
            sfree[i] = [tx]
            tx4.append(tx)
            tq = square_in(xT[:, m, :], m == 0, tx, *(ssq_read if m == 0 else []))
        preload(EXPLN)
        te, tm = rsqrt_rows(7, D, eps_c, rsb[:, :], tq)
        t_out = []
        for m in range(8):
            t1 = V(lambda e, m=m: e.scalar_tensor_tensor(xT[:, m, :], xT[:, m, :], vc(V_LN + m), rsb[:, :],
                                                         ALU.mult, ALU.mult), te, tx4[m])
            t_out.append(DMA(f"o{m % 4}", out_d[m * 128:m * 128 + 128, :], xT[:, m, :], t1))
        assert st.next == len(PLAN)
        pl.close()

        emit(t_out)


def constants():
    i = np.arange(128)
    ii, jj = i[:, None], i[None, :]
    eye = np.eye(128, dtype=np.float32)
    cst = np.zeros((128, NCST), np.float32)
    cst[:, O_IDENT:O_IDENT + 128] = eye
    cst[:, O_NIDENT:O_NIDENT + 128] = -eye
    cst[:, O_ONES:O_ONES + 128] = 1
    inv = np.float32(10000.0) ** (-np.arange(0, 32, 2, dtype=np.float32) / np.float32(32))
    cst[:, O_COL] = inv[i % 16]
    cst[:, O_COL + 1] = np.where(i % 32 < 16, -1, 1)
    cst[:, O_COL + 2] = np.where(i < 32, 1, -1)
    rc = np.zeros((128, NRC), np.float32)
    rc[:, R_NONES:R_NONES + 128] = -1
    rc[:, R_MC:R_MC + 128] = np.where(jj <= ii, 0, NEG)
    rc[:, R_MS:R_MS + 128] = np.where(ii < jj, 0, NEG)
    rc[:, R_MG:R_MG + 128] = np.where((ii // 64 == jj // 64) & (jj >= ii), 0, NEG)
    rc[:, R_TRI:R_TRI + 128] = np.where(ii >= jj, -1, 0)
    gc = np.zeros((128, NGC), np.float32)
    for lv in range(6):
        s = 1 << lv
        gc[:, G_LM + 128 * lv:G_LM + 128 * lv + 128] = (ii // (2 * s) == jj // (2 * s)) & (ii % (2 * s) >= s) & (jj % (2 * s) < s)
    gc[:, G_RM:G_RM + 512] = 1
    gc[0:64, G_RM:G_RM + 512:64] = 0
    return cst, rc, gc


def blocks_of(w, cols, k0=0, kb=None):
    kb = w.shape[0] // 128 - k0 if kb is None else kb
    part = w[128 * k0:128 * (k0 + kb), cols]
    return np.ascontiguousarray(part.reshape(kb, 128, -1).transpose(1, 0, 2)).reshape(-1)


def weights(a):
    w_in, w_in2 = a["w_in"][0], a["w_in_2"][0]
    at = np.cumsum([0, 512, 512, 512, 512, 384, 256, 32, 512, 1024, 1024])
    base = dict(zip(("sbq", "sbk", "sbv", "sz", "cq", "ckv", "kr", "mz", "ga", "gb"), at))
    at2 = np.cumsum([0, 1536, 512, 4, 4, 512, 512, 512, 8])
    base2 = dict(zip(("gqkv", "gz", "g_a", "g_b", "fq", "fk", "fv", "ff"), at2))
    kr = np.zeros((1024, 96), np.float32)
    kr[:, 64:96] = w_in[:, base["kr"]:base["kr"] + 32]
    small = np.zeros((1024, 96), np.float32)
    small[:, 0:4] = w_in2[:, base2["g_a"]:base2["g_a"] + 4]
    small[:, 32:36] = w_in2[:, base2["g_b"]:base2["g_b"] + 4]
    small[:, 64:72] = w_in2[:, base2["ff"]:base2["ff"] + 8]
    ukv = a["w_ukv"][0].reshape(256, 8, 128)
    uk = np.ascontiguousarray(ukv[:, :, 0:64]).reshape(256, 512)
    uv = np.ascontiguousarray(ukv[:, :, 64:128]).reshape(256, 512)
    ada = np.ascontiguousarray(a["w_ada"][0].T)
    every = slice(None)
    out = []
    for name, i, kb, n in chunks():
        c = slice(128 * i, 128 * i + 128)
        if name == "ada":
            out.append(ada[c, :].reshape(-1))
        elif name == "kr":
            out.append(blocks_of(kr, every))
        elif name == "small":
            out.append(blocks_of(small, every))
        elif name in ("sbv", "fv"):
            w, b = (w_in, base["sbv"]) if name == "sbv" else (w_in2, base2["fv"])
            out.append(blocks_of(w, slice(b, b + 512), 2 * i, 2))
        elif name in base:
            out.append(blocks_of(w_in, slice(base[name] + 128 * i, base[name] + 128 * i + 128)))
        elif name in base2:
            out.append(blocks_of(w_in2, slice(base2[name] + 128 * i, base2[name] + 128 * i + 128)))
        elif name == "uq":
            out.append(blocks_of(a["w_uq"][0], slice(288 * i, 288 * i + n)))
        elif name == "uk":
            out.append(blocks_of(uk, every))
        elif name == "uv":
            out.append(blocks_of(uv, every))
        elif name in ("wa", "wb"):
            out.append(blocks_of(a["w_branch_" + name[1]][0], slice(256 * i, 256 * i + 256)))
        elif name == "wo":
            out.append(blocks_of(a["w_out"][0], c))
        elif name == "wo2":
            out.append(blocks_of(a["w_out_2"][0], c))
        elif name == "gt":
            out.append(blocks_of(a["w_gate_up_2"][0], c))
        elif name == "up":
            out.append(blocks_of(a["w_gate_up_2"][0], slice(128 * (FFB + i), 128 * (FFB + i) + 128)))
        elif name == "dn":
            m, q = i // 3, i % 3
            out.append(blocks_of(a["w_down_2"][0], slice(128 * m, 128 * m + 128), 8 * q, kb))
        elif name == "pp":
            out.append(blocks_of(a["w_ple_proj_2"][0], slice(512 * i, 512 * i + 512)))
        elif name == "pg":
            out.append(blocks_of(a["w_ple_gate_2"][0], c))
        assert out[-1].size == 128 * kb * n, (name, i)
    return np.concatenate(out)


def vectors(a):
    v = np.zeros((128, NVEC), np.float32)

    def put(at, x):
        n = x.size // 128
        v[:, at:at + n] = x.reshape(n, 128).T

    put(V_NG, a["norm_gain"])
    put(V_BA, a["b_ada"])
    put(V_AN, a["attn_norm_w_2"])
    put(V_FN, a["ffn_norm_w_2"])
    put(V_PN, a["ple_norm_w_2"])
    put(V_LN, a["final_norm_w_2"])
    put(V_QN, a["q_norm_gain"])
    put(V_KN, a["kv_norm_gain"])
    put(V_GN, a["gdn_norm_w_2"])
    put(V_N1, a["final_norm_gain"])
    v[:, V_CV:V_CV + 48] = a["conv_w_2"][0].reshape(4, 12, 128).transpose(2, 1, 0).reshape(128, 48)
    v[0:4, V_DT] = a["dt_bias_2"][0]
    v[64:72, V_FB] = a["fox_f_bias_2"][0]
    v[0:4, V_AL] = a["a_log_2"][0]
    return v


def layout(inputs):
    a = {k: np.asarray(v) for k, v in inputs.items()}
    cst, rc, gc = constants()
    return {
        "w_all": weights(a), "cst_d": cst, "rc_d": rc, "gc_d": gc, "vec_d": vectors(a),
        "x_d": np.ascontiguousarray(a["x"][0].T), "c_d": np.ascontiguousarray(a["c"]),
        "pos_d": np.ascontiguousarray(a["positions"]), "p_d": np.ascontiguousarray(a["p_2"][0, 0].T),
    }


def kernel(**inputs):
    import concourse.bacc as bacc
    from concourse.bass_utils import run_bass_kernel_spmd

    nc = bacc.Bacc("TRN2", target_bir_lowering=False, num_devices=1)
    arrays = layout(inputs)
    args = [nc.dram_tensor(n, x.shape, mybir.dt.from_np(x.dtype), kind="ExternalInput").ap() for n, x in arrays.items()]
    out = nc.dram_tensor("out_d", (D, S), F32, kind="ExternalOutput").ap()
    build(nc, *args, out)
    r = run_bass_kernel_spmd(nc, [arrays], core_ids=[0])
    return np.ascontiguousarray(r.results[0]["out_d"].T).reshape(1, S, D)
```

```python
import math
from contextlib import ExitStack

import concourse.bass as bass
import numpy as np
from concourse import mybir

F32 = mybir.dt.float32
F32R = mybir.dt.float32r
I32 = mybir.dt.int32
BF16 = mybir.dt.bfloat16
ALU = mybir.AluOpType
ACT = mybir.ActivationFunctionType
AX = mybir.AxisListType

S = 512
D = 1024
NB = D // 128
EPS = 1e-6
NEG = -float(2 ** 100)
FFB = 22
EXPLN = "natural_log_exp_and_others"
SILU = "silu_and_others"

O_IDENT, O_NIDENT, O_ONES, O_NONES, O_TRI, O_COL = 0, 128, 256, 384, 512, 640
NCST = 648
R_MC, R_MS, R_MG = (128 * i for i in range(3))
NRC = 384
G_LM, G_LT = 0, 640
NGC = 768

V_NG, V_BA, V_AN, V_FN, V_PN, V_LN = 0, 8, 32, 40, 48, 56
V_QN, V_KN, V_GN, V_CV = 64, 67, 69, 70
V_DT, V_FB, V_AL, V_N1 = 118, 119, 120, 121
NVEC = 129


def chunks():
    out = [("pp", 0, 2, 512), ("pp", 1, 2, 512)]
    out += [("sbq", i, 8, 128) for i in range(4)] + [("sbk", i, 8, 128) for i in range(4)]
    out += [("sbv", i, 2, 512) for i in range(4)]
    for i in range(8):
        out += [(("cq", i, 8, 128) if i < 3 else ("ckv", i - 3, 8, 128)) if i < 5 else
                ("kr", 0, 8, 96) if i == 5 else ("sz", i - 6, 8, 128), ("ada", 16 + i, 8, 128)]
    out += [("sz", i, 8, 128) for i in (2, 3)] + [("mz", i, 8, 128) for i in range(4)]
    out += [("ga", i, 8, 128) for i in range(8)]
    out += [("uq", 0, 3, 288), ("uq", 1, 3, 288), ("uq", 2, 3, 192), ("uk", 0, 2, 512), ("uv", 0, 2, 512)]
    out += [("gb", i, 8, 128) for i in range(8)]
    out += [("wa", i, 4, 256) for i in range(4)]
    out += [("wb", i, 4, 256) for i in range(4)]
    out += [("wo", i, 8, 128) for i in range(8)]
    out += [("small", 0, 8, 96)] + [("fq", i, 8, 128) for i in range(4)] + [("fk", i, 8, 128) for i in range(4)]
    out += [("fv", i, 2, 512) for i in range(4)]
    out += [("gqkv", i, 8, 128) for i in range(12)] + [("gz", i, 8, 128) for i in range(4)]
    out += [("wo2", i, 8, 128) for i in range(8)]
    for j in range(FFB):
        out += [("gt", j, 8, 128), ("up", j, 8, 128)]
    for m in range(NB):
        out += [("dn", 3 * m, 8, 128), ("dn", 3 * m + 1, 8, 128), ("dn", 3 * m + 2, 6, 128)]
    out += [("pg", i, 8, 128) for i in range(8)]
    return out


def build(nc, w_all, cst_d, rc_d, gc_d, rm_d, vec_d, x_d, c_d, pos_d, ada_d, p_d, out_d):
    PLAN = chunks()
    OFF, at = [], 0
    for _, _, kb, n in PLAN:
        OFF.append(at)
        at += 128 * kb * n

    top = ExitStack()
    with top:
        def sem(n):
            return top.enter_context(nc.semaphore(n))

        queue = {e: [] for e in "SGATV"}
        done = {e: sem("s_" + n) for e, n in zip("GATV", ("pool", "act", "pe", "dve"))}
        count = {e: 0 for e in "GATV"}

        def op(e, fn, *waits, inc=True):
            queue[e].append((waits, fn, inc))
            if inc:
                count[e] += 1
                return (done[e], count[e])
            return None

        def V(fn, *w): return op("V", fn, *w)
        def A(fn, *w): return op("A", fn, *w)
        def G(fn, *w): return op("G", fn, *w)
        def T(fn, *w, inc=False): return op("T", fn, *w, inc=inc)

        dsem = {}

        def DMA(name, dst, src, *w):
            if name not in dsem:
                dsem[name] = [sem("d_" + name), 0]
            d = dsem[name]
            d[1] += 16
            s = d[0]
            queue["S"].append((w, lambda e: e.dma_start(dst, src).then_inc(s, 16), False))
            return (s, d[1])

        def emit(t_out):
            def run(name):
                def body(eng):
                    seen = {}
                    for waits, fn, inc in queue[name]:
                        for s, v in waits:
                            if seen.get(id(s), 0) < v:
                                seen[id(s)] = v
                                eng.wait_ge(s, v)
                        ins = fn(eng)
                        if inc:
                            ins.then_inc(done[name], 1)
                    if name == "S":
                        for s, v in t_out:
                            eng.wait_ge(s, v)
                return body

            with nc.Block() as block:
                block.sync(run("S"))
                block.gpsimd(run("G"))
                block.scalar(run("A"))
                block.vector(run("V"))
                block.tensor(run("T"))

        def GDMA(name, dst, src, *w):
            s = sem("d_" + name)
            queue["G"].append((w, lambda e: e.dma_start(dst, src).then_inc(s, 16), False))
            return (s, 16)

        def sb(stack, name, shape, dt=F32):
            return stack.enter_context(nc.sbuf_tensor(name, shape, dt))

        PB = [top.enter_context(nc.psum_tensor(f"pb{i}", [128, 512], F32)) for i in range(8)]
        free = [[] for _ in range(8)]

        cst = sb(top, "cst", [128, NCST])
        vec = sb(top, "vec", [128, NVEC])
        xT = sb(top, "xT", [128, NB, S])
        NRAW, NHL, LOOK = 3, 4, 2
        raw = sb(top, "raw", [128, NRAW, 1024])
        whi = sb(top, "whi", [128, NHL, 1024], F32R)
        wlo = sb(top, "wlo", [128, NHL, 1024], F32R)
        rcst = sb(top, "rcst", [128, 2, 128], F32R)
        bcst = sb(top, "bcst", [128, 4, 128], BF16)
        sq = sb(top, "sq", [128, 2, S])
        ssq = sb(top, "ssq", [128, S])
        rsb = sb(top, "rsb", [128, S])
        tmpf = sb(top, "tmpf", [128, 2, S])
        mod = sb(top, "mod", [128, 24])
        sc8 = sb(top, "sc8", [128, 16])
        epsc = sb(top, "epsc", [128, 5])

        t_cst = DMA("cst", cst[:, :], cst_d)
        t_vec = DMA("vec", vec[:, :], vec_d)
        ident = cst[:, O_IDENT:O_IDENT + 128]
        ones = cst[:, O_ONES:O_ONES + 128]

        def cb(o):
            return cst[:, o:o + 128]

        def fr(ap):
            return ap.bitcast(F32)

        def vc(i, p0=0, p1=128):
            return vec[p0:p1, i:i + 1]

        with ExitStack() as tmp:
            rcf = sb(tmp, "rcf", [128, NRC])
            t_rcf = DMA("rcf", rcf[:, :], rc_d)
            V(lambda e: e.tensor_copy(bcst[:, 0, :], cb(O_IDENT)), t_cst)
            for i in range(3):
                t_rc = V(lambda e, i=i: e.tensor_copy(bcst[:, i + 1, :], rcf[:, 128 * i:128 * i + 128]), t_rcf)
            V(lambda e: e.tensor_copy(rcst[:, 0, :], cb(O_NONES)), t_cst)
            t_rc = V(lambda e: e.tensor_copy(rcst[:, 1, :], cb(O_TRI)), t_cst)
        identB, mcB, msB, mgB = (bcst[:, i, :] for i in range(4))
        nonesR, triR = rcst[:, 0, :], rcst[:, 1, :]

        class Stream:
            def __init__(self):
                self.dma, self.cv, self.next = 0, 0, 0
                self.tok, self.conv = {}, {}
                self.rawfree = [[] for _ in range(NRAW)]
                self.hlfree = [[] for _ in range(NHL)]
                self.hl = 0

            def load(self, i):
                if i != self.dma or i >= len(PLAN):
                    return
                self.dma += 1
                _, _, kb, n = PLAN[i]
                r = i % NRAW
                src = w_all[OFF[i]:OFF[i] + 128 * kb * n].rearrange("(p n) -> p n", p=128)
                self.tok[i] = DMA(f"raw{r}", raw[:, r, 0:kb * n], src, *self.rawfree[r])

            def convert(self, upto):
                while self.cv < min(upto, len(PLAN)):
                    i = self.cv
                    name, _, kb, n = PLAN[i]
                    r = i % NRAW
                    self.cv += 1
                    if name == "ada":
                        a_ = ada_gate(raw[:, r, :], PLAN[i][1], self.tok[i])
                        self.rawfree[r] = [a_]
                        self.load(i + NRAW)
                        continue
                    h, w = self.hl % NHL, kb * n
                    self.hl += 1
                    src = raw[:, r, 0:w]
                    hi, lo = whi[:, h, 0:w], wlo[:, h, 0:w]
                    th = A(lambda e, a=hi, b=src: e.activation(a, b, ACT.Copy), self.tok[i], *self.hlfree[h])
                    tl = V(lambda e, a=lo, b=src, c=fr(hi): e.tensor_tensor(a, b, c, ALU.subtract),
                           th, *self.hlfree[h])
                    self.rawfree[r] = [th, tl]
                    self.load(i + NRAW)
                    self.conv[i] = (h, tl, hi.rearrange("p (k n) -> p k n", k=kb),
                                    lo.rearrange("p (k n) -> p k n", k=kb))

            def get(self, name, idx, look=LOOK):
                while PLAN[self.next][0] == "ada":
                    self.next += 1
                i = self.next
                assert PLAN[i][:2] == (name, idx), (PLAN[i], name, idx)
                self.next += 1
                self.convert(i + 1 + look)
                h, tl, hi, lo = self.conv.pop(i)
                return hi, lo, tl, h

        st = Stream()
        gate_tok = []

        def ada_gate(w, i, tw):
            t = V(lambda e: e.tensor_tensor_reduce(out=gjunk[0][:, :], in0=w, in1=gcb[0][:, :], scale=1.0, scalar=0.0,
                                                   op0=ALU.mult, op1=ALU.add, accum_out=mod[:, i:i + 1]),
                  tw, *gcb[1], *gate_tok[-1:])
            gate_tok.append(t)
            return t
        gjunk, gcb = [None], [None, []]

        def mm3(out, lh, ll, rh, rl, start, stop, *w):
            T(lambda e: e.matmul(out, lh, rl, start=start, stop=False, skip_group_check=True), *w)
            T(lambda e: e.matmul(out, ll, rh, start=False, stop=False, skip_group_check=True))
            return T(lambda e: e.matmul(out, lh, rh, start=False, stop=stop, skip_group_check=True), inc=True)

        def project(name, idx, m, bank, act, n0=0, kbs=None, start=True, stop=True, chunk=None, order=None):
            hi, lo, tw, slot = chunk or st.get(name, idx)
            ah, al, at_ = act
            kbs = list(kbs or range(hi.shape[1]))
            qs_ = list(order or range(len(kbs)))
            for q in qs_:
                k, first = kbs[q], q == qs_[0]
                w = [at_[k]]
                if first:
                    w += [tw] + (free[bank] if start else [])
                t = mm3(PB[bank][0:m, :], hi[:, q, n0:n0 + m], lo[:, q, n0:n0 + m], ah[:, k, :], al[:, k, :],
                        start and first, stop and q == qs_[-1], *w)
            st.hlfree[slot] = [t]
            return t

        def group(items):
            return [(st.get(name, idx, look=0), m, bank) for name, idx, m, bank in items]

        def project_group(chs, act, order=range(8)):
            ah, al, at_ = act
            order = list(order)
            toks = []
            for k in order:
                for (hi, lo, tw, slot), m, bank in chs:
                    w = [at_[k]] + ([tw] + free[bank] if k == order[0] else [])
                    t = mm3(PB[bank][0:m, :], hi[:, k, 0:m], lo[:, k, 0:m], ah[:, k, :], al[:, k, :],
                            k == order[0], k == order[-1], *w)
                    if k == order[-1]:
                        st.hlfree[slot] = [t]
                        toks.append(t)
            st.convert(st.next + LOOK)
            return toks

        def project_nat(name, count_, kper, banks, act):
            ah, al, at_ = act
            last = count_ * kper - 1
            for c in range(count_):
                hi, lo, tw, slot = st.get(name, c)
                for q in range(kper):
                    k = c * kper + q
                    for t in range(4):
                        cs = slice(128 * t, 128 * t + 128)
                        w = [at_[k], tw] + (free[banks[t]] if k == 0 else [])
                        tok = mm3(PB[banks[t]][:, :], ah[:, k, cs], al[:, k, cs], hi[:, q, :], lo[:, q, :],
                                  k == 0, k == last, *w)
                st.hlfree[slot] = [tok]
            return tok

        def split(f, hi, lo, tf, *w):
            th = A(lambda e: e.activation(hi, f, ACT.Copy), tf, *w)
            return V(lambda e: e.tensor_tensor(lo, f, fr(hi), ALU.subtract), th, tf, *w)

        sqfree = [[], []]
        sqn = [0]

        def square_in(src, first, tsrc, *w):
            i = sqn[0] % 2
            sqn[0] += 1
            dst = ssq[:, :] if first else sq[:, i, :]
            ts = A(lambda e: e.activation(dst, src, ACT.Square), tsrc, *w, *([] if first else sqfree[i]))
            if not first:
                prev = square_in.tok
                ts = V(lambda e: e.tensor_tensor(ssq[:, :], ssq[:, :], dst, ALU.add), ts, prev)
                sqfree[i] = [ts]
            square_in.tok = ts
            return ts

        ssq_read = [[]]

        def rsqrt_rows(bank, n, eps_n, dst, tsrc, bias=0.0, src=None, *w):
            src = ssq[:, :] if src is None else src
            tm = T(lambda e: e.matmul(PB[bank][:, :], ones, src, start=True, stop=True), tsrc, *free[bank], inc=True)
            tl = A(lambda e: e.activation(dst, PB[bank][:, :], ACT.Ln, bias=eps_n, scale=1.0 / n), tm, *w)
            free[bank] = [tl]
            te = A(lambda e: e.activation(dst, dst, ACT.Exp, scale=-0.5, bias=bias), tl)
            return te, tm

        def fence():
            return [(done[e], count[e]) for e in "GATV" if count[e]]

        def norm_split(gcol, te, tok_x, hhi, hlo, hfree, rs=None):
            rs = rsb[:, :] if rs is None else rs
            toks, reads = [], []
            fb = [[], []]
            for b in range(NB):
                t = tmpf[:, b % 2, :]
                tf = V(lambda e, t=t, b=b: e.scalar_tensor_tensor(t, xT[:, b, :], gcol(b), rs, ALU.mult, ALU.mult),
                       te, tok_x[b], *fb[b % 2], *hfree)
                reads.append(tf)
                tl = split(t, hhi[:, b, :], hlo[:, b, :], tf, *hfree)
                fb[b % 2] = [tl]
                toks.append(tl)
            return toks, reads

        V(lambda e: e.memset(epsc[:, 0:1], EPS))
        V(lambda e: e.memset(epsc[:, 1:2], 1.0))
        V(lambda e: e.memset(epsc[:, 2:3], math.log(128 ** -0.5)))
        V(lambda e: e.memset(epsc[:, 4:5], EPS * EPS))
        t_eps = V(lambda e: e.memset(epsc[:, 3:4], math.pi / 2))
        eps_c, one_c, dk_c, hpi_c, eps2_c = (epsc[:, i:i + 1] for i in range(5))

        def preload(name, *w):
            queue["A"].append((w, lambda e: e.preload_act_table_set(name), False))

        ple = nc.dram_tensor("ple_scratch", (D, S), F32, kind="Internal").ap()
        one = ExitStack()
        with one:
            zs = sb(one, "zs", [128, 8, S])
            cosk, sink = (sb(one, n, [128, S]) for n in ("cosk", "sink"))
            krs = sb(one, "krs", [96, S])
            gbt = sb(one, "gbt", [128, NB, S])
            hhi = sb(one, "hhi", [128, NB, S], F32R)
            hlo = sb(one, "hlo", [128, NB, S], F32R)
            gst = ExitStack()
            cbt = sb(gst, "cbt", [128, D])
            junk = sb(gst, "junk", [128, D], BF16)
            pre = ExitStack()
            pf = sb(pre, "pf", [128, 2, S])
            phi = sb(pre, "phi", [128, 2, S], F32R)
            plo = sb(pre, "plo", [128, 2, S], F32R)
            adab = sb(pre, "adab", [128, 8, D])
            posi = sb(pre, "posi", [128, S], I32)
            ang = sb(pre, "ang", [128, S])
            rn = sb(pre, "rn", [128, S])
            rk = sb(pre, "rk", [128, S])
            t_c = GDMA("c", cbt[:, :], c_d.to_broadcast([128, D]))
            t_pos = GDMA("pos", posi[:, :], pos_d.to_broadcast([128, S]))
            t_x = [DMA(f"x{b}", xT[:, b, :], x_d[b * 128:b * 128 + 128, :]) for b in range(NB)]
            t_ada = [DMA(f"ada{i}", adab[:, i, :], ada_d[128 * i:128 * i + 128, :]) for i in range(8)]
            t_p = DMA("p", pf[:, :, :], p_d.rearrange("(a p) n -> p a n", p=128))
            for i in range(NRAW):
                st.load(i)

            t = G(lambda e: e.tensor_copy(ang[:, :], posi[:, :]), t_pos)
            t = G(lambda e: e.tensor_scalar(ang[:, :], ang[:, :], cst[:, O_COL:O_COL + 1], None, ALU.mult), t, t_cst)
            parts, rest = [], 2 * math.pi
            for _ in range(4):
                q = 2.0 ** (math.floor(math.log2(rest)) - 11)
                parts.append(math.floor(rest / q) * q)
                rest -= parts[-1]
            for step_ in (2048.0, 1.0):
                t = G(lambda e, s_=step_: e.tensor_scalar(rn[:, :], ang[:, :], 1 / (2 * math.pi * s_), 12582912.0,
                                                          ALU.mult, ALU.add), t)
                t = G(lambda e: e.tensor_scalar(rn[:, :], rn[:, :], 12582912.0, None, ALU.subtract), t)
                for pt in parts:
                    t = G(lambda e, k=-step_ * pt: e.tensor_scalar(rk[:, :], rn[:, :], k, None, ALU.mult), t)
                    t = G(lambda e: e.tensor_tensor(ang[:, :], ang[:, :], rk[:, :], ALU.add), t)
            lim = float(np.float32(3.1415925))
            t_ang = G(lambda e: e.tensor_scalar(ang[:, :], ang[:, :], lim, -lim, ALU.min, ALU.max), t)

            preload(EXPLN)
            for b in range(NB):
                i = b % 2
                ts = A(lambda e, b=b, i=i: e.activation(sq[:, i, :], xT[:, b, :], ACT.Square), t_x[b], *sqfree[i])
                tm = T(lambda e, b=b, i=i: e.matmul(PB[7][:, :], ones, sq[:, i, :], start=b == 0, stop=b == 7),
                       ts, t_cst, inc=True)
                sqfree[i] = [tm]
            tl = A(lambda e: e.activation(rsb[:, :], PB[7][:, :], ACT.Ln, bias=eps_c, scale=1.0 / D), tm, t_eps)
            te = A(lambda e: e.activation(rsb[:, :], rsb[:, :], ACT.Exp, scale=-0.5), tl)
            free[7] = [tl]
            t_xr = [V(lambda e, b=b: e.tensor_tensor(xT[:, b, :], xT[:, b, :], rsb[:, :], ALU.mult), te, t_x[b])
                    for b in range(NB)]

            def ada(which):
                for i in which:
                    t = V(lambda e, i=i: e.tensor_tensor_reduce(
                        out=junk[:, :], in0=adab[:, i % 8, :], in1=cbt[:, :], scale=1.0, scalar=0.0, op0=ALU.mult,
                        op1=ALU.add, accum_out=mod[:, i:i + 1]), t_ada[i], t_c, *gate_tok[-1:])
                    gate_tok.append(t)
                    if i < 8:
                        t_ada.append(DMA(f"ada{8 + i}", adab[:, i, :], ada_d[1024 + 128 * i:1152 + 128 * i, :], t))

            ada(range(8))

            tpl = [split(pf[:, k, :], phi[:, k, :], plo[:, k, :], t_p) for k in range(2)]
            gjunk[0], gcb[0], gcb[1] = junk, cbt, [t_c]
            t_ple = []
            for i in range(2):
                ch = st.get("pp", i, 0)
                for q in range(4):
                    m = 4 * i + q
                    b = m % 4
                    tp = project(None, None, 128, b, (phi, plo, tpl), n0=128 * q, chunk=ch)
                    te = A(lambda e, m=m, b=b: e.activation(zs[:, m, :], PB[b][:, :], ACT.Copy, scale=0.5), tp, t_rc)
                    free[b] = [te]
                    t_ple.append(DMA("ple", ple[128 * m:128 * m + 128, :], zs[:, m, :], te))
            t_ple = t_ple[-1]

            ada(range(8, 16))
            t = gate_tok[-1]
            t = V(lambda e: e.tensor_tensor(mod[:, 0:16], mod[:, 0:16], vec[:, V_BA:V_BA + 16], ALU.add), t, t_vec)
            t_mod = V(lambda e: e.scalar_tensor_tensor(sc8[:, 0:8], mod[:, 8:16], 1.0, vec[:, V_NG:V_NG + 8],
                                                       ALU.add, ALU.mult), t)
            chs = group([("sbq", i, 128, i) for i in range(4)])
            th, fb = [], [[], []]
            t_xused = []
            for b in range(NB):
                y = tmpf[:, b % 2, :]
                tf = V(lambda e, y=y, b=b: e.tensor_scalar(y, xT[:, b, :], sc8[:, b:b + 1], mod[:, b:b + 1],
                                                           ALU.mult, ALU.add), t_mod, t_xr[b], *fb[b % 2])
                t_xused.append(tf)
                tl = split(y, hhi[:, b, :], hlo[:, b, :], tf)
                fb[b % 2] = [tl]
                th.append(tl)
            h1 = (hhi, hlo, th)

            def drain(g):
                for _ in g:
                    pass

            def step(g, n=1):
                for _ in range(n):
                    next(g, None)

            ring = [0]

            def nextbank(n=4):
                b = ring[0] % n
                ring[0] += 1
                return b

            preload(SILU)
            ts = A(lambda e: e.activation(sink[:, :], ang[:, :], ACT.Sin), t_ang, t_rc)
            tc = A(lambda e: e.activation(rn[:, :], ang[:, :], ACT.Abs), t_ang)
            t_cos = A(lambda e: e.activation(cosk[:, :], rn[:, :], ACT.Sin, scale=-1.0, bias=hpi_c), tc, t_eps)
            preload(EXPLN)
            t_rope = V(lambda e: e.tensor_scalar(sink[:, :], sink[:, :], cst[:, O_COL + 1:O_COL + 2], None, ALU.mult), ts)
            f_pre = fence()
            pre.close()

            gax = xT
            LEN = [512, 384, 256, 128]
            BK = [0, 1, 2, 1]
            BO = [0, 0, 0, 384]
            SO = [0, 512, 1024, 896]
            THIRDS = ((0, 512), (1, 512), (2, 256))
            qs = 96 ** -0.5
            SWAP = [(i + 16) % 32 for i in range(32)]
            rope_free, rope_pool = [[*fb[0], *fb[1]], [t_xr[-1]]], []
            ropes, square_reads = [0], {}
            tga, tgb, tzs, tcq = [None] * 8, [None] * 8, [None] * 8, [None] * 5
            late = {}

            def rope(bank, dst, tp, *w):
                i = ropes[0] % 2
                ropes[0] += 1
                buf = (tmpf, sq)[i]
                if i:
                    w0 = (*sqfree[0], *sqfree[1])
                else:
                    w0 = ()
                x, r0, r1 = PB[bank][64:96, :], buf[64:96, 0, :], buf[64:96, 1, :]
                t1 = V(lambda e: e.stream_shuffle(r0, x, SWAP), tp, *rope_free[i], *w0)
                t2 = V(lambda e: e.tensor_tensor(r1, x, cosk[64:96, :], ALU.mult), tp, t_cos, *rope_free[i], *w0)
                t1 = V(lambda e: e.tensor_tensor(r0, r0, sink[64:96, :], ALU.mult), t1, t_rope)
                t3 = G(lambda e: e.tensor_tensor(dst, r0, r1, ALU.add), t1, t2, *rope_pool, *w)
                rope_free[i] = [t3]
                rope_pool[:] = [t3]
                if i:
                    sqfree[0], sqfree[1] = [t3], [t3]
                return t2, t3

            def latent_norm(lo_, n_, g_, rk):
                te, tm = rsqrt_rows(7, rk, eps_c, rsb[:, :], square_in.tok, 0.0, None, *t_xr, *(late["rsb"] if lo_ else []))
                ssq_read[0] = [tm]
                for m in range(n_):
                    k = lo_ + m
                    tcq[k] = V(lambda e, k=k, g=g_ + m: e.scalar_tensor_tensor(
                        gbt[:, k, :], gbt[:, k, :], vc(g), rsb[:, :], ALU.mult, ALU.mult), te, square_reads[k])
                late["rsb"] = [tcq[lo_ + n_ - 1]]

            def filler_a():
                for m in range(5):
                    tp = project(*(("cq", m) if m < 3 else ("ckv", m - 3)), 128, 7, h1)
                    tcq[m] = V(lambda e, m=m: e.tensor_copy(gbt[:, m, :], PB[7][:, :]), tp)
                    free[7] = [tcq[m]]
                    if m == 3:
                        latent_norm(0, 3, V_QN, 384)
                    square_reads[m] = square_in(gbt[:, m, :], m in (0, 3), tcq[m], *(ssq_read[0] if m in (0, 3) else []))
                    yield
                tp = project("kr", 0, 96, 7, h1)
                t2, late["kr"] = rope(7, krs[64:96, :], tp)
                free[7] = [t2]
                latent_norm(3, 2, V_KN, 256)
                yield
                for m in range(8):
                    tp = project(*(("sz", m) if m < 4 else ("mz", m - 4)), 128, 7, h1)
                    tzs[m] = V(lambda e, m=m: e.tensor_copy(zs[:, m, :], PB[7][:, :]), tp, t_ple)
                    free[7] = [tzs[m]]
                    yield
                for m in range(8):
                    tp = project("ga", m, 128, 7, h1)
                    tga[m] = V(lambda e, m=m: e.tensor_copy(gax[:, m, :], PB[7][:, :]), tp, t_xused[m])
                    free[7] = [tga[m]]
                    yield

            fa = filler_a()
            t_oa = [None] * 4
            with ExitStack() as s1:
                qp = sb(s1, "qp", [128, 8, S])
                kp = sb(s1, "kp", [128, 4, S])
                sbv = sb(s1, "sbv", [128, 4, S])
                sp = sb(s1, "sp", [128, 2, 1280])
                sph = sb(s1, "sph", [128, 1280], F32R)
                spl = sb(s1, "spl", [128, 1280], F32R)
                tz = []
                for r in range(2):
                    tz.append(G(lambda e, r=r: e.memset(
                        qp[64 - 64 * r:128 - 64 * r, :, :].rearrange("p (m r) n -> p m r n", r=2)[:, :, r, :], 0.0),
                        *f_pre, *tz))
                tqp, tkp = [], []
                tps = project_group(chs, h1)

                def evac_q(m, b, tp):
                    for r in range(2):
                        te = A(lambda e, b=b, m=m, r=r: e.activation(
                            qp[64 * r:64 * r + 64, 2 * m + r, :], PB[b][64 * r:64 * r + 64, :], ACT.Copy, scale=0.125),
                            tp, *f_pre)
                        tqp.append(te)
                    free[b] = [te]
                for m in range(4):
                    evac_q(m, m, tps[m])
                for m in range(4):
                    b = 4 + m % 4
                    tp = project("sbk", m, 128, b, h1)
                    te = V(lambda e, b=b, m=m: e.tensor_copy(kp[:, m, :], PB[b][:, :]), tp, *f_pre)
                    free[b] = [te]
                    tkp.append(te)
                tp = project_nat("sbv", 4, 2, [3, 4, 5, 6], h1)
                for t_ in range(4):
                    te = A(lambda e, t_=t_: e.activation(sbv[:, t_, :], PB[3 + t_][:, :], ACT.Copy), tp, *f_pre)
                    free[3 + t_] = [te]
                t_sbv = te
                use = [f_pre, f_pre]
                useh = [f_pre]
                tqk, tmx, tsp, tln = {}, {}, {}, {}

                def sb_qk(h):
                    z = 3 * (h % 2)
                    for kb in (0, 1, 3, 2):
                        n, o = LEN[kb], BO[kb]
                        out = PB[z + BK[kb]][:, o:o + n]
                        T(lambda e, out=out, kb=kb, first=kb != 3: e.matmul(
                            out, kp[:, h // 2, 128 * kb:128 * kb + 128], qp[:, h, 128 * kb:512],
                            start=first, stop=False, skip_group_check=True), tqp[h], tz[h % 2], tkp[h // 2], *free[z + BK[kb]])
                        tqk[h] = T(lambda e, out=out: e.matmul(out[:, 0:128], identB, msB, start=False, stop=False,
                                                               skip_group_check=True), t_rc, inc=True)

                def sb_pre(h):
                    z, i = 3 * (h % 2), h % 2
                    for b, n in THIRDS:
                        t1 = V(lambda e, b=b, n=n: e.tensor_scalar(sp[:, i, 512 * b:512 * b + n], PB[z + b][:, 0:n], 40.0,
                                                                   None, ALU.min), tqk[h], *use[i])
                    t1 = A(lambda e: e.activation(sp[:, i, :], sp[:, i, :], ACT.Exp), t1)
                    t1 = A(lambda e: e.activation(sp[:, i, :], sp[:, i, :], ACT.Ln, bias=one_c), t1)
                    tln[h] = t1

                def sb_pre2(h):
                    z, i, t1 = 3 * (h % 2), h % 2, tln[h]
                    for b, n in THIRDS:
                        v = sp[:, i, 512 * b:512 * b + n]
                        t2 = V(lambda e, b=b, n=n, v=v: e.tensor_tensor(v, PB[z + b][:, 0:n], v, ALU.max), t1)
                    tmx[h] = t2
                    t3 = G(lambda e: e.tensor_copy(sph[:, :], sp[:, i, :]), t2, tz[1], *rope_pool, *useh[0])
                    tsp[h] = G(lambda e: e.tensor_tensor(spl[:, :], sp[:, i, :], fr(sph[:, :]), ALU.subtract), t3)

                def sb_suffix(h):
                    z, i = 3 * (h % 2), h % 2
                    for kb in range(4):
                        out = PB[z + BK[kb]][:, BO[kb] + 128 * (3 - kb):BO[kb] + 128 * (4 - kb)]
                        w = cb(O_TRI if kb == 3 else O_NONES)
                        tk = T(lambda e, out=out, w=w: e.matmul(out, w, sp[:, i, 896:1024], start=False, stop=False,
                                                                skip_group_check=True), tmx[h], inc=True)
                    for kb in range(3):
                        for jb in range(kb, 3):
                            o = BO[kb] + 128 * (jb - kb)
                            out = PB[z + BK[kb]][:, o:o + LEN[jb]]
                            w = triR if jb == kb else nonesR
                            for src in (sph, spl):
                                v = src[:, SO[jb]:SO[jb] + LEN[jb]]
                                tk = T(lambda e, out=out, w=w, v=v: e.matmul(out, w, v, start=False, stop=False,
                                                                             skip_group_check=True),
                                       tsp[h], inc=True)
                    useh[0] = [tk]
                    for b, n in THIRDS:
                        te = A(lambda e, b=b, n=n: e.activation(sp[:, i, 512 * b:512 * b + n], PB[z + b][:, 0:n], ACT.Exp),
                               tk, tsp[h])
                        free[z + b] = [te]
                    return te

                def sb_pv(h, tw):
                    r0, pr, i = 64 * (h % 2), h // 2, h % 2
                    for kb in range(4):
                        tk = T(lambda e, kb=kb: e.matmul(
                            PB[6][r0:r0 + 64, 128 * kb:512], sbv[:, kb, 64 * h:64 * h + 64],
                            sp[:, i, SO[kb]:SO[kb] + LEN[kb]], start=kb == 0, stop=kb == 3, skip_group_check=True),
                            tw, t_sbv, *free[6], inc=True)
                    use[i] = [tk]
                    if h % 2:
                        te = V(lambda e: e.tensor_copy(qp[:, 2 * pr, :], PB[6][:, :]), tk, tqk[h], tqk[h - 1])
                        free[6] = [te]
                        t_oa[pr] = te

                sb_qk(0)
                sb_pre(0)
                sb_pre2(0)
                step(fa, 1)
                for h in range(8):
                    if h < 7:
                        sb_qk(h + 1)
                    step(fa)
                    tw = sb_suffix(h)
                    if h < 7:
                        sb_pre(h + 1)
                        step(fa)
                        sb_pre2(h + 1)
                    if h == 6:
                        preload(SILU)
                        for m in range(8):
                            tzs[m] = A(lambda e, m=m: e.activation(zs[:, m, :], zs[:, m, :], ACT.Silu), tzs[m])
                        preload(EXPLN)
                    sb_pv(h, tw)
                    if h in (0, 2, 4, 6):
                        step(fa)
                for m in range(4):
                    tzs[m] = V(lambda e, m=m: e.tensor_tensor(zs[:, m, :], zs[:, m, :], qp[:, 2 * m, :], ALU.mult),
                               tzs[m], t_oa[m])
                f1 = fence()
            gst.close()

            s2 = ExitStack()
            qc = sb(s2, "qc", [128, 8, S])
            kc = sb(s2, "kc", [128, 8, S])
            vb = sb(s2, "vb", [128, 4, S])
            s3 = ExitStack()
            chi = sb(s3, "chi", [128, 5, S], F32R)
            clo = sb(s3, "clo", [128, 5, S], F32R)
            tcl = [split(gbt[:, k, :], chi[:, k, :], clo[:, k, :], tcq[k], *f1) for k in range(5)]
            cact = (chi, clo, tcl)
            drain(fa)
            t_kc = V(lambda e: e.tensor_scalar(kc[64:96, :, :], krs[64:96, :].rearrange("p (a b) -> p a b", a=1)
                                               .to_broadcast([32, 8, S]), qs, None, ALU.mult), late["kr"], *f1)
            tqc, tkc = [], []
            for h in range(8):
                if h in (0, 3, 6):
                    ch = st.get("uq", h // 3)
                b = nextbank()
                tp = project(None, None, 96, b, cact, n0=96 * (h % 3), chunk=ch)
                te = A(lambda e, h=h, b=b: e.activation(qc[0:64, h, :], PB[b][0:64, :], ACT.Copy), tp, *f1)
                t2, t3 = rope(b, qc[64:96, h, :], tp, *f1)
                free[b] = [te, t2]
                tqc.append((te, t3))
            ch = st.get("uk", 0)
            for p_ in range(4):
                b = nextbank()
                tp = project(None, None, 128, b, (chi[:, 3:5, :], clo[:, 3:5, :], tcl[3:5]), n0=128 * p_, chunk=ch)
                t1 = A(lambda e, p_=p_, b=b: e.activation(kc[0:64, 2 * p_, :], PB[b][0:64, :], ACT.Copy, scale=qs), tp, *f1)
                t2 = V(lambda e, p_=p_, b=b: e.tensor_scalar(kc[0:64, 2 * p_ + 1, :], PB[b][64:128, :], qs, None, ALU.mult),
                       tp, *f1)
                free[b] = [t1, t2]
                tkc.append((t1, t2))
            hi, lo, tw, slot = st.get("uv", 0)
            for t_ in range(4):
                cs = slice(128 * t_, 128 * t_ + 128)
                b = 3 + t_
                for k in range(2):
                    tok = mm3(PB[b][:, :], chi[:, 3 + k, cs], clo[:, 3 + k, cs], hi[:, k, :], lo[:, k, :],
                              k == 0, k == 1, tw, tcl[3 + k], *free[b])
                t_vb = A(lambda e, t_=t_, b=b: e.activation(vb[:, t_, :], PB[b][:, :], ACT.Copy), tok, *f1)
                free[b] = [t_vb]
            st.hlfree[slot] = [tok]
            preload(SILU)
            for m in range(8):
                tga[m] = A(lambda e, m=m: e.activation(gax[:, m, :], gax[:, m, :], ACT.Tanh, scale=0.5), tga[m])
            preload(EXPLN)
            f_c = [tok, t_vb, t_kc]
            s3.close()
            t_oh = []

            def filler_b():
                for m in range(8):
                    b = 7
                    tp = project("gb", m, 128, b, h1)
                    tgb[m] = V(lambda e, m=m, b=b: e.tensor_copy(gbt[:, m, :], PB[b][:, :]), tp, *tcl)
                    free[b] = [tgb[m]]
                    if m == 7:
                        late["gb"] = tp
                        t_oh.extend(split(zs[:, k, :], hhi[:, k, :], hlo[:, k, :], tzs[k], tp) for k in range(4))
                    yield
                for i in range(4):
                    ch = st.get("wa", i)
                    for q in range(2):
                        m, b = 2 * i + q, 7
                        tp = project(None, None, 128, b, (hhi, hlo, t_oh), n0=128 * q, chunk=ch)
                        tga[m] = V(lambda e, m=m, b=b: e.scalar_tensor_tensor(gax[:, m, :], gax[:, m, :], 1.0, PB[b][:, :],
                                                                              ALU.add, ALU.mult), tp, tga[m])
                        free[b] = [tga[m]]
                        yield

            QB, QO = [1, 2, 1, 0], [384, 0, 0, 0]
            QN = [128, 256, 384, 512]
            PO = [896, 1024, 512, 0]

            def softmax_attention(pfx, scr, f0, q_of, k_of, tq_of, v_all, tv, combine, fill, nfill, cbias=None):
                P = sb(scr, pfx + "P", [128, 1280])
                PT = sb(scr, pfx + "PT", [128, 1280])
                nm = sb(scr, pfx + "nm", [128, 2, 4])
                rs = sb(scr, pfx + "rs", [128, 2, 4])
                state = {"P": f0, "PT": f0}
                texp = {}

                def qk(h):
                    for qi in (3, 2, 0, 1):
                        o, n, b = QO[qi], QN[qi], QB[qi]
                        out = PB[b][:, o:o + n]
                        T(lambda e, out=out, q_=q_of(h, qi), k_=k_of(h, n), qi=qi: e.matmul(
                            out, q_, k_, start=qi != 0, stop=False, skip_group_check=True), *tq_of(h), *free[b])
                        tk = T(lambda e, out=out, n=n, qi=qi: e.matmul(
                            out[:, n - 128:n], identB, mcB, start=False, stop=qi != 2, skip_group_check=True), inc=True)
                    if cbias:
                        cbias("used", h, tk)
                    i = h % 2
                    src = {qi: PB[QB[qi]][:, QO[qi]:QO[qi] + QN[qi]] for qi in range(4)}
                    cb_, tcb = cbias("get", h, None) if cbias else (None, None)
                    for qi in (3, 2, 0, 1):
                        d = P[:, PO[qi]:PO[qi] + QN[qi]]
                        if cbias:
                            tm = V(lambda e, s_=src[qi], qi=qi, d=d: e.tensor_tensor_reduce(
                                out=d, in0=s_, in1=cb_[:, 0:QN[qi]], scale=1.0, scalar=-3.0e38, op0=ALU.add, op1=ALU.max,
                                accum_out=nm[:, i, qi:qi + 1]), tk, tcb, *state["P"])
                        else:
                            tm = V(lambda e, s_=src[qi], qi=qi: e.tensor_reduce(nm[:, i, qi:qi + 1], s_, AX.X, ALU.max),
                                   tk, *state["P"])
                    if cbias:
                        cbias("done", h, tm)
                    tm2 = V(lambda e: e.tensor_scalar(nm[:, i, :], nm[:, i, :], -1.0, None, ALU.mult), tm)
                    for qi in (3, 2, 0, 1):
                        d = P[:, PO[qi]:PO[qi] + QN[qi]]
                        te = A(lambda e, s_=d if cbias else src[qi], qi=qi, d=d: e.activation(
                            d, s_, ACT.Exp, bias=nm[:, i, qi:qi + 1], accum_out=rs[:, i, qi:qi + 1]), tm2, *state["P"])
                    for b in range(3):
                        free[b] = [tm] if cbias else [te]
                    tr = V(lambda e: e.reciprocal(rs[:, i, :], rs[:, i, :]), te)
                    for qi in (3, 2, 0, 1):
                        d = P[:, PO[qi]:PO[qi] + QN[qi]]
                        texp[h] = V(lambda e, qi=qi, d=d: e.tensor_scalar(d, d, rs[:, i, qi:qi + 1], None, ALU.mult), tr, te)

                def turn(h):
                    toks = []
                    for kb, b, o in ((0, 3, 0), (1, 4, 0), (3, 4, 384), (2, 6, 0)):
                        for qi in range(kb, 4):
                            src = P[:, PO[qi] + 128 * kb:PO[qi] + 128 * kb + 128]
                            dst = PB[b][:, o + 128 * (qi - kb):o + 128 * (qi - kb) + 128]
                            tk = T(lambda e, src=src, dst=dst: e.transpose(dst, src, ident), texp[h], *free[b], inc=True)
                        if kb == 1:
                            continue
                        n, d0 = {0: (512, 0), 3: (512, 512), 2: (256, 1024)}[kb]
                        dd, ss = PT[:, d0:d0 + n], PB[b][:, 0:n]
                        if kb == 3:
                            te = A(lambda e, dd=dd, ss=ss: e.activation(dd, ss, ACT.Copy), tk, *state["PT"])
                        else:
                            te = V(lambda e, dd=dd, ss=ss: e.tensor_copy(dd, ss), tk, *state["PT"])
                        free[b] = [te]
                        toks.append(te)
                    state["P"] = [tk]
                    return toks

                def pv(h, toks):
                    r0 = 64 * (h % 2)
                    for kb in range(4):
                        tk = T(lambda e, kb=kb: e.matmul(
                            PB[5][r0:r0 + 64, 128 * kb:512], v_all[:, kb, 64 * h:64 * h + 64],
                            PT[:, SO[kb]:SO[kb] + LEN[kb]], start=kb == 0, stop=kb == 3, skip_group_check=True),
                            *toks, *tv, *free[5], inc=True)
                    state["PT"] = [tk]
                    if h % 2:
                        free[5] = [combine(h // 2, 5, tk)]

                qk(0)
                step(fill, nfill)
                for h in range(8):
                    toks = turn(h)
                    if h < 7:
                        qk(h + 1)
                    step(fill, nfill)
                    pv(h, toks)
                    step(fill, nfill)
                    yield

            def comb(pr, bank, tk):
                tzs[4 + pr] = V(lambda e: e.tensor_tensor(zs[:, 4 + pr, :], zs[:, 4 + pr, :], PB[bank][:, :], ALU.mult),
                                tk, tzs[4 + pr])
                r = tzs[4 + pr]
                if "gb" in late:
                    while late["oh"] <= pr:
                        k = 4 + late["oh"]
                        t_oh.append(split(zs[:, k, :], hhi[:, k, :], hlo[:, k, :], tzs[k], late["gb"]))
                        late["oh"] += 1
                return r

            late["oh"] = 0
            fw = filler_b()
            drain(softmax_attention(
                "m", s2, f_c, lambda h, qi: qc[0:96, h, 128 * qi:128 * qi + 128], lambda h, n: kc[0:96, h, 0:n],
                lambda h: (*tqc[h], *tkc[h // 2], t_kc), vb, [t_vb], comb, fw, 1))
            drain(fw)
            f2 = fence()
            s2.close()

            s5 = ExitStack()
            mhi = sb(s5, "mhi", [128, NB, S], F32R)
            mlo = sb(s5, "mlo", [128, NB, S], F32R)
            t_gate = V(lambda e: e.tensor_tensor(mod[:, 16:24], mod[:, 16:24], vec[:, V_BA + 16:V_BA + 24], ALU.add),
                       gate_tok[-1])
            t_gate = V(lambda e: e.tensor_scalar(mod[:, 16:24], mod[:, 16:24], 0.5, None, ALU.mult), t_gate)
            preload(SILU)
            tmg = []
            t_x = []
            for i in range(4):
                ch = st.get("wb", i)
                for q in range(2):
                    m, b = 2 * i + q, nextbank()
                    tgb[m] = A(lambda e, m=m: e.activation(gbt[:, m, :], gbt[:, m, :], ACT.Tanh, scale=0.5), tgb[m])
                    tp = project(None, None, 128, b, (hhi[:, 4:8, :], hlo[:, 4:8, :], t_oh[4:8]), n0=128 * q, chunk=ch)
                    t1 = V(lambda e, m=m, b=b: e.scalar_tensor_tensor(gbt[:, m, :], gbt[:, m, :], 1.0, PB[b][:, :],
                                                                      ALU.add, ALU.mult), tp, tgb[m])
                    free[b] = [t1]
                    t1 = V(lambda e, m=m: e.tensor_tensor(gbt[:, m, :], gbt[:, m, :], gax[:, m, :], ALU.add), t1, tga[m])
                    t_x.append(GDMA(f"xx{m}", xT[:, m, :], x_d[m * 128:m * 128 + 128, :], t1))
                    tmg.append(split(gbt[:, m, :], mhi[:, m, :], mlo[:, m, :], t1, *f2))
            ssq2 = sb(s5, "ssq2", [128, S])
            t_g12 = V(lambda e: e.tensor_tensor(sc8[:, 8:16], vec[:, V_N1:V_N1 + 8], vec[:, V_AN:V_AN + 8], ALU.mult), t_vec)
            preload(EXPLN)
            tx1 = []
            chs = [(st.get("wo", m), 128, 4 + m) for m in range(2)]
            tps = project_group(chs, (mhi, mlo, tmg))
            for m in range(8):
                b = 4 + m if m < 2 else nextbank()
                tp = tps[m] if m < 2 else project("wo", m, 128, b, (mhi, mlo, tmg))
                tx = V(lambda e, m=m, b=b: e.scalar_tensor_tensor(
                    xT[:, m, :], PB[b][:, :], mod[:, 16 + m:17 + m], xT[:, m, :], ALU.mult, ALU.add), tp, t_x[m], t_gate)
                free[b] = [tx]
                tx1.append(tx)
                tq = square_in(xT[:, m, :], m == 0, tx, *(ssq_read[0] if m == 0 else []))
                i = sqn[0] % 2
                sqn[0] += 1
                d2 = ssq2[:, :] if m == 0 else sq[:, i, :]
                tq2 = A(lambda e, m=m, d2=d2: e.activation(d2, xT[:, m, :], ACT.Square, scale=vc(V_N1 + m)), tx,
                        *(f2 if m == 0 else sqfree[i]))
                if m:
                    tq2 = V(lambda e, d2=d2: e.tensor_tensor(ssq2[:, :], ssq2[:, :], d2, ALU.add), tq2, t_pr2)
                    sqfree[i] = [tq2]
                t_pr2 = tq2
            tc = V(lambda e: e.scalar_tensor_tensor(ssq2[:, :], ssq[:, :], EPS, ssq2[:, :], ALU.mult, ALU.add), tq, tq2)
            te12, tmc = rsqrt_rows(7, D, eps2_c, sq[:, 0, :], tc, 0.0, ssq2[:, :], *sqfree[0])
            t_r1, tm = rsqrt_rows(6, D, eps_c, rsb[:, :], tq, 0.0, None, *late["rsb"])
            f3 = fence()
            s5.close()

        k2 = ExitStack()
        fqo = sb(k2, "fqo", [128, 4, S])
        gzs = sb(k2, "gzs", [128, 4, S])
        gq = sb(k2, "gq", [128, 12, S])
        rowt = sb(k2, "rowt", [128, S])
        gcst = sb(k2, "gcst", [128, NGC])
        fk = sb(k2, "fk", [128, 4, S])
        fv = sb(k2, "fv", [128, 4, S])
        cols = sb(k2, "cols", [128, 3, 4, 4])
        hs = ExitStack()
        hhi = sb(hs, "hhi2", [128, NB, S], F32R)
        hlo = sb(hs, "hlo2", [128, NB, S], F32R)
        rmk = sb(hs, "rmk", [96, S])
        lg = sb(hs, "lg", [96, S])
        pr_ = sb(hs, "pr_", [96, 2])
        cbuf = sb(hs, "cbuf", [128, 2, S + 3])
        t_gc = GDMA("gcst", gcst[:, :], gc_d, *f3)
        t_rm = GDMA("rmk", rmk[:, :], rm_d, *f3)
        chs = group([("small", 0, 96, 3), ("fq", 0, 128, 0), ("fq", 1, 128, 1), ("fq", 2, 128, 2)])
        th, reads = norm_split(lambda b: sc8[:, 8 + b:9 + b], te12, [(t_g12)] * 8, hhi, hlo, f3, sq[:, 0, :])
        sqfree[0] = [reads[-1]]
        ssq_read[0] = [tm]
        h2 = (hhi, hlo, th)
        tps = project_group(chs, h2)

        s1c = cst[0:96, O_COL + 2:O_COL + 3]
        t1 = V(lambda e: e.tensor_tensor(pr_[:, 0:1], vc(V_DT, 0, 96), vc(V_FB, 0, 96), ALU.add), t_vec, *f3)
        ta = A(lambda e: e.activation(pr_[:, 1:2], vc(V_AL, 0, 96), ACT.Exp), *f3)
        ta = V(lambda e: e.tensor_scalar(pr_[:, 1:2], pr_[:, 1:2], -1.0, None, ALU.mult), ta)
        t1 = V(lambda e: e.tensor_scalar(rowt[0:96, :], PB[3][0:96, :], pr_[:, 0:1], s1c, ALU.add, ALU.mult), t1, tps[0], *f3)
        free[3] = [t1]
        t2 = V(lambda e: e.tensor_scalar(lg[:, :], rowt[0:96, :], 40.0, None, ALU.min), t1)
        t2 = A(lambda e: e.activation(lg[:, :], lg[:, :], ACT.Exp), t2)
        t2 = A(lambda e: e.activation(lg[:, :], lg[:, :], ACT.Ln, bias=one_c[0:96, :]), t2)

        tf_ = []
        for m in range(8):
            b = m if m < 3 else 4 + m % 4
            tp = tps[m + 1] if m < 3 else project(*(("fq", m) if m < 4 else ("fk", m - 4)), 128, b, h2)
            d = fqo[:, m, :] if m < 4 else fk[:, m - 4, :]
            te = A(lambda e, b=b, d=d, m=m: e.activation(d, PB[b][:, :], ACT.Copy, scale=0.125 if m < 4 else 1.0), tp, *f3)
            free[b] = [te]
            tf_.append(te)
            if m == 4:
                t2 = V(lambda e: e.tensor_tensor(lg[:, :], lg[:, :], rowt[0:96, :], ALU.max), t2)
                t2 = V(lambda e: e.tensor_scalar(lg[:, :], lg[:, :], pr_[:, 1:2], None, ALU.mult), t2, ta)
                t3 = V(lambda e: e.tensor_tensor_scan(rowt[0:96, :], rmk[:, :], lg[:, :], 0.0, ALU.mult, ALU.add), t2, t_rm)
                c3 = rowt[0:32, :].rearrange("p (c j) -> p c j", j=64)
                t4 = V(lambda e: e.tensor_tensor(rowt[96:128, :].rearrange("p (c j) -> p c j", j=64),
                                                 c3[:, :, 63:64].to_broadcast([32, 8, 64]), c3, ALU.subtract), t3)
                t_row = V(lambda e: e.tensor_copy(rowt[32:64, :], lg[32:64, :]), t3)
            if m > 3:
                for k in (2 * m - 8, 2 * m - 7):
                    tx1[k] = V(lambda e, k=k: e.scalar_tensor_tensor(
                        xT[:, k, :], xT[:, k, :], vc(V_N1 + k), rsb[:, :], ALU.mult, ALU.mult), t_r1, reads[k])
        tp = project_nat("fv", 4, 2, [0, 1, 2, 3], h2)
        for t_ in range(4):
            te = A(lambda e, t_=t_: e.activation(fv[:, t_, :], PB[t_][:, :], ACT.Copy), tp, *f3)
            free[t_] = [te]
        t_fv = te

        tz = G(lambda e: e.memset(cbuf[:, :, 0:3], 0.0), *f3)
        tgq, tgz = [None] * 12, [None] * 4
        cfree = [[tz], [tz]]

        def conv(m, b, tp):
            i = m % 2
            x = cbuf[:, i, :]
            te = A(lambda e: e.activation(x[:, 3:S + 3], PB[b][:, :], ACT.Copy), tp, *cfree[i], *f3)
            free[b] = [te]
            y = gq[:, m, :]
            t = V(lambda e: e.tensor_scalar(y, x[:, 3:S + 3], vc(V_CV + 4 * m + 3), None, ALU.mult), te, tz, *f3)
            for j in range(3):
                t = V(lambda e, j=j: e.scalar_tensor_tensor(y, x[:, j:S + j], vc(V_CV + 4 * m + j), y, ALU.mult, ALU.add), t)
            cfree[i] = [t]
            tgq[m] = t

        def filler_q():
            for m in range(12):
                b = 7
                tp = project("gqkv", m, 128, b, h2)
                conv(m, b, tp)
                yield

        fx = ExitStack()
        cbt2 = sb(fx, "cbt2", [128, 2, S])
        qz = sb(fx, "qz", [128, 2, S])
        tz0 = V(lambda e: e.memset(qz[:, :, :], 0.0), *f3)
        cbias_used = [list(f3), list(f3)]
        cbtok, tqz, texq = {}, {}, {}

        def make_q(h):
            r0, i = 64 * (h % 2), h % 2
            tqz[h] = V(lambda e: e.tensor_copy(qz[r0:r0 + 64, i, :], fqo[r0:r0 + 64, h // 2, :]), tz0, tf_[h // 2],
                       *([texq[h - 2]] if h > 1 else []))

        def make_cb(h):
            tk = T(lambda e: e.matmul(PB[6][:, :], ident[:, 64 + h:65 + h].to_broadcast([128, 128]), rowt[:, :],
                                      start=True, stop=True), t_row, t4, *free[6], inc=True)
            cbtok[h] = A(lambda e: e.activation(cbt2[:, h % 2, :], PB[6][:, :], ACT.Copy, scale=-1.0), tk, *cbias_used[h % 2])
            free[6] = [cbtok[h]]

        def cbias(what, h, tok):
            if what == "get":
                return cbt2[:, h % 2, :], cbtok[h]
            if what == "used":
                texq[h] = tok
                if h < 7:
                    make_cb(h + 1)
            if what == "done":
                cbias_used[h % 2] = [tok]
                if h < 7:
                    make_q(h + 1)

        tfo = []

        def comb2(pr, bank, tk):
            te = A(lambda e: e.activation(fqo[:, pr, :], PB[bank][:, :], ACT.Copy), tk, tqz[2 * pr], tqz[2 * pr + 1])
            tfo.append(te)
            return te

        make_q(0)
        make_cb(0)
        fq_ = filler_q()

        def pace():
            for n in range(17):
                if n % 2 or n in (0, 4, 8, 12):
                    next(fq_, None)
                yield
        drain(softmax_attention(
            "f", fx, f3, lambda h, qi: qz[:, h % 2, 128 * qi:128 * qi + 128], lambda h, n: fk[:, h // 2, 0:n],
            lambda h: (tqz[h], tf_[4 + h // 2]), fv, [t_fv], comb2, pace(), 1, cbias))
        drain(fq_)
        f4a = fence()
        fx.close()

        preload(SILU)
        for m in range(12):
            tgq[m] = A(lambda e, m=m: e.activation(gq[:, m, :], gq[:, m, :], ACT.Silu), tgq[m])
        preload(EXPLN)
        l2free = [[th[-1]], [th[-1]]]
        tsq = {}

        def l2_square(m):
            i = m % 2
            tsq[m] = A(lambda e: e.activation(sq[:, i, :], gq[:, m, :], ACT.Square), tgq[m], *sqfree[i])

        def l2_norm(m):
            i, b = m % 2, 4 + m % 4
            te, tm = rsqrt_rows(b, 1, eps_c, tmpf[:, i, :], tsq[m], dk_c if m < 4 else 0.0, sq[:, i, :], *l2free[i])
            sqfree[i] = [tm]
            if m < 6:
                l2_square(m + 2)
            tgq[m] = V(lambda e: e.tensor_tensor(gq[:, m, :], gq[:, m, :], tmpf[:, i, :], ALU.mult), te)
            l2free[i] = [tgq[m]]
        l2_square(0)
        l2_square(1)
        for m in range(4):
            tp = project("gz", m, 128, m, h2)
            tgz[m] = V(lambda e, m=m: e.tensor_copy(gzs[:, m, :], PB[m][:, :]), tp, *f3)
            free[m] = [tgz[m]]
            if m:
                for k in ((0, 1, 2), (3, 4, 5), (6, 7))[m - 1]:
                    l2_norm(k)
        f4 = fence()
        hs.close()

        ga_, gb_ = ExitStack(), ExitStack()
        NT, X, QKT = (sb(ga_, n, [128, 4, S]) for n in ("NT", "X", "QKT"))
        st2 = sb(ga_, "st2", [128, 2, S])
        vn2 = sb(ga_, "vn2", [128, 2, S])
        EE = sb(ga_, "EE", [128, 4, 8])
        rso = sb(ga_, "rso", [128, 4, 4])
        Y, KBG = (sb(gb_, n, [128, 4, S]) for n in ("Y", "KBG"))
        nat = st2[:, 1, :].rearrange("p (a b) -> p a b", a=4)
        KDEC, VBN = gq[:, 4:8, :], gq[:, 8:12, :]
        pp_, sg_ = tmpf, ssq
        U, W = X, NT

        def hh(x, h, t_):
            return x[:, h, 128 * t_:128 * t_ + 128]

        def bc4(i, h):
            return cols[:, i, :, h:h + 1].to_broadcast([128, 4, 128])

        def v3(x):
            return x.rearrange("p (a b) -> p a b", a=4)

        def c3_(o, src=None):
            src = cst if src is None else src
            return src[:, o:o + 128].rearrange("p (a b) -> p a b", a=1).to_broadcast([128, 4, 128])

        gring = [0]

        def gbank():
            gring[0] += 1
            return gring[0] % 8

        def four(b, lhs, rhs, *w, start=True, stop=True):
            for t_ in range(4):
                tk = T(lambda e, t_=t_: e.matmul(PB[b][:, 128 * t_:128 * t_ + 128], lhs(t_), rhs(t_), start=start, stop=stop,
                                                 skip_group_check=True), *w, *(free[b] if start else []), inc=True)
            return tk

        def turn4(b, src, *w):
            for t_ in range(4):
                tk = T(lambda e, t_=t_: e.transpose(PB[b][:, 128 * t_:128 * t_ + 128], src(t_), ident), *w, *free[b], inc=True)
            return tk

        tkb, tkd, tvn, tnt, tqk2, teg, tqg, tW, tU = ({} for _ in range(9))
        tX, tY, tP = {}, {}, {}

        def delta():
            b = gbank()
            tk = turn4(b, lambda t_: rowt[:, 128 * t_:128 * t_ + 128], t_row, t4)
            te = V(lambda e, b=b: e.tensor_copy(nat, v3(PB[b][:, :])), tk, *f4)
            free[b] = [te]
            t1 = V(lambda e: e.tensor_tensor(cols[:, 1, :, :], nat[:, :, 0:4], nat[:, :, 32:36], ALU.add), te)
            A(lambda e: e.activation(cols[:, 0, :, :], nat[:, :, 32:36], ACT.Exp), te)
            A(lambda e: e.activation(cols[:, 2, :, :], nat[:, :, 96:100], ACT.Exp), te)
            t_cols = A(lambda e: e.activation(cols[:, 1, :, :], cols[:, 1, :, :], ACT.Exp), t1)
            tzs_ = V(lambda e: e.memset(vn2[:, :, :], 0.0), *f4)
            late["vn"] = tzs_
            late["nat"] = t_cols
            dfree = {(i, j): list(f4) for i in range(2) for j in range(2)}
            egfree = [list(f4), list(f4)]
            tdec = {}

            def decays(h):
                b, egb = gbank(), (rsb, ssq)[h % 2]
                tk = T(lambda e: e.matmul(PB[b][:, :], ident[:, h:h + 1].to_broadcast([128, 128]), rowt[:, :],
                                          start=True, stop=False, skip_group_check=True), t_row, t4, *free[b], inc=True)
                teg[h] = A(lambda e: e.activation(egb[:, :], PB[b][:, :], ACT.Exp), tk, *egfree[h % 2])
                tee = V(lambda e: e.tensor_copy(EE[:, h, :].rearrange("p (a b) -> p a b", b=1),
                                                egb[:, :].rearrange("p (a b) -> p a b", b=64)[:, :, 63:64]),
                        teg[h], *f4)
                tdec[h] = [b, tee]

            def scores(h):
                b, tee = tdec[h]
                B, d, b2, egb = PB[b], (sq, tmpf)[h % 2][:, 0, :], gbank(), (rsb, ssq)[h % 2]
                for t_ in range(4):
                    c = slice(128 * t_, 128 * t_ + 128)
                    T(lambda e, c=c: e.matmul(B[:, c], rowt[:, c], cst[:, O_NIDENT + h:O_NIDENT + h + 1]
                                              .to_broadcast([128, 128]), start=False, stop=False,
                                              skip_group_check=True), teg[h])
                    tk = T(lambda e, c=c: e.matmul(B[:, c], identB, mgB, start=False, stop=False, skip_group_check=True),
                           inc=True)
                td = A(lambda e: e.activation(d, B[:, :], ACT.Exp), tk, *dfree[h % 2, 0])
                tk = four(b2, lambda t_: hh(gq, 4 + h, t_), lambda t_: hh(gq, h, t_), tgq[4 + h], tgq[h])
                tqk2[h] = V(lambda e: e.tensor_tensor(QKT[:, h, :], PB[b2][:, :], d, ALU.mult), tk, td, *f4)
                free[b2] = [tqk2[h]]
                dfree[h % 2, 0] = [tqk2[h]]
                tqg[h] = V(lambda e: e.tensor_tensor(gq[:, h, :], gq[:, h, :], egb[:, :], ALU.mult), teg[h], tk)
                egfree[h % 2] = [tqg[h], tee]
                tdec[h].append(td)

            def keys(h):
                b, _, td = tdec[h]
                B, d, b2 = PB[b], (sq, tmpf)[h % 2][:, 1, :], gbank()
                tk = T(lambda e: e.matmul(B[:, :], ident[:, 32 + h:33 + h].to_broadcast([128, 128]), rowt[:, :],
                                          start=False, stop=True, skip_group_check=True), td, inc=True)
                tdb = A(lambda e: e.activation(d, B[:, :], ACT.Exp), tk, *dfree[h % 2, 1])
                free[b] = [tdb]
                tk = four(b2, lambda t_: hh(gq, 4 + h, t_), lambda t_: hh(gq, 4 + h, t_), tgq[4 + h])
                tnt[h] = V(lambda e: e.tensor_tensor(NT[:, h, :], PB[b2][:, :], d, ALU.mult), tk, tdb, *f4)
                free[b2] = [tnt[h]]
                dfree[h % 2, 1] = [tnt[h]]
                ty = G(lambda e: e.tensor_tensor(v3(Y[:, h, :]), v3(NT[:, h, :]), c3_(G_LT, gcst), ALU.mult),
                       tnt[h], t_gc, *f4)
                tY[h] = G(lambda e: e.tensor_tensor(v3(Y[:, h, :]), c3_(O_IDENT), v3(Y[:, h, :]), ALU.subtract), ty)

            def turn_v(h):
                b = gbank()
                tk = turn4(b, lambda t_: hh(gq, 8 + h, t_), tgq[8 + h])
                tvn[h] = V(lambda e: e.tensor_tensor(v3(VBN[:, h, :]), v3(PB[b][:, :]), bc4(0, h), ALU.mult), tk, t_cols)
                free[b] = [tvn[h]]

            def turn_k(h):
                b = gbank()
                tk = turn4(b, lambda t_: hh(gq, 4 + h, t_))
                tkb[h] = V(lambda e: e.tensor_tensor(v3(KBG[:, h, :]), v3(PB[b][:, :]), bc4(1, h), ALU.mult),
                           tk, t_cols, *f4)
                tkd[h] = V(lambda e: e.tensor_tensor(v3(KDEC[:, h, :]), v3(PB[b][:, :]), bc4(2, h), ALU.mult),
                           tk, t_cols)
                free[b] = [tkd[h]]

            def turn_y(h):
                b = gbank()
                tk = turn4(b, lambda t_: hh(Y, h, t_), tY[h])
                tX[h] = A(lambda e: e.activation(X[:, h, :], PB[b][:, :], ACT.Copy), tk, *f4)
                free[b] = [tX[h]]

            for h in (0, 2):
                decays(h)
                decays(h + 1)
                scores(h)
                turn_v(h)
                scores(h + 1)
                keys(h)
                turn_v(h + 1)
                keys(h + 1)
                turn_k(h)
                turn_k(h + 1)
                yield
                if h == 2:
                    for k in range(4):
                        turn_y(k)

            pfree = [[tqk2[3], tnt[3]], [tqk2[3], tnt[3]]]

            def level_p(lv, h):
                b, i = gbank(), h % 2
                tk = four(b, lambda t_: hh(NT, h, t_), lambda t_: hh(X, h, t_), tnt[h], tX[h])
                tP[h] = (V(lambda e: e.tensor_tensor(v3(pp_[:, i, :]), v3(PB[b][:, :]), c3_(G_LM + 128 * lv - 128, gcst),
                                                     ALU.mult), tk, t_gc, *pfree[i]), tk)
                free[b] = [tP[h][0]]

            def level_u(lv, h):
                i = h % 2
                tpp, tkx = tP[h]
                if lv < 5:
                    b = gbank()
                    tk = four(b, lambda t_: hh(Y, h, t_), lambda t_: hh(pp_, i, t_), tpp, tY[h])
                    tX[h] = V(lambda e, b=b: e.tensor_tensor(X[:, h, :], X[:, h, :], PB[b][:, :], ALU.subtract), tk, tkx, tX[h])
                    free[b] = [tX[h]]
                b = gbank()
                tk = four(b, lambda t_: hh(pp_, i, t_), lambda t_: hh(Y, h, t_), tpp, tY[h])
                pfree[i] = [tk]
                tY[h] = V(lambda e: e.tensor_tensor(Y[:, h, :], Y[:, h, :], PB[b][:, :], ALU.subtract), tk, tY[h])
                free[b] = [tY[h]]

            preload(SILU)
            for m in range(4):
                tgz[m] = A(lambda e, m=m: e.activation(gzs[:, m, :], gzs[:, m, :], ACT.Silu), tgz[m])
            preload(EXPLN)
            units = [(lv, h) for lv in range(1, 6) for h in range(4)]
            level_p(*units[0])
            for n, (lv, h) in enumerate(units):
                if n + 1 < len(units):
                    level_p(*units[n + 1])
                level_u(lv, h)
                yield

            for h in range(4):
                b = gbank()
                tk = four(b, lambda t_, h=h: hh(KBG, h, t_), lambda t_, h=h: hh(Y, h, t_), tkb[h], tY[h])
                tW[h] = A(lambda e, h=h, b=b: e.activation(W[:, h, :], PB[b][:, :], ACT.Copy), tk, tP[h][1])
                free[b] = [tW[h]]
                if h % 2:
                    yield
            for t_ in range(4):
                b = gbank()
                for h in range(4):
                    tk = T(lambda e, t_=t_, h=h, b=b: e.matmul(PB[b][:, 128 * h:128 * h + 128], hh(Y, h, t_), hh(VBN, h, t_),
                                                               start=True, stop=True, skip_group_check=True),
                           tvn[h], tY[h], *free[b], inc=True)
                tU[t_] = A(lambda e, t_=t_, b=b: e.activation(U[:, t_, :], PB[b][:, :], ACT.Copy), tk,
                           *(x[1] for x in tP.values()))
                free[b] = [tU[t_]]
                if t_ % 2:
                    yield

        drain(delta())
        f5 = fence()
        gb_.close()

        hs = ExitStack()
        hhi = sb(hs, "hhi3", [128, NB, S], F32R)
        hlo = sb(hs, "hlo3", [128, NB, S], F32R)
        tm_ = [None] * 8
        tS = V(lambda e: e.memset(st2[:, 0, :], 0.0), *f5)
        tfree_S = [[], list(f5)]
        tvf = [[], []]
        t_sg = []
        tgo, tg_nat = {}, {}
        tgate = []

        def out_norm(t_):
            b = 4 + t_ % 2
            for h in range(4):
                ts = A(lambda e, h=h: e.activation(sq[:, t_ % 2, 128 * h:128 * h + 128], PB[b][:, 128 * h:128 * h + 128],
                                                   ACT.Square, accum_out=rso[:, t_, h:h + 1]), tgo[t_], *sqfree[t_ % 2], *f5)
            sqfree[t_ % 2] = [ts]
            t1 = A(lambda e: e.activation(rso[:, t_, :], rso[:, t_, :], ACT.Ln, bias=eps_c, scale=1.0 / 128), ts)
            t1 = A(lambda e: e.activation(rso[:, t_, :], rso[:, t_, :], ACT.Exp, scale=-0.5), t1)
            tg_nat[t_] = V(lambda e: e.tensor_tensor(
                v3(VBN[:, t_, :]), v3(PB[b][:, :]), rso[:, t_, :].rearrange("p (a b) -> p a b", b=1)
                .to_broadcast([128, 4, 128]), ALU.mult), t1)
            free[b] = [tg_nat[t_]]

        def out_turn(t_):
            b = 6 + t_ % 2
            tk = turn4(b, lambda h: VBN[:, t_, 128 * h:128 * h + 128], tg_nat[t_])
            c = slice(128 * t_, 128 * t_ + 128)
            tgate.append(V(lambda e: e.scalar_tensor_tensor(gzs[:, :, c], v3(PB[b][:, :]), vc(V_GN), gzs[:, :, c],
                                                            ALU.mult, ALU.mult), tk))
            free[b] = [tgate[-1]]

        for m in range(4):
            tm_[4 + m] = split(fqo[:, m, :], hhi[:, 4 + m, :], hlo[:, 4 + m, :], tfo[m], *f5)
        for c in range(8):
            t_, p0, cur, nx = c // 2, 64 * (c % 2), c % 2, (c + 1) % 2
            cs = slice(64 * c, 64 * c + 64)
            wb_, sb_, ob = c % 2, 2 + c % 2, 4 + t_ % 2
            for h in range(4):
                tk = T(lambda e, h=h, p0=p0, cs=cs, cur=cur, wb_=wb_: e.matmul(
                    PB[wb_][p0:p0 + 64, 128 * h:128 * h + 128], W[:, h, cs], st2[:, cur, 128 * h:128 * h + 128],
                    start=True, stop=True, skip_group_check=True), tW[h], tS, *free[wb_], inc=True)
            tv_ = V(lambda e, t_=t_, p0=p0, wb_=wb_, c=c: e.tensor_tensor(
                vn2[p0:p0 + 64, c % 2, :], U[p0:p0 + 64, t_, :], PB[wb_][p0:p0 + 64, :], ALU.subtract),
                tk, tU[t_], *tvf[c % 2], late["vn"])
            free[wb_] = [tv_]
            for h in range(4):
                tko = T(lambda e, h=h, cs=cs, cur=cur, ob=ob, p0=p0: e.matmul(
                    PB[ob][p0:p0 + 64, 128 * h:128 * h + 128], gq[:, h, cs], st2[:, cur, 128 * h:128 * h + 128],
                    start=h == 0, stop=False, skip_group_check=True), tqg[h], tS, *free[ob], inc=True)
            if c < 7:
                tsg = G(lambda e, c=c, cur=cur: e.tensor_tensor(v3(sg_[:, :]), v3(st2[:, cur, :]),
                                                               EE[:, :, c:c + 1].to_broadcast([128, 4, 128]),
                                                               ALU.mult), tS, *t_sg, *f5)
                for h in range(4):
                    tk = T(lambda e, h=h, t_=t_, sb_=sb_, c=c: e.matmul(
                        PB[sb_][:, 128 * h:128 * h + 128], KDEC[:, h, 128 * t_:128 * t_ + 128],
                        vn2[:, c % 2, 128 * h:128 * h + 128], start=True, stop=True, skip_group_check=True),
                        tv_, tkd[h], *free[sb_], inc=True)
                tS = V(lambda e, nx=nx, sb_=sb_: e.tensor_tensor(st2[:, nx, :], sg_[:, :], PB[sb_][:, :], ALU.add),
                       tk, tsg, *tfree_S[nx])
                free[sb_] = [tS]
                t_sg = [tS]
            for h in range(4):
                tk = T(lambda e, h=h, p0=p0, t_=t_, ob=ob, c=c: e.matmul(
                    PB[ob][p0:p0 + 64, 128 * h:128 * h + 128], QKT[:, h, 128 * t_ + p0:128 * t_ + p0 + 64],
                    vn2[:, c % 2, 128 * h:128 * h + 128], start=False, stop=True, skip_group_check=True),
                    tv_, tqk2[h], inc=True)
            tvf[c % 2] = [tk]
            tfree_S[cur] = [tk]
            if c % 2:
                tgo[t_] = tk
                out_norm(t_)
                if t_:
                    out_turn(t_ - 1)
        chs = group([("wo2", i, 128, i) for i in range(4)])
        free_o = list(tgate)
        out_turn(3)
        for m in range(4):
            tm_[m] = split(gzs[:, m, :], hhi[:, m, :], hlo[:, m, :], tgate[-1], *f5)

        def residual(bank, m, tp, txs):
            tx = V(lambda e: e.tensor_tensor(xT[:, m, :], xT[:, m, :], PB[bank][:, :], ALU.add), tp, txs[m])
            free[bank] = [tx]
            return tx, square_in(xT[:, m, :], m == 0, tx, *(ssq_read[0] if m == 0 else []))

        ssq_read[0] = [tS]
        tps = project_group(chs, (hhi, hlo, tm_), (4, 5, 6, 7, 0, 1, 2, 3))
        tx2 = []
        for m in range(4):
            tx, tq = residual(m, m, tps[m], tx1)
            tx2.append(tx)
        for m in range(4, 8):
            b = m
            tp = project("wo2", m, 128, b, (hhi, hlo, tm_))
            tx, tq = residual(b, m, tp, tx1)
            tx2.append(tx)
        f6 = fence()
        hs.close()
        ga_.close()
        k2.close()

        ff = ExitStack()
        ahi = sb(ff, "ahi", [128, FFB, S], F32R)
        alo = sb(ff, "alo", [128, FFB, S], F32R)
        hs = ExitStack()
        hhi = sb(hs, "hhi4", [128, NB, S], F32R)
        hlo = sb(hs, "hlo4", [128, NB, S], F32R)
        chs = group([("gt", 0, 128, 0), ("up", 0, 128, 1), ("gt", 1, 128, 2), ("up", 1, 128, 3)])
        te, tm = rsqrt_rows(7, D, eps_c, rsb[:, :], tq, 0.0, None, tx1[-1], *tqg.values())
        ssq_read[0] = [tm]
        th, reads = norm_split(lambda b: vc(V_FN + b), te, tx2, hhi, hlo, f6)
        h3 = (hhi, hlo, th)
        preload(SILU)
        tps = project_group(chs, h3)
        sfree = [[th[-1]], [th[-1]]]
        tact = []
        for j in range(FFB):
            i = j % 2
            b0, b1 = 2 * (j % 4), 2 * (j % 4) + 1
            tp = tps[2 * j] if j < 2 else project("gt", j, 128, b0, h3)
            s_ = tmpf[:, i, :]
            ts = A(lambda e, s_=s_, b0=b0: e.activation(s_, PB[b0][:, :], ACT.Silu), tp, *sfree[i])
            free[b0] = [ts]
            tp = tps[2 * j + 1] if j < 2 else project("up", j, 128, b1, h3)
            t1 = V(lambda e, s_=s_, b1=b1: e.tensor_tensor(s_, s_, PB[b1][:, :], ALU.mult), ts, tp)
            free[b1] = [t1]
            tl = split(s_, ahi[:, j, :], alo[:, j, :], t1, *f6)
            sfree[i] = [tl]
            tact.append(tl)
        f7 = fence()
        hs.close()
        pl = ExitStack()
        hhi = sb(pl, "hhi5", [128, NB, S], F32R)
        hlo = sb(pl, "hlo5", [128, NB, S], F32R)
        plr = sb(pl, "plr", [128, 4, S])
        tPL = [GDMA(f"pl{m}", plr[:, m, :], ple[128 * m:128 * m + 128, :], t_ple, *f7) for m in range(4)]
        tx3 = []
        for m in range(8):
            b = 4 + m % 2
            for q in range(3):
                tp = project("dn", 3 * m + q, 128, b, (ahi, alo, tact), kbs=range(8 * q, min(8 * q + 8, FFB)),
                             start=q == 0, stop=q == 2)
            if m == 0:
                preload(EXPLN)
            tx, tq = residual(b, m, tp, tx2)
            tx3.append(tx)

        chs = group([("pg", i, 128, i) for i in range(4)])
        te, tm = rsqrt_rows(7, D, eps_c, rsb[:, :], tq, 0.0, None, reads[-1])
        ssq_read[0] = [tm]
        th, reads = norm_split(lambda b: vc(V_PN + b), te, tx3, hhi, hlo, f7)
        preload(SILU)
        tps = project_group(chs, (hhi, hlo, th))
        tx4 = []
        sfree = [[th[-1]], [th[-1]]]
        for m in range(8):
            b, i = m, m % 2
            tp = tps[m] if m < 4 else project("pg", m, 128, b, (hhi, hlo, th))
            s_ = tmpf[:, i, :]
            t1 = A(lambda e, s_=s_, b=b: e.activation(s_, PB[b][:, :], ACT.Tanh, scale=0.5), tp, *sfree[i])
            free[b] = [t1]
            t1 = V(lambda e, s_=s_, m=m: e.scalar_tensor_tensor(s_, s_, 1.0, plr[:, m % 4, :], ALU.add, ALU.mult), t1, tPL[m])
            if m < 4:
                tPL.append(DMA(f"pl{m + 4}", plr[:, m, :], ple[128 * m + 512:128 * m + 640, :], t1))
            tx = V(lambda e, s_=s_, m=m: e.tensor_tensor(xT[:, m, :], xT[:, m, :], s_, ALU.add), t1, tx3[m])
            sfree[i] = [tx]
            tx4.append(tx)
            tq = square_in(xT[:, m, :], m == 0, tx, *(ssq_read[0] if m == 0 else []))
        for m in range(2):
            tx4[m] = A(lambda e, m=m: e.activation(xT[:, m, :], xT[:, m, :], ACT.Copy, scale=vc(V_LN + m)), tx4[m])
        preload(EXPLN)
        te, tm = rsqrt_rows(7, D, eps_c, rsb[:, :], tq, 0.0, None, reads[-1])
        t_out = []
        for m in (0, 2, 3, 4, 1, 5, 6, 7):
            if m < 2:
                t1 = G(lambda e, m=m: e.tensor_tensor(xT[:, m, :], xT[:, m, :], rsb[:, :], ALU.mult), te, tx4[m])
                t_out.append(DMA(f"o{m}", out_d[m * 128:m * 128 + 128, :], xT[:, m, :], t1))
                continue
            t1 = V(lambda e, m=m: e.scalar_tensor_tensor(xT[:, m, :], xT[:, m, :], vc(V_LN + m), rsb[:, :],
                                                         ALU.mult, ALU.mult), te, tx4[m])
            t_out.append(DMA(f"o{m}", out_d[m * 128:m * 128 + 128, :], xT[:, m, :], t1))
        assert st.next == len(PLAN)
        pl.close()
        ff.close()

        emit(t_out)

def constants():
    i = np.arange(128)
    ii, jj = i[:, None], i[None, :]
    eye = np.eye(128, dtype=np.float32)
    cst = np.zeros((128, NCST), np.float32)
    cst[:, O_IDENT:O_IDENT + 128] = eye
    cst[:, O_NIDENT:O_NIDENT + 128] = -eye
    cst[:, O_ONES:O_ONES + 128] = 1
    cst[:, O_NONES:O_NONES + 128] = -1
    cst[:, O_TRI:O_TRI + 128] = np.where(ii >= jj, -1, 0)
    inv = np.float32(10000.0) ** (-np.arange(0, 32, 2, dtype=np.float32) / np.float32(32))
    cst[:, O_COL] = inv[i % 16]
    cst[:, O_COL + 1] = np.where(i % 32 < 16, -1, 1)
    cst[:, O_COL + 2] = np.where(i < 32, 1, -1)
    rc = np.zeros((128, NRC), np.float32)
    rc[:, R_MC:R_MC + 128] = np.where(jj <= ii, 0, NEG)
    rc[:, R_MS:R_MS + 128] = np.where(ii < jj, 0, NEG)
    rc[:, R_MG:R_MG + 128] = np.where((ii // 64 == jj // 64) & (jj >= ii), 0, NEG)
    gc = np.zeros((128, NGC), np.float32)
    for lv in range(1, 6):
        s = 1 << lv
        lower = (ii // (2 * s) == jj // (2 * s)) & (ii % (2 * s) >= s) & (jj % (2 * s) < s)
        gc[:, G_LM + 128 * (lv - 1):G_LM + 128 * lv] = lower
    gc[:, G_LT:G_LT + 128] = (ii // 2 == jj // 2) & (jj % 2 == 1) & (ii % 2 == 0)
    rm = np.ones((96, 512), np.float32)
    rm[0:64, ::64] = 0
    return cst, rc, gc, rm


def blocks_of(w, cols, k0=0, kb=None):
    kb = w.shape[0] // 128 - k0 if kb is None else kb
    part = w[128 * k0:128 * (k0 + kb), cols]
    return np.ascontiguousarray(part.reshape(kb, 128, -1).transpose(1, 0, 2)).reshape(-1)


def weights(a):
    w_in, w_in2 = a["w_in"][0], a["w_in_2"][0]
    at = np.cumsum([0, 512, 512, 512, 512, 384, 256, 32, 512, 1024, 1024])
    base = dict(zip(("sbq", "sbk", "sbv", "sz", "cq", "ckv", "kr", "mz", "ga", "gb"), at))
    at2 = np.cumsum([0, 1536, 512, 4, 4, 512, 512, 512, 8])
    base2 = dict(zip(("gqkv", "gz", "g_a", "g_b", "fq", "fk", "fv", "ff"), at2))
    kr = np.zeros((1024, 96), np.float32)
    kr[:, 64:96] = w_in[:, base["kr"]:base["kr"] + 32]
    small = np.zeros((1024, 96), np.float32)
    small[:, 0:4] = w_in2[:, base2["g_a"]:base2["g_a"] + 4]
    small[:, 32:36] = w_in2[:, base2["g_b"]:base2["g_b"] + 4]
    small[:, 64:72] = w_in2[:, base2["ff"]:base2["ff"] + 8]
    ukv = a["w_ukv"][0].reshape(256, 8, 128)
    uk = np.ascontiguousarray(ukv[:, :, 0:64]).reshape(256, 512)
    uv = np.ascontiguousarray(ukv[:, :, 64:128]).reshape(256, 512)
    ada = np.ascontiguousarray(a["w_ada"][0].T)
    every = slice(None)
    out = []
    for name, i, kb, n in chunks():
        c = slice(128 * i, 128 * i + 128)
        if name == "ada":
            out.append(ada[c, :].reshape(-1))
        elif name == "kr":
            out.append(blocks_of(kr, every))
        elif name == "small":
            out.append(blocks_of(small, every))
        elif name in ("sbv", "fv"):
            w, b = (w_in, base["sbv"]) if name == "sbv" else (w_in2, base2["fv"])
            out.append(blocks_of(w, slice(b, b + 512), 2 * i, 2))
        elif name in base:
            out.append(blocks_of(w_in, slice(base[name] + 128 * i, base[name] + 128 * i + 128)))
        elif name in base2:
            out.append(blocks_of(w_in2, slice(base2[name] + 128 * i, base2[name] + 128 * i + 128)))
        elif name == "uq":
            out.append(blocks_of(a["w_uq"][0], slice(288 * i, 288 * i + n)))
        elif name == "uk":
            out.append(blocks_of(uk, every))
        elif name == "uv":
            out.append(blocks_of(uv, every))
        elif name in ("wa", "wb"):
            out.append(blocks_of(a["w_branch_" + name[1]][0], slice(256 * i, 256 * i + 256)))
        elif name == "wo":
            out.append(blocks_of(a["w_out"][0], c))
        elif name == "wo2":
            out.append(blocks_of(a["w_out_2"][0], c))
        elif name == "gt":
            out.append(blocks_of(a["w_gate_up_2"][0], c))
        elif name == "up":
            out.append(blocks_of(a["w_gate_up_2"][0], slice(128 * (FFB + i), 128 * (FFB + i) + 128)))
        elif name == "dn":
            m, q = i // 3, i % 3
            out.append(blocks_of(a["w_down_2"][0], slice(128 * m, 128 * m + 128), 8 * q, kb))
        elif name == "pp":
            out.append(blocks_of(a["w_ple_proj_2"][0], slice(512 * i, 512 * i + 512)))
        elif name == "pg":
            out.append(blocks_of(a["w_ple_gate_2"][0], c))
        assert out[-1].size == 128 * kb * n, (name, i)
    return np.concatenate(out)


def vectors(a):
    v = np.zeros((128, NVEC), np.float32)

    def put(at, x):
        n = x.size // 128
        v[:, at:at + n] = x.reshape(n, 128).T

    put(V_NG, a["norm_gain"])
    put(V_BA, a["b_ada"])
    put(V_AN, a["attn_norm_w_2"])
    put(V_FN, a["ffn_norm_w_2"])
    put(V_PN, a["ple_norm_w_2"])
    put(V_LN, a["final_norm_w_2"])
    put(V_QN, a["q_norm_gain"])
    put(V_KN, a["kv_norm_gain"])
    put(V_GN, a["gdn_norm_w_2"])
    put(V_N1, a["final_norm_gain"])
    v[:, V_CV:V_CV + 48] = a["conv_w_2"][0].reshape(4, 12, 128).transpose(2, 1, 0).reshape(128, 48)
    v[0:4, V_DT] = a["dt_bias_2"][0]
    v[64:72, V_FB] = a["fox_f_bias_2"][0]
    v[0:4, V_AL] = a["a_log_2"][0]
    return v


def layout(inputs):
    a = {k: np.asarray(v) for k, v in inputs.items()}
    cst, rc, gc, rm = constants()
    return {
        "w_all": weights(a), "cst_d": cst, "rc_d": rc, "gc_d": gc, "rm_d": rm, "vec_d": vectors(a),
        "x_d": np.ascontiguousarray(a["x"][0].T), "c_d": np.ascontiguousarray(a["c"]),
        "pos_d": np.ascontiguousarray(a["positions"]),
        "ada_d": np.ascontiguousarray(a["w_ada"][0].T[0:2048]), "p_d": np.ascontiguousarray(a["p_2"][0, 0].T),
    }


def kernel(**inputs):
    import concourse.bacc as bacc
    from concourse.bass_utils import run_bass_kernel_spmd

    nc = bacc.Bacc("TRN2", target_bir_lowering=False, num_devices=1)
    arrays = layout(inputs)
    args = [nc.dram_tensor(n, x.shape, mybir.dt.from_np(x.dtype), kind="ExternalInput").ap() for n, x in arrays.items()]
    out = nc.dram_tensor("out_d", (D, S), F32, kind="ExternalOutput").ap()
    build(nc, *args, out)
    r = run_bass_kernel_spmd(nc, [arrays], core_ids=[0])
    return np.ascontiguousarray(r.results[0]["out_d"].T).reshape(1, S, D)
```

```python
import math
from contextlib import ExitStack

import concourse.bass as bass
import numpy as np
from concourse import mybir

F32 = mybir.dt.float32
F32R = mybir.dt.float32r
I32 = mybir.dt.int32
BF16 = mybir.dt.bfloat16
ALU = mybir.AluOpType
ACT = mybir.ActivationFunctionType
AX = mybir.AxisListType

S = 512
D = 1024
NB = D // 128
EPS = 1e-6
NEG = -float(2 ** 100)
FFB = 22
EXPLN = "natural_log_exp_and_others"
SILU = "silu_and_others"

O_IDENT, O_NIDENT, O_ONES, O_NONES, O_TRI, O_COL = 0, 128, 256, 384, 512, 640
NCST = 648
R_MC, R_MS, R_MG = (128 * i for i in range(3))
NRC = 384
G_LM, G_LT = 0, 640
NGC = 768

V_NG, V_BA, V_AN, V_FN, V_PN, V_LN = 0, 8, 32, 40, 48, 56
V_QN, V_KN, V_GN, V_CV = 64, 67, 69, 70
V_DT, V_FB, V_AL, V_N1 = 118, 119, 120, 121
NVEC = 129


def chunks():
    out = [("pp", 0, 2, 512), ("pp", 1, 2, 512)]
    out += [("sbq", i, 8, 128) for i in range(4)] + [("sbk", i, 8, 128) for i in range(4)]
    out += [("sbv", i, 2, 512) for i in range(4)]
    for i in range(8):
        out += [(("cq", i, 8, 128) if i < 3 else ("ckv", i - 3, 8, 128)) if i < 5 else
                ("kr", 0, 8, 96) if i == 5 else ("sz", i - 6, 8, 128), ("ada", 16 + i, 8, 128)]
    out += [("sz", i, 8, 128) for i in (2, 3)] + [("mz", i, 8, 128) for i in range(4)]
    out += [("ga", i, 8, 128) for i in range(8)]
    out += [("uq", 0, 3, 288), ("uq", 1, 3, 288), ("uq", 2, 3, 192), ("uk", 0, 2, 512), ("uv", 0, 2, 512)]
    out += [("gb", i, 8, 128) for i in range(8)]
    out += [("wa", i, 4, 256) for i in range(4)]
    out += [("wb", i, 4, 256) for i in range(4)]
    out += [("wo", i, 8, 128) for i in range(8)]
    out += [("small", 0, 8, 96)] + [("fq", i, 8, 128) for i in range(4)] + [("fk", i, 8, 128) for i in range(4)]
    out += [("fv", i, 2, 512) for i in range(4)]
    out += [("gqkv", i, 8, 128) for i in range(12)] + [("gz", i, 8, 128) for i in range(4)]
    out += [("wo2", i, 8, 128) for i in range(8)]
    for j in range(FFB):
        out += [("gt", j, 8, 128), ("up", j, 8, 128)]
    for m in range(NB):
        out += [("dn", 3 * m, 8, 128), ("dn", 3 * m + 1, 8, 128), ("dn", 3 * m + 2, 6, 128)]
    out += [("pg", i, 8, 128) for i in range(8)]
    return out


def build(nc, w_all, cst_d, rc_d, gc_d, rm_d, vec_d, x_d, c_d, pos_d, ada_d, p_d, out_d):
    PLAN = chunks()
    OFF, at = [], 0
    for _, _, kb, n in PLAN:
        OFF.append(at)
        at += 128 * kb * n

    top = ExitStack()
    with top:
        def sem(n):
            return top.enter_context(nc.semaphore(n))

        queue = {e: [] for e in "SGATV"}
        done = {e: sem("s_" + n) for e, n in zip("GATV", ("pool", "act", "pe", "dve"))}
        count = {e: 0 for e in "GATV"}

        def op(e, fn, *waits, inc=True):
            queue[e].append((waits, fn, inc))
            if inc:
                count[e] += 1
                return (done[e], count[e])
            return None

        def V(fn, *w): return op("V", fn, *w)
        def A(fn, *w): return op("A", fn, *w)
        def G(fn, *w): return op("G", fn, *w)
        def T(fn, *w, inc=False): return op("T", fn, *w, inc=inc)

        dsem = {}

        def DMA(name, dst, src, *w):
            if name not in dsem:
                dsem[name] = [sem("d_" + name), 0]
            d = dsem[name]
            d[1] += 16
            s = d[0]
            queue["S"].append((w, lambda e: e.dma_start(dst, src).then_inc(s, 16), False))
            return (s, d[1])

        def emit(t_out):
            def run(name):
                def body(eng):
                    seen = {}
                    for waits, fn, inc in queue[name]:
                        for s, v in waits:
                            if seen.get(id(s), 0) < v:
                                seen[id(s)] = v
                                eng.wait_ge(s, v)
                        ins = fn(eng)
                        if inc:
                            ins.then_inc(done[name], 1)
                    if name == "S":
                        for s, v in t_out:
                            eng.wait_ge(s, v)
                return body

            with nc.Block() as block:
                block.sync(run("S"))
                block.gpsimd(run("G"))
                block.scalar(run("A"))
                block.vector(run("V"))
                block.tensor(run("T"))

        def GDMA(name, dst, src, *w):
            s = sem("d_" + name)
            queue["G"].append((w, lambda e: e.dma_start(dst, src).then_inc(s, 16), False))
            return (s, 16)

        def sb(stack, name, shape, dt=F32):
            return stack.enter_context(nc.sbuf_tensor(name, shape, dt))

        PB = [top.enter_context(nc.psum_tensor(f"pb{i}", [128, 512], F32)) for i in range(8)]
        free = [[] for _ in range(8)]

        cst = sb(top, "cst", [128, NCST])
        vec = sb(top, "vec", [128, NVEC])
        xT = sb(top, "xT", [128, NB, S])
        NRAW, NHL, LOOK = 3, 4, 2
        raw = sb(top, "raw", [128, NRAW, 1024])
        whi = sb(top, "whi", [128, NHL, 1024], F32R)
        wlo = sb(top, "wlo", [128, NHL, 1024], F32R)
        rcst = sb(top, "rcst", [128, 3, 128], F32R)
        bcst = sb(top, "bcst", [128, 4, 128], BF16)
        sq = sb(top, "sq", [128, 2, S])
        ssq = sb(top, "ssq", [128, S])
        rsb = sb(top, "rsb", [128, S])
        tmpf = sb(top, "tmpf", [128, 2, S])
        mod = sb(top, "mod", [128, 24])
        sc8 = sb(top, "sc8", [128, 16])
        epsc = sb(top, "epsc", [128, 5])

        t_cst = DMA("cst", cst[:, :], cst_d)
        t_vec = DMA("vec", vec[:, :], vec_d)
        ident = cst[:, O_IDENT:O_IDENT + 128]
        ones = cst[:, O_ONES:O_ONES + 128]

        def cb(o):
            return cst[:, o:o + 128]

        def fr(ap):
            return ap.bitcast(F32)

        def vc(i, p0=0, p1=128):
            return vec[p0:p1, i:i + 1]

        with ExitStack() as tmp:
            rcf = sb(tmp, "rcf", [128, NRC])
            t_rcf = DMA("rcf", rcf[:, :], rc_d)
            V(lambda e: e.tensor_copy(bcst[:, 0, :], cb(O_IDENT)), t_cst)
            for i in range(3):
                t_rc = V(lambda e, i=i: e.tensor_copy(bcst[:, i + 1, :], rcf[:, 128 * i:128 * i + 128]), t_rcf)
            V(lambda e: e.tensor_copy(rcst[:, 0, :], cb(O_NONES)), t_cst)
            V(lambda e: e.tensor_copy(rcst[:, 2, :], cb(O_IDENT)), t_cst)
            t_rc = V(lambda e: e.tensor_copy(rcst[:, 1, :], cb(O_TRI)), t_cst)
        identB, mcB, msB, mgB = (bcst[:, i, :] for i in range(4))
        nonesR, triR, identR = (rcst[:, i, :] for i in range(3))

        class Stream:
            def __init__(self):
                self.dma, self.cv, self.next = 0, 0, 0
                self.tok, self.conv = {}, {}
                self.rawfree = [[] for _ in range(NRAW)]
                self.hlfree = [[] for _ in range(NHL)]
                self.hl = 0

            def load(self, i):
                if i != self.dma or i >= len(PLAN):
                    return
                self.dma += 1
                _, _, kb, n = PLAN[i]
                r = i % NRAW
                src = w_all[OFF[i]:OFF[i] + 128 * kb * n].rearrange("(p n) -> p n", p=128)
                self.tok[i] = DMA(f"raw{r}", raw[:, r, 0:kb * n], src, *self.rawfree[r])

            def convert(self, upto):
                while self.cv < min(upto, len(PLAN)):
                    i = self.cv
                    name, _, kb, n = PLAN[i]
                    r = i % NRAW
                    self.cv += 1
                    if name == "ada":
                        a_ = ada_gate(raw[:, r, :], PLAN[i][1], self.tok[i])
                        self.rawfree[r] = [a_]
                        self.load(i + NRAW)
                        continue
                    h, w = self.hl % NHL, kb * n
                    self.hl += 1
                    src = raw[:, r, 0:w]
                    hi, lo = whi[:, h, 0:w], wlo[:, h, 0:w]
                    th = A(lambda e, a=hi, b=src: e.activation(a, b, ACT.Copy), self.tok[i], *self.hlfree[h])
                    tl = V(lambda e, a=lo, b=src, c=fr(hi): e.tensor_tensor(a, b, c, ALU.subtract),
                           th, *self.hlfree[h])
                    self.rawfree[r] = [th, tl]
                    self.load(i + NRAW)
                    self.conv[i] = (h, tl, hi.rearrange("p (k n) -> p k n", k=kb),
                                    lo.rearrange("p (k n) -> p k n", k=kb))

            def get(self, name, idx, look=LOOK):
                while PLAN[self.next][0] == "ada":
                    self.next += 1
                i = self.next
                assert PLAN[i][:2] == (name, idx), (PLAN[i], name, idx)
                self.next += 1
                self.convert(i + 1 + look)
                h, tl, hi, lo = self.conv.pop(i)
                return hi, lo, tl, h

        st = Stream()
        gate_tok = []

        def ada_gate(w, i, tw):
            t = V(lambda e: e.tensor_tensor_reduce(out=gjunk[0][:, :], in0=w, in1=gcb[0][:, :], scale=1.0, scalar=0.0,
                                                   op0=ALU.mult, op1=ALU.add, accum_out=mod[:, i:i + 1]),
                  tw, *gcb[1], *gate_tok[-1:])
            gate_tok.append(t)
            return t
        gjunk, gcb = [None], [None, []]

        def mm3(out, lh, ll, rh, rl, start, stop, *w):
            T(lambda e: e.matmul(out, lh, rl, start=start, stop=False, skip_group_check=True), *w)
            T(lambda e: e.matmul(out, ll, rh, start=False, stop=False, skip_group_check=True))
            return T(lambda e: e.matmul(out, lh, rh, start=False, stop=stop, skip_group_check=True), inc=True)

        def project(name, idx, m, bank, act, n0=0, kbs=None, start=True, stop=True, chunk=None, order=None, ktok=None):
            hi, lo, tw, slot = chunk or st.get(name, idx)
            ah, al, at_ = act
            kbs = list(kbs or range(hi.shape[1]))
            qs_ = list(order or range(len(kbs)))
            for q in qs_:
                k, first = kbs[q], q == qs_[0]
                w = [at_[k]]
                if first:
                    w += [tw] + (free[bank] if start else [])
                t = mm3(PB[bank][0:m, :], hi[:, q, n0:n0 + m], lo[:, q, n0:n0 + m], ah[:, k, :], al[:, k, :],
                        start and first, stop and q == qs_[-1], *w)
                if ktok is not None:
                    ktok.append(t)
            st.hlfree[slot] = [t]
            return t

        def group(items):
            return [(st.get(name, idx, look=0), m, bank) for name, idx, m, bank in items]

        def project_group(chs, act, order=range(8), hi=None):
            ah, al, at_ = act
            order = list(order)
            toks = []
            for k in order:
                first, last = k == order[0], k == order[-1]
                def high(ch):
                    (whi_, wlo_, tw, slot), m, bank = ch
                    w = [(hi or at_)[k]] + ([tw] + free[bank] if first else [])
                    for w_, st_, w in ((wlo_, first, w), (whi_, False, [])):
                        T(lambda e, w_=w_, st_=st_, k=k: e.matmul(PB[bank][0:m, :], w_[:, k, 0:m], ah[:, k, :], start=st_,
                                                                  stop=False, skip_group_check=True), *w)

                def low(ch):
                    (whi_, wlo_, tw, slot), m, bank = ch
                    t = T(lambda e, k=k, last=last: e.matmul(PB[bank][0:m, :], whi_[:, k, 0:m], al[:, k, :], start=False,
                                                             stop=last, skip_group_check=True), at_[k], inc=True)
                    if last:
                        st.hlfree[slot] = [t]
                        toks.append(t)
                for part in ([(high, low)] if last else [(high,), (low,)]):
                    for ch in chs:
                        for f in part:
                            f(ch)
            st.convert(st.next + LOOK)
            return toks

        def project_nat(name, count_, kper, banks, act):
            ah, al, at_ = act
            last = count_ * kper - 1
            for c in range(count_):
                hi, lo, tw, slot = st.get(name, c)
                for q in range(kper):
                    k = c * kper + q
                    for t in range(4):
                        cs = slice(128 * t, 128 * t + 128)
                        w = [at_[k], tw] + (free[banks[t]] if k == 0 else [])
                        tok = mm3(PB[banks[t]][:, :], ah[:, k, cs], al[:, k, cs], hi[:, q, :], lo[:, q, :],
                                  k == 0, k == last, *w)
                st.hlfree[slot] = [tok]
            return tok

        def split(f, hi, lo, tf, *w):
            th = A(lambda e: e.activation(hi, f, ACT.Copy), tf, *w)
            split.hi = th
            return V(lambda e: e.tensor_tensor(lo, f, fr(hi), ALU.subtract), th, tf, *w)

        sqfree = [[], []]
        sqn = [0]

        def square_in(src, first, tsrc, *w):
            i = sqn[0] % 2
            sqn[0] += 1
            dst = ssq[:, :] if first else sq[:, i, :]
            ts = A(lambda e: e.activation(dst, src, ACT.Square), tsrc, *w, *([] if first else sqfree[i]))
            if not first:
                prev = square_in.tok
                ts = V(lambda e: e.tensor_tensor(ssq[:, :], ssq[:, :], dst, ALU.add), ts, prev)
                sqfree[i] = [ts]
            square_in.tok = ts
            return ts

        ssq_read = [[]]

        def rsqrt_rows(bank, n, eps_n, dst, tsrc, bias=0.0, src=None, *w, more=None):
            src = ssq[:, :] if src is None else src
            tm = T(lambda e: e.matmul(PB[bank][:, :], ones, src, start=True, stop=more is None), tsrc, *free[bank], inc=True)
            if more:
                tm = T(lambda e: e.matmul(PB[bank][:, :], ones, more[0], start=False, stop=True), more[1], inc=True)
            tl = A(lambda e: e.activation(dst, PB[bank][:, :], ACT.Ln, bias=eps_n, scale=1.0 / n), tm, *w)
            free[bank] = [tl]
            te = A(lambda e: e.activation(dst, dst, ACT.Exp, scale=-0.5, bias=bias), tl)
            return te, tm

        def last_square(src, tsrc):
            i = sqn[0] % 2
            sqn[0] += 1
            return (sq[:, i, :], A(lambda e: e.activation(sq[:, i, :], src, ACT.Square), tsrc, *sqfree[i])), i

        def fence():
            return [(done[e], count[e]) for e in "GATV" if count[e]]

        def norm_split(gcol, te, tok_x, hhi, hlo, hfree, rs=None, then=None):
            rs = rsb[:, :] if rs is None else rs
            toks, reads, tok_hi = [], [], []
            norm_split.hi = tok_hi
            fb = [[], []]
            for b in range(NB):
                t = tmpf[:, b % 2, :]
                tf = V(lambda e, t=t, b=b: e.scalar_tensor_tensor(t, xT[:, b, :], gcol(b), rs, ALU.mult, ALU.mult),
                       te, tok_x[b], *fb[b % 2], *hfree)
                reads.append(tf)
                tl = split(t, hhi[:, b, :], hlo[:, b, :], tf, *hfree)
                fb[b % 2] = [tl]
                toks.append(tl)
                tok_hi.append(split.hi)
                if b == 0 and then:
                    then()
            return toks, reads

        V(lambda e: e.memset(epsc[:, 0:1], EPS))
        V(lambda e: e.memset(epsc[:, 1:2], 1.0))
        V(lambda e: e.memset(epsc[:, 2:3], math.log(128 ** -0.5)))
        V(lambda e: e.memset(epsc[:, 4:5], EPS * EPS))
        t_eps = V(lambda e: e.memset(epsc[:, 3:4], math.pi / 2))
        eps_c, one_c, dk_c, hpi_c, eps2_c = (epsc[:, i:i + 1] for i in range(5))

        def preload(name, *w):
            queue["A"].append((w, lambda e: e.preload_act_table_set(name), False))

        ple = nc.dram_tensor("ple_scratch", (D, S), F32, kind="Internal").ap()
        one = ExitStack()
        with one:
            zs = sb(one, "zs", [128, 8, S])
            cosk, sink = (sb(one, n, [128, S]) for n in ("cosk", "sink"))
            krs = sb(one, "krs", [96, S])
            gbt = sb(one, "gbt", [128, NB, S])
            hhi = sb(one, "hhi", [128, NB, S], F32R)
            hlo = sb(one, "hlo", [128, NB, S], F32R)
            gst = ExitStack()
            cbt = sb(gst, "cbt", [128, D])
            junk = sb(gst, "junk", [128, D], BF16)
            pre = ExitStack()
            pf = sb(pre, "pf", [128, 2, S])
            phi = sb(pre, "phi", [128, 2, S], F32R)
            plo = sb(pre, "plo", [128, 2, S], F32R)
            adab = sb(pre, "adab", [128, 8, D])
            posi = sb(pre, "posi", [128, S], I32)
            ang = sb(pre, "ang", [128, S])
            rn = sb(pre, "rn", [128, S])
            rk = sb(pre, "rk", [128, S])
            t_c = GDMA("c", cbt[:, :], c_d.to_broadcast([128, D]))
            t_pos = GDMA("pos", posi[:, :], pos_d.to_broadcast([128, S]))
            t_x = [DMA(f"x{b}", xT[:, b, :], x_d[b * 128:b * 128 + 128, :]) for b in range(NB)]
            t_p = DMA("p", pf[:, :, :], p_d.rearrange("(a p) n -> p a n", p=128))
            for i in range(NRAW):
                st.load(i)
            def ada_rows(n):
                return ada_d[128 * (n // 2) + 1024 * (n % 2):128 * (n // 2) + 1024 * (n % 2) + 128, :]
            t_ada = [DMA(f"ada{n}", adab[:, n, :], ada_rows(n)) for n in range(8)]

            t = G(lambda e: e.tensor_copy(ang[:, :], posi[:, :]), t_pos)
            t = G(lambda e: e.tensor_scalar(ang[:, :], ang[:, :], cst[:, O_COL:O_COL + 1], None, ALU.mult), t, t_cst)
            parts, rest = [], 2 * math.pi
            for _ in range(4):
                q = 2.0 ** (math.floor(math.log2(rest)) - 11)
                parts.append(math.floor(rest / q) * q)
                rest -= parts[-1]
            for step_ in (2048.0, 1.0):
                t = G(lambda e, s_=step_: e.tensor_scalar(rn[:, :], ang[:, :], 1 / (2 * math.pi * s_), 12582912.0,
                                                          ALU.mult, ALU.add), t)
                t = G(lambda e: e.tensor_scalar(rn[:, :], rn[:, :], 12582912.0, None, ALU.subtract), t)
                for pt in parts:
                    t = G(lambda e, k=-step_ * pt: e.tensor_scalar(rk[:, :], rn[:, :], k, None, ALU.mult), t)
                    t = G(lambda e: e.tensor_tensor(ang[:, :], ang[:, :], rk[:, :], ALU.add), t)
            lim = float(np.float32(3.1415925))
            t_ang = G(lambda e: e.tensor_scalar(ang[:, :], ang[:, :], lim, -lim, ALU.min, ALU.max), t)

            preload(EXPLN)
            for b in range(NB):
                i = b % 2
                ts = A(lambda e, b=b, i=i: e.activation(sq[:, i, :], xT[:, b, :], ACT.Square), t_x[b], *sqfree[i])
                tm = T(lambda e, b=b, i=i: e.matmul(PB[7][:, :], ones, sq[:, i, :], start=b == 0, stop=b == 7),
                       ts, t_cst, inc=True)
                sqfree[i] = [tm]
            tl = A(lambda e: e.activation(rsb[:, :], PB[7][:, :], ACT.Ln, bias=eps_c, scale=1.0 / D), tm, t_eps)
            te = A(lambda e: e.activation(rsb[:, :], rsb[:, :], ACT.Exp, scale=-0.5), tl)
            free[7] = [tl]
            t_xr = [V(lambda e, b=b: e.tensor_tensor(xT[:, b, :], xT[:, b, :], rsb[:, :], ALU.mult), te, t_x[b])
                    for b in range(NB)]

            tpl = [split(pf[:, k, :], phi[:, k, :], plo[:, k, :], t_p) for k in range(2)]
            gjunk[0], gcb[0], gcb[1] = junk, cbt, [t_c]
            t_ple = []
            for i in range(2):
                ch = st.get("pp", i, 2 - i)
                for q in range(4):
                    m = 4 * i + q
                    b = m % 4
                    tp = project(None, None, 128, b, (phi, plo, tpl), n0=128 * q, chunk=ch)
                    te = A(lambda e, m=m, b=b: e.activation(zs[:, m, :], PB[b][:, :], ACT.Copy, scale=0.5), tp, t_rc)
                    free[b] = [te]
                    t_ple.append(DMA("ple", ple[128 * m:128 * m + 128, :], zs[:, m, :], te))
            t_ple = t_ple[-1]

            t_bc = V(lambda e: e.tensor_scalar(sc8[:, 0:8], vec[:, V_BA + 8:V_BA + 16], 1.0, None, ALU.add), t_vec)
            th, fb, t_xused, thi = [], [[], []], [], []

            def low(b):
                y, hi, lo = tmpf[:, b % 2, :], hhi[:, b, :], hlo[:, b, :]
                th.append(V(lambda e: e.tensor_tensor(lo, y, fr(hi), ALU.subtract), thi[b], t_xused[b]))
                fb[b % 2] = [th[b]]
            chs = group([("sbq", 0, 128, 0)])
            for b in range(NB):
                if b == 3:
                    chs += group([("sbq", i, 128, i) for i in range(1, 4)])
                for n in (2 * b, 2 * b + 1):
                    t = V(lambda e, n=n: e.tensor_tensor_reduce(
                        out=junk[:, :], in0=adab[:, n % 8, :], in1=cbt[:, :], scale=1.0, scalar=0.0, op0=ALU.mult,
                        op1=ALU.add, accum_out=mod[:, n // 2 + 8 * (n % 2):n // 2 + 8 * (n % 2) + 1]),
                        t_ada[n], t_c, *gate_tok[-1:])
                    gate_tok.append(t)
                    if n < 8:
                        t_ada.append(DMA(f"ada{8 + n}", adab[:, n, :], ada_rows(8 + n), t))
                t1 = V(lambda e, b=b: e.tensor_tensor(mod[:, b:b + 1], mod[:, b:b + 1], vc(V_BA + b), ALU.add), t, t_vec)
                t2 = V(lambda e, b=b: e.scalar_tensor_tensor(sc8[:, b:b + 1], mod[:, 8 + b:9 + b], sc8[:, b:b + 1],
                                                             vc(V_NG + b), ALU.add, ALU.mult), t, t_bc)
                y = tmpf[:, b % 2, :]
                tf = A(lambda e, y=y, b=b: e.activation(y, xT[:, b, :], ACT.Identity, scale=sc8[:, b:b + 1],
                                                        bias=mod[:, b:b + 1]), t1, t2, t_xr[b], *fb[b % 2])
                t_xused.append(tf)
                thi.append(A(lambda e, y=y, d=hhi[:, b, :]: e.activation(d, y, ACT.Copy), tf))
                if b:
                    low(b - 1)
            low(NB - 1)
            h1 = (hhi, hlo, th)

            def drain(g):
                for _ in g:
                    pass

            def step(g, n=1):
                for _ in range(n):
                    next(g, None)

            ring = [0]

            def nextbank(n=4):
                b = ring[0] % n
                ring[0] += 1
                return b

            preload(SILU)
            ts = A(lambda e: e.activation(sink[:, :], ang[:, :], ACT.Sin), t_ang, t_rc)
            tc = A(lambda e: e.activation(rn[:, :], ang[:, :], ACT.Abs), t_ang)
            t_cos = A(lambda e: e.activation(cosk[:, :], rn[:, :], ACT.Sin, scale=-1.0, bias=hpi_c), tc, t_eps)
            preload(EXPLN)
            t_rope = V(lambda e: e.tensor_scalar(sink[:, :], sink[:, :], cst[:, O_COL + 1:O_COL + 2], None, ALU.mult), ts)
            f_pre = fence()
            pre.close()

            gax = xT
            LEN = [512, 384, 256, 128]
            BK = [0, 1, 2, 1]
            BO = [0, 0, 0, 384]
            SO = [0, 512, 1024, 896]
            THIRDS = ((0, 512), (1, 512), (2, 256))
            qs = 96 ** -0.5
            SWAP = [(i + 16) % 32 for i in range(32)]
            rope_free, rope_pool = [[*fb[0], *fb[1]], [t_xr[-1]]], []
            ropes, square_reads = [0], {}
            tga, tgb, tzs, tcq = [None] * 8, [None] * 8, [None] * 8, [None] * 5
            late = {}

            def rope(bank, dst, tp, *w):
                i = ropes[0] % 2
                ropes[0] += 1
                buf = (tmpf, sq)[i]
                if i:
                    w0 = (*sqfree[0], *sqfree[1])
                else:
                    w0 = ()
                x, r0, r1 = PB[bank][64:96, :], buf[64:96, 0, :], buf[64:96, 1, :]
                t1 = V(lambda e: e.stream_shuffle(r0, x, SWAP), tp, *rope_free[i], *w0)
                t2 = V(lambda e: e.tensor_tensor(r1, x, cosk[64:96, :], ALU.mult), tp, t_cos, *rope_free[i], *w0)
                t1 = V(lambda e: e.tensor_tensor(r0, r0, sink[64:96, :], ALU.mult), t1, t_rope)
                t3 = G(lambda e: e.tensor_tensor(dst, r0, r1, ALU.add), t1, t2, *rope_pool, *w)
                rope_free[i] = [t3]
                rope_pool[:] = [t3]
                if i:
                    sqfree[0], sqfree[1] = [t3], [t3]
                return t2, t3

            def latent_norm(lo_, n_, g_, rk):
                te, tm = rsqrt_rows(6, rk, eps_c, rsb[:, :], square_in.tok, 0.0, None, *t_xr, *(late["rsb"] if lo_ else []))
                ssq_read[0] = [tm]
                for m in range(n_):
                    k = lo_ + m
                    tcq[k] = V(lambda e, k=k, g=g_ + m: e.scalar_tensor_tensor(
                        gbt[:, k, :], gbt[:, k, :], vc(g), rsb[:, :], ALU.mult, ALU.mult), te, square_reads[k])
                late["rsb"] = [tcq[lo_ + n_ - 1]]

            def filler_a():
                for m in range(5):
                    tp = project(*(("cq", m) if m < 3 else ("ckv", m - 3)), 128, 7, h1)
                    tcq[m] = V(lambda e, m=m: e.tensor_copy(gbt[:, m, :], PB[7][:, :]), tp)
                    free[7] = [tcq[m]]
                    if m == 3:
                        yield
                        latent_norm(0, 3, V_QN, 384)
                    square_reads[m] = square_in(gbt[:, m, :], m in (0, 3), tcq[m], *(ssq_read[0] if m in (0, 3) else []))
                    if m != 3:
                        yield
                tp = project("kr", 0, 96, 7, h1)
                t2, late["kr"] = rope(7, krs[64:96, :], tp)
                free[7] = [t2]
                yield
                latent_norm(3, 2, V_KN, 256)
                for m in range(8):
                    tp = project(*(("sz", m) if m < 4 else ("mz", m - 4)), 128, 7, h1)
                    tzs[m] = V(lambda e, m=m: e.tensor_copy(zs[:, m, :], PB[7][:, :]), tp, t_ple)
                    free[7] = [tzs[m]]
                    yield
                for m in range(6):
                    b = 0 if m == 4 else 7
                    tp = project("ga", m, 128, b, h1)
                    tga[m] = V(lambda e, m=m, b=b: e.tensor_copy(gax[:, m, :], PB[b][:, :]), tp, t_xused[m])
                    free[b] = [tga[m]]
                    yield
                tps = [project("ga", m, 128, b, h1) for m, b in ((6, 0), (7, 3))]
                yield
                for m, b in ((6, 0), (7, 3)):
                    tga[m] = A(lambda e, m=m, b=b: e.activation(gax[:, m, :], PB[b][:, :], ACT.Copy), tps[m - 6], t_xused[m])
                    free[b] = [tga[m]]

            fa = filler_a()
            t_oa = [None] * 4
            with ExitStack() as s1:
                qp = sb(s1, "qp", [128, 8, S])
                kp = sb(s1, "kp", [128, 4, S])
                sbv = sb(s1, "sbv", [128, 4, S])
                sp = sb(s1, "sp", [128, 2, 1280])
                sph = sb(s1, "sph", [128, 1280], F32R)
                spl = sb(s1, "spl", [128, 1280], F32R)
                tz = []
                for r in range(2):
                    tz.append(G(lambda e, r=r: e.memset(
                        qp[64 - 64 * r:128 - 64 * r, :, :].rearrange("p (m r) n -> p m r n", r=2)[:, :, r, :], 0.0),
                        *f_pre, *tz))
                tqp, tkp = [], []
                tps = project_group(chs, h1, hi=thi)

                def evac_q(m, b, tp):
                    for r in range(2):
                        te = A(lambda e, b=b, m=m, r=r: e.activation(
                            qp[64 * r:64 * r + 64, 2 * m + r, :], PB[b][64 * r:64 * r + 64, :], ACT.Copy, scale=0.125),
                            tp, *f_pre)
                        tqp.append(te)
                    free[b] = [te]
                for m in range(4):
                    evac_q(m, m, tps[m])
                for m in range(4):
                    b = 4 + m % 4
                    tp = project("sbk", m, 128, b, h1)
                    te = V(lambda e, b=b, m=m: e.tensor_copy(kp[:, m, :], PB[b][:, :]), tp, *f_pre)
                    free[b] = [te]
                    tkp.append(te)
                tp = project_nat("sbv", 4, 2, [3, 4, 5, 6], h1)
                for t_ in range(4):
                    te = A(lambda e, t_=t_: e.activation(sbv[:, t_, :], PB[3 + t_][:, :], ACT.Copy), tp, *f_pre)
                    free[3 + t_] = [te]
                t_sbv = te
                use = [f_pre, f_pre]
                useh = [f_pre]
                tqk, tmx, tsp, tln = {}, {}, {}, {}

                def sb_qk(h):
                    z = 3 * (h % 2)
                    for kb in (0, 1, 3, 2):
                        n, o = LEN[kb], BO[kb]
                        out = PB[z + BK[kb]][:, o:o + n]
                        T(lambda e, out=out, kb=kb, first=kb != 3: e.matmul(
                            out, kp[:, h // 2, 128 * kb:128 * kb + 128], qp[:, h, 128 * kb:512],
                            start=first, stop=False, skip_group_check=True), tqp[h], tz[h % 2], tkp[h // 2], *free[z + BK[kb]])
                        tqk[h] = T(lambda e, out=out: e.matmul(out[:, 0:128], identB, msB, start=False, stop=False,
                                                               skip_group_check=True), t_rc, inc=True)

                def sb_pre(h):
                    z, i = 3 * (h % 2), h % 2
                    for b, n in THIRDS:
                        t1 = V(lambda e, b=b, n=n: e.tensor_scalar(sp[:, i, 512 * b:512 * b + n], PB[z + b][:, 0:n], 40.0,
                                                                   None, ALU.min), tqk[h], *use[i])
                    t1 = A(lambda e: e.activation(sp[:, i, :], sp[:, i, :], ACT.Exp), t1)
                    t1 = A(lambda e: e.activation(sp[:, i, :], sp[:, i, :], ACT.Ln, bias=one_c), t1)
                    tln[h] = t1

                def sb_pre2(h):
                    z, i, t1 = 3 * (h % 2), h % 2, tln[h]
                    for b, n in THIRDS:
                        v = sp[:, i, 512 * b:512 * b + n]
                        t2 = V(lambda e, b=b, n=n, v=v: e.tensor_tensor(v, PB[z + b][:, 0:n], v, ALU.max), t1)
                    tmx[h] = t2
                    t3 = A(lambda e: e.activation(sph[:, :], sp[:, i, :], ACT.Copy), t2, *useh[0])
                    t4 = V(lambda e: e.tensor_tensor(spl[:, 1024:], sp[:, i, 1024:], fr(sph[:, 1024:]), ALU.subtract), t3,
                           *useh[0])
                    t3 = G(lambda e: e.tensor_tensor(spl[:, 0:896], sp[:, i, 0:896], fr(sph[:, 0:896]), ALU.subtract),
                           t3, tz[1], *rope_pool, *useh[0])
                    tsp[h] = (t3, t4)

                def sb_suffix(h):
                    z, i = 3 * (h % 2), h % 2
                    for kb in range(4):
                        out = PB[z + BK[kb]][:, BO[kb] + 128 * (3 - kb):BO[kb] + 128 * (4 - kb)]
                        w = cb(O_TRI if kb == 3 else O_NONES)
                        tk = T(lambda e, out=out, w=w: e.matmul(out, w, sp[:, i, 896:1024], start=False, stop=False,
                                                                skip_group_check=True), tmx[h], inc=True)
                    for kb in range(3):
                        for jb in range(kb, 3):
                            o = BO[kb] + 128 * (jb - kb)
                            out = PB[z + BK[kb]][:, o:o + LEN[jb]]
                            w = triR if jb == kb else nonesR
                            for src in (sph, spl):
                                v = src[:, SO[jb]:SO[jb] + LEN[jb]]
                                tk = T(lambda e, out=out, w=w, v=v: e.matmul(out, w, v, start=False, stop=False,
                                                                             skip_group_check=True),
                                       *tsp[h], inc=True)
                    useh[0] = [tk]
                    for b, n in THIRDS:
                        te = A(lambda e, b=b, n=n: e.activation(sp[:, i, 512 * b:512 * b + n], PB[z + b][:, 0:n], ACT.Exp),
                               tk, *tsp[h])
                        free[z + b] = [te]
                    return te

                def sb_pv(pr, tw):
                    for kb in range(4):
                        for i in range(2):
                            tk = T(lambda e, kb=kb, i=i: e.matmul(
                                PB[6][64 * i:64 * i + 64, 128 * kb:512],
                                sbv[:, kb, 128 * pr + 64 * i:128 * pr + 64 * i + 64],
                                sp[:, i, SO[kb]:SO[kb] + LEN[kb]], start=kb == 0, stop=kb == 3, skip_group_check=True),
                                *tw, t_sbv, *free[6], inc=kb == 3)
                    use[0], use[1] = [tk], [tk]
                    te = V(lambda e: e.tensor_copy(qp[:, 2 * pr, :], PB[6][:, :]), tk, tqk[2 * pr], tqk[2 * pr + 1])
                    free[6] = [te]
                    t_oa[pr] = te

                sb_qk(0)
                sb_pre(0)
                sb_pre2(0)
                step(fa)
                for pr in range(4):
                    h = 2 * pr
                    sb_qk(h + 1)
                    step(fa)
                    tw = [sb_suffix(h)]
                    sb_pre(h + 1)
                    step(fa)
                    sb_pre2(h + 1)
                    if pr < 3:
                        sb_qk(h + 2)
                    step(fa)
                    tw.append(sb_suffix(h + 1))
                    step(fa)
                    sb_pv(pr, tw)
                    if pr < 3:
                        sb_pre(h + 2)
                        step(fa)
                        if pr == 2:
                            preload(SILU)
                            for m in range(8):
                                tzs[m] = A(lambda e, m=m: e.activation(zs[:, m, :], zs[:, m, :], ACT.Silu), tzs[m])
                            preload(EXPLN)
                        sb_pre2(h + 2)
                for m in range(4):
                    tzs[m] = V(lambda e, m=m: e.tensor_tensor(zs[:, m, :], zs[:, m, :], qp[:, 2 * m, :], ALU.mult),
                               tzs[m], t_oa[m])
                f1 = fence()
            gst.close()

            s2 = ExitStack()
            qc = sb(s2, "qc", [128, 8, S])
            kc = sb(s2, "kc", [128, 8, S])
            vb = sb(s2, "vb", [128, 4, S])
            s3 = ExitStack()
            chi = sb(s3, "chi", [128, 5, S], F32R)
            clo = sb(s3, "clo", [128, 5, S], F32R)
            step(fa)
            tcl = [split(gbt[:, k, :], chi[:, k, :], clo[:, k, :], tcq[k], *f1) for k in range(5)]
            cact = (chi, clo, tcl)
            drain(fa)
            t_kc = V(lambda e: e.tensor_scalar(kc[64:96, :, :], krs[64:96, :].rearrange("p (a b) -> p a b", a=1)
                                               .to_broadcast([32, 8, S]), qs, None, ALU.mult), late["kr"], *f1)
            tqc, tkc = [], []
            for h in range(8):
                if h in (0, 3, 6):
                    ch = st.get("uq", h // 3)
                b = nextbank()
                tp = project(None, None, 96, b, cact, n0=96 * (h % 3), chunk=ch)
                te = A(lambda e, h=h, b=b: e.activation(qc[0:64, h, :], PB[b][0:64, :], ACT.Copy), tp, *f1)
                t2, t3 = rope(b, qc[64:96, h, :], tp, *f1)
                free[b] = [te, t2]
                tqc.append((te, t3))
            ch = st.get("uk", 0)
            for p_ in range(4):
                b = nextbank()
                tp = project(None, None, 128, b, (chi[:, 3:5, :], clo[:, 3:5, :], tcl[3:5]), n0=128 * p_, chunk=ch)
                t1 = A(lambda e, p_=p_, b=b: e.activation(kc[0:64, 2 * p_, :], PB[b][0:64, :], ACT.Copy, scale=qs), tp, *f1)
                t2 = V(lambda e, p_=p_, b=b: e.tensor_scalar(kc[0:64, 2 * p_ + 1, :], PB[b][64:128, :], qs, None, ALU.mult),
                       tp, *f1)
                free[b] = [t1, t2]
                tkc.append((t1, t2))
            hi, lo, tw, slot = st.get("uv", 0)
            for t_ in range(4):
                cs = slice(128 * t_, 128 * t_ + 128)
                b = 3 + t_
                for k in range(2):
                    tok = mm3(PB[b][:, :], chi[:, 3 + k, cs], clo[:, 3 + k, cs], hi[:, k, :], lo[:, k, :],
                              k == 0, k == 1, tw, tcl[3 + k], *free[b])
                t_vb = A(lambda e, t_=t_, b=b: e.activation(vb[:, t_, :], PB[b][:, :], ACT.Copy), tok, *f1)
                free[b] = [t_vb]
            st.hlfree[slot] = [tok]
            f_c = [tok, t_vb, t_kc]
            s3.close()
            t_oh = []

            def filler_b():
                for m in range(8):
                    b = 7
                    kt = []
                    tp = project("gb", m, 128, b, h1, ktok=kt)
                    tgb[m] = V(lambda e, m=m, b=b: e.tensor_copy(gbt[:, m, :], PB[b][:, :]), tp, *tcl)
                    free[b] = [tgb[m]]
                    if m == 2:
                        preload(SILU)
                        for k in range(8):
                            tga[k] = A(lambda e, k=k: e.activation(gax[:, k, :], gax[:, k, :], ACT.Tanh, scale=0.5), tga[k])
                        preload(EXPLN)
                    if m == 7:
                        late["gb"] = tp
                        t_oh.extend(split(zs[:, k, :], hhi[:, k, :], hlo[:, k, :], tzs[k], kt[k]) for k in range(4))
                    yield
                for i in range(4):
                    ch = st.get("wa", i)
                    for q in range(2):
                        m = 2 * i + q
                        b = 7 if m < 5 else m - 5
                        tp = project(None, None, 128, b, (hhi, hlo, t_oh), n0=128 * q, chunk=ch)
                        tga[m] = V(lambda e, m=m, b=b: e.scalar_tensor_tensor(gax[:, m, :], gax[:, m, :], 1.0, PB[b][:, :],
                                                                              ALU.add, ALU.mult), tp, tga[m])
                        free[b] = [tga[m]]
                        yield

            QB, QO = [1, 2, 1, 0], [384, 0, 0, 0]
            QN = [128, 256, 384, 512]
            PO = [896, 1024, 512, 0]

            def softmax_attention(pfx, scr, f0, q_of, k_of, tq_of, v_all, tv, combine, fill, cbias=None):
                P = sb(scr, pfx + "P", [128, 1280])
                PT = sb(scr, pfx + "PT", [128, 2, 1280])
                nm = sb(scr, pfx + "nm", [128, 2, 4])
                rs = sb(scr, pfx + "rs", [128, 2, 4])
                state = {"P": f0, "PT": f0}
                texp = {}

                def qk(h):
                    for qi in (3, 2, 0, 1):
                        o, n, b = QO[qi], QN[qi], QB[qi]
                        out = PB[b][:, o:o + n]
                        T(lambda e, out=out, q_=q_of(h, qi), k_=k_of(h, n), qi=qi: e.matmul(
                            out, q_, k_, start=qi != 0, stop=False, skip_group_check=True), *tq_of(h), *free[b])
                        tk = T(lambda e, out=out, n=n, qi=qi: e.matmul(
                            out[:, n - 128:n], identB, mcB, start=False, stop=qi != 2, skip_group_check=True), inc=True)
                    if cbias:
                        cbias("used", h, tk)
                    i = h % 2
                    src = {qi: PB[QB[qi]][:, QO[qi]:QO[qi] + QN[qi]] for qi in range(4)}
                    cb_, tcb = cbias("get", h, None) if cbias else (None, None)
                    for qi in (3, 2, 0, 1):
                        d = P[:, PO[qi]:PO[qi] + QN[qi]]
                        if cbias:
                            tm = V(lambda e, s_=src[qi], qi=qi, d=d: e.tensor_tensor_reduce(
                                out=d, in0=s_, in1=cb_[:, 0:QN[qi]], scale=1.0, scalar=-3.0e38, op0=ALU.add, op1=ALU.max,
                                accum_out=nm[:, i, qi:qi + 1]), tk, tcb, *state["P"])
                        else:
                            tm = V(lambda e, s_=src[qi], qi=qi: e.tensor_reduce(nm[:, i, qi:qi + 1], s_, AX.X, ALU.max),
                                   tk, *state["P"])
                    if cbias:
                        cbias("done", h, tm)
                    tm2 = V(lambda e: e.tensor_scalar(nm[:, i, :], nm[:, i, :], -1.0, None, ALU.mult), tm)
                    for qi in (3, 2, 0, 1):
                        d = P[:, PO[qi]:PO[qi] + QN[qi]]
                        te = A(lambda e, s_=d if cbias else src[qi], qi=qi, d=d: e.activation(
                            d, s_, ACT.Exp, bias=nm[:, i, qi:qi + 1], accum_out=rs[:, i, qi:qi + 1]), tm2, *state["P"])
                    for b in range(3):
                        free[b] = [tm] if cbias else [te]
                    tr = V(lambda e: e.reciprocal(rs[:, i, :], rs[:, i, :]), te)
                    for qi in (3, 2, 0, 1):
                        d = P[:, PO[qi]:PO[qi] + QN[qi]]
                        texp[h] = V(lambda e, qi=qi, d=d: e.tensor_scalar(d, d, rs[:, i, qi:qi + 1], None, ALU.mult), tr, te)

                def turn(h):
                    toks = []
                    for kb, b, o in ((0, 3, 0), (1, 4, 0), (3, 4, 384), (2, 6, 0)):
                        for qi in range(kb, 4):
                            src = P[:, PO[qi] + 128 * kb:PO[qi] + 128 * kb + 128]
                            dst = PB[b][:, o + 128 * (qi - kb):o + 128 * (qi - kb) + 128]
                            tk = T(lambda e, src=src, dst=dst: e.transpose(dst, src, ident), texp[h], *free[b], inc=True)
                        if kb == 1:
                            continue
                        n, d0 = {0: (512, 0), 3: (512, 512), 2: (256, 1024)}[kb]
                        dd, ss = PT[:, h % 2, d0:d0 + n], PB[b][:, 0:n]
                        if kb == 3 or (cbias and kb == 0):
                            te = A(lambda e, dd=dd, ss=ss: e.activation(dd, ss, ACT.Copy), tk, *state["PT"])
                        else:
                            te = V(lambda e, dd=dd, ss=ss: e.tensor_copy(dd, ss), tk, *state["PT"])
                        free[b] = [te]
                        toks.append(te)
                    state["P"] = [tk]
                    return toks

                def pv(pr, toks):
                    for kb in range(4):
                        for i in range(2):
                            tk = T(lambda e, kb=kb, i=i: e.matmul(
                                PB[5][64 * i:64 * i + 64, 128 * kb:512],
                                v_all[:, kb, 128 * pr + 64 * i:128 * pr + 64 * i + 64],
                                PT[:, i, SO[kb]:SO[kb] + LEN[kb]], start=kb == 0, stop=kb == 3, skip_group_check=True),
                                *toks, *tv, *free[5], inc=kb == 3)
                    state["PT"] = [tk]
                    free[5] = [combine(pr, 5, tk)]

                qk(0)
                step(fill)
                for pr in range(4):
                    h = 2 * pr
                    toks = turn(h)
                    qk(h + 1)
                    step(fill)
                    toks += turn(h + 1)
                    if pr < 3:
                        qk(h + 2)
                    step(fill)
                    pv(pr, toks)
                    step(fill)

            def comb(pr, bank, tk):
                tzs[4 + pr] = V(lambda e: e.tensor_tensor(zs[:, 4 + pr, :], zs[:, 4 + pr, :], PB[bank][:, :], ALU.mult),
                                tk, tzs[4 + pr])
                r = tzs[4 + pr]
                if "gb" in late:
                    while late["oh"] <= pr:
                        k = 4 + late["oh"]
                        t_oh.append(split(zs[:, k, :], hhi[:, k, :], hlo[:, k, :], tzs[k], late["gb"]))
                        late["oh"] += 1
                return r

            late["oh"] = 0
            fw = filler_b()
            softmax_attention(
                "m", s2, f_c, lambda h, qi: qc[0:96, h, 128 * qi:128 * qi + 128], lambda h, n: kc[0:96, h, 0:n],
                lambda h: (*tqc[h], *tkc[h // 2], t_kc), vb, [t_vb], comb, fw)
            drain(fw)
            f2 = fence()
            s2.close()

            s5 = ExitStack()
            mhi = sb(s5, "mhi", [128, NB, S], F32R)
            mlo = sb(s5, "mlo", [128, NB, S], F32R)
            t_gate = V(lambda e: e.tensor_tensor(mod[:, 16:24], mod[:, 16:24], vec[:, V_BA + 16:V_BA + 24], ALU.add),
                       gate_tok[-1])
            t_gate = V(lambda e: e.tensor_scalar(mod[:, 16:24], mod[:, 16:24], 0.5, None, ALU.mult), t_gate)
            preload(SILU)
            tmg = []
            t_x = []
            for i in range(4):
                ch = st.get("wb", i)
                for q in range(2):
                    m, b = 2 * i + q, nextbank()
                    tgb[m] = A(lambda e, m=m: e.activation(gbt[:, m, :], gbt[:, m, :], ACT.Tanh, scale=0.5), tgb[m])
                    tp = project(None, None, 128, b, (hhi[:, 4:8, :], hlo[:, 4:8, :], t_oh[4:8]), n0=128 * q, chunk=ch)
                    t1 = V(lambda e, m=m, b=b: e.scalar_tensor_tensor(gbt[:, m, :], gbt[:, m, :], 1.0, PB[b][:, :],
                                                                      ALU.add, ALU.mult), tp, tgb[m])
                    free[b] = [t1]
                    t1 = V(lambda e, m=m: e.tensor_tensor(gbt[:, m, :], gbt[:, m, :], gax[:, m, :], ALU.add), t1, tga[m])
                    t_x.append(GDMA(f"xx{m}", xT[:, m, :], x_d[m * 128:m * 128 + 128, :], t1))
                    tmg.append(split(gbt[:, m, :], mhi[:, m, :], mlo[:, m, :], t1, *f2))
            ssq2 = sb(s5, "ssq2", [128, S])
            t_g12 = V(lambda e: e.tensor_tensor(sc8[:, 8:16], vec[:, V_N1:V_N1 + 8], vec[:, V_AN:V_AN + 8], ALU.mult), t_vec)
            preload(EXPLN)
            tx1 = []
            chs = [(st.get("wo", m), 128, 4 + m) for m in range(2)]
            tps = project_group(chs, (mhi, mlo, tmg))
            for m in range(8):
                b = 4 + m if m < 2 else nextbank()
                tp = tps[m] if m < 2 else project("wo", m, 128, b, (mhi, mlo, tmg))
                if m == 7:
                    chs = group([("small", 0, 96, 3), ("fq", 0, 128, 0), ("fq", 1, 128, 1)])
                tx = V(lambda e, m=m, b=b: e.scalar_tensor_tensor(
                    xT[:, m, :], PB[b][:, :], mod[:, 16 + m:17 + m], xT[:, m, :], ALU.mult, ALU.add), tp, t_x[m], t_gate)
                free[b] = [tx]
                tx1.append(tx)
                tq = square_in(xT[:, m, :], m == 0, tx, *(ssq_read[0] if m == 0 else []))
                i = sqn[0] % 2
                sqn[0] += 1
                d2 = ssq2[:, :] if m == 0 else sq[:, i, :]
                tq2 = A(lambda e, m=m, d2=d2: e.activation(d2, xT[:, m, :], ACT.Square, scale=vc(V_N1 + m)), tx,
                        *(f2 if m == 0 else sqfree[i]))
                if m:
                    tq2 = V(lambda e, d2=d2: e.tensor_tensor(ssq2[:, :], ssq2[:, :], d2, ALU.add), tq2, t_pr2)
                    sqfree[i] = [tq2]
                t_pr2 = tq2
            tc = V(lambda e: e.scalar_tensor_tensor(ssq2[:, :], ssq[:, :], EPS, ssq2[:, :], ALU.mult, ALU.add), tq, tq2)
            te12, tmc = rsqrt_rows(7, D, eps2_c, sq[:, 0, :], tc, 0.0, ssq2[:, :], *sqfree[0])
            tmr = T(lambda e: e.matmul(PB[6][:, :], ones, ssq[:, :], start=True, stop=True), tq, *free[6], inc=True)
            f3 = fence()
            s5.close()

        k2 = ExitStack()
        fqo = sb(k2, "fqo", [128, 4, S])
        gzs = sb(k2, "gzs", [128, 4, S])
        gq = sb(k2, "gq", [128, 12, S])
        rowt = sb(k2, "rowt", [128, S])
        rhi = sb(k2, "rhi", [128, S], F32R)
        rlo = sb(k2, "rlo", [128, S], F32R)
        gcst = sb(k2, "gcst", [128, NGC])
        fk = sb(k2, "fk", [128, 4, S])
        fv = sb(k2, "fv", [128, 4, S])
        cols = sb(k2, "cols", [128, 3, 4, 4])
        hs = ExitStack()
        hhi = sb(hs, "hhi2", [128, NB, S], F32R)
        hlo = sb(hs, "hlo2", [128, NB, S], F32R)
        rmk = sb(hs, "rmk", [96, S])
        lg = sb(hs, "lg", [96, S])
        pr_ = sb(hs, "pr_", [96, 2])
        cbuf = sb(hs, "cbuf", [128, 2, S + 3])
        t_gc = GDMA("gcst", gcst[:, :], gc_d, *f3)
        t_rm = GDMA("rmk", rmk[:, :], rm_d, *f3)
        th, reads = norm_split(lambda b: sc8[:, 8 + b:9 + b], te12, [(t_g12)] * 8, hhi, hlo, f3, sq[:, 0, :],
                               lambda: chs.extend(group([("fq", 2, 128, 2)])))
        tl = A(lambda e: e.activation(rsb[:, :], PB[6][:, :], ACT.Ln, bias=eps_c, scale=1.0 / D), tmr, *late["rsb"])
        free[6] = [tl]
        t_r1 = A(lambda e: e.activation(rsb[:, :], rsb[:, :], ACT.Exp, scale=-0.5), tl)
        sqfree[0] = [reads[-1]]
        ssq_read[0] = [tmr]
        h2 = (hhi, hlo, th)
        tps = project_group(chs, h2, hi=norm_split.hi)

        s1c = cst[0:96, O_COL + 2:O_COL + 3]
        t1 = V(lambda e: e.tensor_tensor(pr_[:, 0:1], vc(V_DT, 0, 96), vc(V_FB, 0, 96), ALU.add), t_vec, *f3)
        ta = A(lambda e: e.activation(pr_[:, 1:2], vc(V_AL, 0, 96), ACT.Exp), *f3)
        ta = V(lambda e: e.tensor_scalar(pr_[:, 1:2], pr_[:, 1:2], -1.0, None, ALU.mult), ta)
        t1 = V(lambda e: e.tensor_scalar(rowt[0:96, :], PB[3][0:96, :], pr_[:, 0:1], s1c, ALU.add, ALU.mult), t1, tps[0], *f3)
        free[3] = [t1]
        t2 = V(lambda e: e.tensor_scalar(lg[:, :], rowt[0:96, :], 40.0, None, ALU.min), t1)
        t2 = A(lambda e: e.activation(lg[:, :], lg[:, :], ACT.Exp), t2)
        t2 = A(lambda e: e.activation(lg[:, :], lg[:, :], ACT.Ln, bias=one_c[0:96, :]), t2)

        tf_ = []
        for m in range(8):
            b = m if m < 3 else 4 + m % 4
            tp = tps[m + 1] if m < 3 else project(*(("fq", m) if m < 4 else ("fk", m - 4)), 128, b, h2)
            d = fqo[:, m, :] if m < 4 else fk[:, m - 4, :]
            te = A(lambda e, b=b, d=d, m=m: e.activation(d, PB[b][:, :], ACT.Copy, scale=0.125 if m < 4 else 1.0), tp, *f3)
            free[b] = [te]
            tf_.append(te)
            if m == 4:
                t2 = V(lambda e: e.tensor_tensor(lg[:, :], lg[:, :], rowt[0:96, :], ALU.max), t2)
                t2 = V(lambda e: e.tensor_scalar(lg[:, :], lg[:, :], pr_[:, 1:2], None, ALU.mult), t2, ta)
                t3 = V(lambda e: e.tensor_tensor_scan(rowt[0:96, :], rmk[:, :], lg[:, :], 0.0, ALU.mult, ALU.add), t2, t_rm)
                c3 = rowt[0:32, :].rearrange("p (c j) -> p c j", j=64)
                t4 = V(lambda e: e.tensor_tensor(rowt[96:128, :].rearrange("p (c j) -> p c j", j=64),
                                                 c3[:, :, 63:64].to_broadcast([32, 8, 64]), c3, ALU.subtract), t3)
                t_row = V(lambda e: e.tensor_copy(rowt[32:64, :], lg[32:64, :]), t3)
                t_rs = split(rowt[:, :], rhi[:, :], rlo[:, :], t_row, t4, *f3)
            if m > 3:
                for k in (2 * m - 8, 2 * m - 7):
                    tx1[k] = V(lambda e, k=k: e.scalar_tensor_tensor(
                        xT[:, k, :], xT[:, k, :], vc(V_N1 + k), rsb[:, :], ALU.mult, ALU.mult), t_r1, reads[k])
        nat = rsb[:, :].rearrange("p (a b) -> p a b", a=4)
        for t_ in range(4):
            tk = T(lambda e, t_=t_: e.transpose(PB[7][:, 128 * t_:128 * t_ + 128], rowt[:, 128 * t_:128 * t_ + 128], ident),
                   t_row, t4, *free[7], inc=True)
        te = V(lambda e: e.tensor_copy(nat, PB[7][:, :].rearrange("p (a b) -> p a b", a=4)), tk, *tx1)
        free[7] = [te]
        t1 = V(lambda e: e.tensor_tensor(cols[:, 1, :, :], nat[:, :, 0:4], nat[:, :, 32:36], ALU.add), te, *f3)
        A(lambda e: e.activation(cols[:, 0, :, :], nat[:, :, 32:36], ACT.Exp), te, *f3)
        A(lambda e: e.activation(cols[:, 2, :, :], nat[:, :, 96:100], ACT.Exp), te)
        t_cols = A(lambda e: e.activation(cols[:, 1, :, :], cols[:, 1, :, :], ACT.Exp), t1)
        tp = project_nat("fv", 4, 2, [0, 1, 2, 3], h2)
        for t_ in range(4):
            te = A(lambda e, t_=t_: e.activation(fv[:, t_, :], PB[t_][:, :], ACT.Copy), tp, *f3)
            free[t_] = [te]
        t_fv = te

        tz = G(lambda e: e.memset(cbuf[:, :, 0:3], 0.0), *f3)
        tgq, tgz = [None] * 12, [None] * 4
        cfree = [[tz], [tz]]

        def conv(m, b, tp):
            i = m % 2
            x = cbuf[:, i, :]
            te = A(lambda e: e.activation(x[:, 3:S + 3], PB[b][:, :], ACT.Copy), tp, *cfree[i], *f3)
            free[b] = [te]
            y = gq[:, m, :]
            t = V(lambda e: e.tensor_scalar(y, x[:, 3:S + 3], vc(V_CV + 4 * m + 3), None, ALU.mult), te, tz, *f3)
            for j in range(3):
                t = V(lambda e, j=j: e.scalar_tensor_tensor(y, x[:, j:S + j], vc(V_CV + 4 * m + j), y, ALU.mult, ALU.add), t)
            cfree[i] = [t]
            tgq[m] = t

        def filler_q():
            for m in range(12):
                b = 7
                tp = project("gqkv", m, 128, b, h2)
                conv(m, b, tp)
                yield

        fx = ExitStack()
        cbt2 = sb(fx, "cbt2", [128, 2, S])
        qz = sb(fx, "qz", [128, 2, S])
        tz0 = V(lambda e: e.memset(qz[:, :, :], 0.0), *f3)
        cbias_used = [list(f3), list(f3)]
        cbtok, tqz, texq = {}, {}, {}

        def make_q(h):
            r0, i = 64 * (h % 2), h % 2
            tqz[h] = V(lambda e: e.tensor_copy(qz[r0:r0 + 64, i, :], fqo[r0:r0 + 64, h // 2, :]), tz0, tf_[h // 2],
                       *([texq[h - 2]] if h > 1 else []))

        def make_cb(h):
            tk = spread(6, 64 + h, True, True, *free[6])
            cbtok[h] = A(lambda e: e.activation(cbt2[:, h % 2, :], PB[6][:, :], ACT.Copy, scale=-1.0), tk, *cbias_used[h % 2])
            free[6] = [cbtok[h]]

        def cbias(what, h, tok):
            if what == "get":
                return cbt2[:, h % 2, :], cbtok[h]
            if what == "used":
                texq[h] = tok
                if h < 7:
                    make_cb(h + 1)
            if what == "done":
                cbias_used[h % 2] = [tok]
                if h < 7:
                    make_q(h + 1)

        tfo = []

        def comb2(pr, bank, tk):
            te = A(lambda e: e.activation(fqo[:, pr, :], PB[bank][:, :], ACT.Copy), tk, tqz[2 * pr], tqz[2 * pr + 1])
            tfo.append(te)
            return te

        def spread(b, row, start, stop, *w):
            sel = identR[:, row:row + 1].to_broadcast([128, 128])
            T(lambda e: e.matmul(PB[b][:, :], sel, rlo[:, :], start=start, stop=False, skip_group_check=True), t_rs, *w)
            return T(lambda e: e.matmul(PB[b][:, :], sel, rhi[:, :], start=False, stop=stop, skip_group_check=True), inc=True)

        make_q(0)
        make_cb(0)
        fq_ = filler_q()

        softmax_attention(
            "f", fx, f3, lambda h, qi: qz[:, h % 2, 128 * qi:128 * qi + 128], lambda h, n: fk[:, h // 2, 0:n],
            lambda h: (tqz[h], tf_[4 + h // 2]), fv, [t_fv], comb2, fq_, cbias)
        drain(fq_)
        f4a = fence()
        fx.close()

        preload(SILU)
        for m in range(12):
            tgq[m] = A(lambda e, m=m: e.activation(gq[:, m, :], gq[:, m, :], ACT.Silu), tgq[m])
        preload(EXPLN)
        l2free = [[th[-1]], [th[-1]]]
        tsq = {}

        def l2_square(m):
            i = m % 2
            tsq[m] = V(lambda e: e.tensor_tensor(sq[:, i, :], gq[:, m, :], gq[:, m, :], ALU.mult), tgq[m], *sqfree[i])

        def l2_norm(m):
            i, b = m % 2, 4 + m % 4
            te, tm = rsqrt_rows(b, 1, eps_c, tmpf[:, i, :], tsq[m], dk_c if m < 4 else 0.0, sq[:, i, :], *l2free[i])
            sqfree[i] = [tm]
            if m < 6:
                l2_square(m + 2)
            tgq[m] = V(lambda e: e.tensor_tensor(gq[:, m, :], gq[:, m, :], tmpf[:, i, :], ALU.mult), te)
            l2free[i] = [tgq[m]]
        l2_square(0)
        l2_square(1)
        for m in range(4):
            tp = project("gz", m, 128, m, h2)
            tgz[m] = V(lambda e, m=m: e.tensor_copy(gzs[:, m, :], PB[m][:, :]), tp, *f3)
            free[m] = [tgz[m]]
            if m:
                for k in ((0, 1, 2), (3, 4, 5), (6, 7))[m - 1]:
                    l2_norm(k)
        f4 = fence()
        hs.close()

        ga_, gb_ = ExitStack(), ExitStack()
        NT, X, QKT = (sb(ga_, n, [128, 4, S]) for n in ("NT", "X", "QKT"))
        st2 = sb(ga_, "st2", [128, 2, S])
        vn2 = sb(ga_, "vn2", [128, 2, S])
        EE = sb(ga_, "EE", [128, 4, 8])
        rso = sb(ga_, "rso", [128, 4, 4])
        Y, KBG = (sb(gb_, n, [128, 4, S]) for n in ("Y", "KBG"))
        KDEC, VBN = gq[:, 4:8, :], gq[:, 8:12, :]
        pp_, sg_ = tmpf, ssq
        U, W = X, NT

        def hh(x, h, t_):
            return x[:, h, 128 * t_:128 * t_ + 128]

        def bc4(i, h):
            return cols[:, i, :, h:h + 1].to_broadcast([128, 4, 128])

        def v3(x):
            return x.rearrange("p (a b) -> p a b", a=4)

        def c3_(o, src=None):
            src = cst if src is None else src
            return src[:, o:o + 128].rearrange("p (a b) -> p a b", a=1).to_broadcast([128, 4, 128])

        gring = [0]

        def gbank():
            gring[0] += 1
            return gring[0] % 8

        def four(b, lhs, rhs, *w, start=True, stop=True):
            for t_ in range(4):
                tk = T(lambda e, t_=t_: e.matmul(PB[b][:, 128 * t_:128 * t_ + 128], lhs(t_), rhs(t_), start=start, stop=stop,
                                                 skip_group_check=True), *w, *(free[b] if start else []), inc=True)
            return tk

        def turn4(b, src, *w):
            for t_ in range(4):
                tk = T(lambda e, t_=t_: e.transpose(PB[b][:, 128 * t_:128 * t_ + 128], src(t_), ident), *w, *free[b], inc=True)
            return tk

        tkb, tkd, tvn, tnt, tqk2, teg, tqg, tW, tU = ({} for _ in range(9))
        tX, tY, tP = {}, {}, {}

        def delta():
            late["vn"] = G(lambda e: e.memset(vn2[:, :, :], 0.0), *f4)
            dfree = {(i, j): list(f4) for i in range(2) for j in range(2)}
            egfree = [list(f4), list(f4)]
            tdec = {}

            def decays(h):
                b, egb = gbank(), (rsb, ssq)[h % 2]
                tk = spread(b, h, True, False, *free[b])
                teg[h] = A(lambda e: e.activation(egb[:, :], PB[b][:, :], ACT.Exp), tk, *egfree[h % 2])
                tee = V(lambda e: e.tensor_copy(EE[:, h, :].rearrange("p (a b) -> p a b", b=1),
                                                egb[:, :].rearrange("p (a b) -> p a b", b=64)[:, :, 63:64]),
                        teg[h], *f4)
                tdec[h] = [b, tee]

            def scores(h):
                b, tee = tdec[h]
                B, d, b2, egb = PB[b], (sq, tmpf)[h % 2][:, 0, :], gbank(), (rsb, ssq)[h % 2]
                for t_ in range(4):
                    c = slice(128 * t_, 128 * t_ + 128)
                    T(lambda e, c=c: e.matmul(B[:, c], rowt[:, c], cst[:, O_NIDENT + h:O_NIDENT + h + 1]
                                              .to_broadcast([128, 128]), start=False, stop=False,
                                              skip_group_check=True), teg[h])
                    tk = T(lambda e, c=c: e.matmul(B[:, c], identB, mgB, start=False, stop=False, skip_group_check=True),
                           inc=True)
                td = A(lambda e: e.activation(d, B[:, :], ACT.Exp), tk, *dfree[h % 2, 0])
                tk = four(b2, lambda t_: hh(gq, 4 + h, t_), lambda t_: hh(gq, h, t_), tgq[4 + h], tgq[h])
                tqk2[h] = V(lambda e: e.tensor_tensor(QKT[:, h, :], PB[b2][:, :], d, ALU.mult), tk, td, *f4)
                free[b2] = [tqk2[h]]
                dfree[h % 2, 0] = [tqk2[h]]
                tqg[h] = V(lambda e: e.tensor_tensor(gq[:, h, :], gq[:, h, :], egb[:, :], ALU.mult), teg[h], tk)
                egfree[h % 2] = [tqg[h], tee]
                tdec[h].append(td)

            def keys(h):
                b, _, td = tdec[h]
                B, d, b2 = PB[b], (sq, tmpf)[h % 2][:, 1, :], gbank()
                tk = spread(b, 32 + h, False, True, td)
                tdb = A(lambda e: e.activation(d, B[:, :], ACT.Exp), tk, *dfree[h % 2, 1])
                free[b] = [tdb]
                tk = four(b2, lambda t_: hh(gq, 4 + h, t_), lambda t_: hh(gq, 4 + h, t_), tgq[4 + h])
                tnt[h] = V(lambda e: e.tensor_tensor(NT[:, h, :], PB[b2][:, :], d, ALU.mult), tk, tdb, *f4)
                free[b2] = [tnt[h]]
                dfree[h % 2, 1] = [tnt[h]]
                ty = G(lambda e: e.tensor_tensor(v3(Y[:, h, :]), v3(NT[:, h, :]), c3_(G_LT, gcst), ALU.mult),
                       tnt[h], t_gc, *f4)
                tY[h] = G(lambda e: e.tensor_tensor(v3(Y[:, h, :]), c3_(O_IDENT), v3(Y[:, h, :]), ALU.subtract), ty)

            def turn_v(h):
                b = gbank()
                tk = turn4(b, lambda t_: hh(gq, 8 + h, t_), tgq[8 + h])
                tvn[h] = V(lambda e: e.tensor_tensor(v3(VBN[:, h, :]), v3(PB[b][:, :]), bc4(0, h), ALU.mult), tk, t_cols)
                free[b] = [tvn[h]]

            def turn_k(h):
                b = gbank()
                tk = turn4(b, lambda t_: hh(gq, 4 + h, t_))
                tkb[h] = V(lambda e: e.tensor_tensor(v3(KBG[:, h, :]), v3(PB[b][:, :]), bc4(1, h), ALU.mult),
                           tk, t_cols, *f4)
                tkd[h] = V(lambda e: e.tensor_tensor(v3(KDEC[:, h, :]), v3(PB[b][:, :]), bc4(2, h), ALU.mult),
                           tk, t_cols)
                free[b] = [tkd[h]]

            def turn_y(h):
                b = gbank()
                tk = turn4(b, lambda t_: hh(Y, h, t_), tY[h])
                tX[h] = A(lambda e: e.activation(X[:, h, :], PB[b][:, :], ACT.Copy), tk, *f4)
                free[b] = [tX[h]]

            for h in (0, 2):
                decays(h)
                decays(h + 1)
                scores(h)
                turn_v(h)
                scores(h + 1)
                keys(h)
                turn_v(h + 1)
                keys(h + 1)
                turn_k(h)
                turn_k(h + 1)
                yield
                if h == 2:
                    for k in range(4):
                        turn_y(k)

            pfree = [[tqk2[3], tnt[3]], [tqk2[3], tnt[3]]]

            def level_p(lv, h):
                b, i = gbank(), h % 2
                tk = four(b, lambda t_: hh(NT, h, t_), lambda t_: hh(X, h, t_), tnt[h], tX[h])
                tP[h] = (V(lambda e: e.tensor_tensor(v3(pp_[:, i, :]), v3(PB[b][:, :]), c3_(G_LM + 128 * lv - 128, gcst),
                                                     ALU.mult), tk, t_gc, *pfree[i]), tk)
                free[b] = [tP[h][0]]

            def level_u(lv, h):
                i = h % 2
                tpp, tkx = tP[h]
                if lv < 5:
                    b = gbank()
                    tk = four(b, lambda t_: hh(Y, h, t_), lambda t_: hh(pp_, i, t_), tpp, tY[h])
                    tX[h] = V(lambda e, b=b: e.tensor_tensor(X[:, h, :], X[:, h, :], PB[b][:, :], ALU.subtract), tk, tkx, tX[h])
                    free[b] = [tX[h]]
                b = gbank()
                tk = four(b, lambda t_: hh(pp_, i, t_), lambda t_: hh(Y, h, t_), tpp, tY[h])
                pfree[i] = [tk]
                tY[h] = V(lambda e: e.tensor_tensor(Y[:, h, :], Y[:, h, :], PB[b][:, :], ALU.subtract), tk, tY[h])
                free[b] = [tY[h]]

            preload(SILU)
            for m in range(4):
                tgz[m] = A(lambda e, m=m: e.activation(gzs[:, m, :], gzs[:, m, :], ACT.Silu), tgz[m])
            preload(EXPLN)
            units = [(lv, h) for lv in range(1, 6) for h in range(4)]
            level_p(*units[0])
            for n, (lv, h) in enumerate(units):
                if n + 1 < len(units):
                    level_p(*units[n + 1])
                level_u(lv, h)
                yield

            for h in range(4):
                b = gbank()
                tk = four(b, lambda t_, h=h: hh(KBG, h, t_), lambda t_, h=h: hh(Y, h, t_), tkb[h], tY[h])
                tW[h] = A(lambda e, h=h, b=b: e.activation(W[:, h, :], PB[b][:, :], ACT.Copy), tk, tP[h][1])
                free[b] = [tW[h]]
                if h % 2:
                    yield
            for t_ in range(4):
                b = gbank()
                for h in range(4):
                    tk = T(lambda e, t_=t_, h=h, b=b: e.matmul(PB[b][:, 128 * h:128 * h + 128], hh(Y, h, t_), hh(VBN, h, t_),
                                                               start=True, stop=True, skip_group_check=True),
                           tvn[h], tY[h], *free[b], inc=True)
                tU[t_] = A(lambda e, t_=t_, b=b: e.activation(U[:, t_, :], PB[b][:, :], ACT.Copy), tk,
                           *(x[1] for x in tP.values()))
                free[b] = [tU[t_]]
                if t_ % 2:
                    yield

        drain(delta())
        f5 = fence()
        gb_.close()

        hs = ExitStack()
        hhi = sb(hs, "hhi3", [128, NB, S], F32R)
        hlo = sb(hs, "hlo3", [128, NB, S], F32R)
        tm_ = [None] * 8
        tS = V(lambda e: e.memset(st2[:, 0, :], 0.0), *f5)
        tfree_S = [[], list(f5)]
        tvf = [[], []]
        t_sg = []
        tgo, tg_nat = {}, {}
        tgate = []

        def out_norm(t_):
            b = 4 + t_ % 2
            for h in range(4):
                ts = A(lambda e, h=h: e.activation(sq[:, t_ % 2, 128 * h:128 * h + 128], PB[b][:, 128 * h:128 * h + 128],
                                                   ACT.Square, accum_out=rso[:, t_, h:h + 1]), tgo[t_], *sqfree[t_ % 2], *f5)
            sqfree[t_ % 2] = [ts]
            t1 = A(lambda e: e.activation(rso[:, t_, :], rso[:, t_, :], ACT.Ln, bias=eps_c, scale=1.0 / 128), ts)
            t1 = A(lambda e: e.activation(rso[:, t_, :], rso[:, t_, :], ACT.Exp, scale=-0.5), t1)
            tg_nat[t_] = V(lambda e: e.tensor_tensor(
                v3(VBN[:, t_, :]), v3(PB[b][:, :]), rso[:, t_, :].rearrange("p (a b) -> p a b", b=1)
                .to_broadcast([128, 4, 128]), ALU.mult), t1)
            free[b] = [tg_nat[t_]]

        def out_turn(t_):
            b = 6 + t_ % 2
            tk = turn4(b, lambda h: VBN[:, t_, 128 * h:128 * h + 128], tg_nat[t_])
            c = slice(128 * t_, 128 * t_ + 128)
            tgate.append(V(lambda e: e.scalar_tensor_tensor(gzs[:, :, c], v3(PB[b][:, :]), vc(V_GN), gzs[:, :, c],
                                                            ALU.mult, ALU.mult), tk))
            free[b] = [tgate[-1]]

        for m in range(4):
            tm_[4 + m] = split(fqo[:, m, :], hhi[:, 4 + m, :], hlo[:, 4 + m, :], tfo[m], *f5)
        for c in range(8):
            t_, p0, cur, nx = c // 2, 64 * (c % 2), c % 2, (c + 1) % 2
            cs = slice(64 * c, 64 * c + 64)
            wb_, sb_, ob = c % 2, 2 + c % 2, 4 + t_ % 2
            for h in range(4):
                tk = T(lambda e, h=h, p0=p0, cs=cs, cur=cur, wb_=wb_: e.matmul(
                    PB[wb_][p0:p0 + 64, 128 * h:128 * h + 128], W[:, h, cs], st2[:, cur, 128 * h:128 * h + 128],
                    start=True, stop=True, skip_group_check=True), tW[h], tS, *free[wb_], inc=True)
            tv_ = V(lambda e, t_=t_, p0=p0, wb_=wb_, c=c: e.tensor_tensor(
                vn2[p0:p0 + 64, c % 2, :], U[p0:p0 + 64, t_, :], PB[wb_][p0:p0 + 64, :], ALU.subtract),
                tk, tU[t_], *tvf[c % 2], late["vn"])
            free[wb_] = [tv_]
            for h in range(4):
                tko = T(lambda e, h=h, cs=cs, cur=cur, ob=ob, p0=p0: e.matmul(
                    PB[ob][p0:p0 + 64, 128 * h:128 * h + 128], gq[:, h, cs], st2[:, cur, 128 * h:128 * h + 128],
                    start=h == 0, stop=False, skip_group_check=True), tqg[h], tS, *free[ob], inc=True)
            if c < 7:
                tsg = G(lambda e, c=c, cur=cur: e.tensor_tensor(v3(sg_[:, :]), v3(st2[:, cur, :]),
                                                               EE[:, :, c:c + 1].to_broadcast([128, 4, 128]),
                                                               ALU.mult), tS, *t_sg, *f5)
                for h in range(4):
                    tk = T(lambda e, h=h, t_=t_, sb_=sb_, c=c: e.matmul(
                        PB[sb_][:, 128 * h:128 * h + 128], KDEC[:, h, 128 * t_:128 * t_ + 128],
                        vn2[:, c % 2, 128 * h:128 * h + 128], start=True, stop=True, skip_group_check=True),
                        tv_, tkd[h], *free[sb_], inc=True)
                tS = V(lambda e, nx=nx, sb_=sb_: e.tensor_tensor(st2[:, nx, :], sg_[:, :], PB[sb_][:, :], ALU.add),
                       tk, tsg, *tfree_S[nx])
                free[sb_] = [tS]
                t_sg = [tS]
            for h in range(4):
                tk = T(lambda e, h=h, p0=p0, t_=t_, ob=ob, c=c: e.matmul(
                    PB[ob][p0:p0 + 64, 128 * h:128 * h + 128], QKT[:, h, 128 * t_ + p0:128 * t_ + p0 + 64],
                    vn2[:, c % 2, 128 * h:128 * h + 128], start=False, stop=True, skip_group_check=True),
                    tv_, tqk2[h], inc=True)
            tvf[c % 2] = [tk]
            tfree_S[cur] = [tk]
            if c % 2:
                tgo[t_] = tk
                out_norm(t_)
                if t_:
                    out_turn(t_ - 1)
        chs = group([("wo2", i, 128, i) for i in range(4)])
        free_o = list(tgate)
        out_turn(3)
        for m in range(4):
            tm_[m] = split(gzs[:, m, :], hhi[:, m, :], hlo[:, m, :], tgate[-1], *f5)

        def residual(bank, m, tp, txs):
            tx = V(lambda e: e.tensor_tensor(xT[:, m, :], xT[:, m, :], PB[bank][:, :], ALU.add), tp, txs[m])
            free[bank] = [tx]
            if m == 7:
                return tx, last_square(xT[:, m, :], tx)
            return tx, square_in(xT[:, m, :], m == 0, tx, *(ssq_read[0] if m == 0 else []))

        ssq_read[0] = [tS]
        tps = project_group(chs, (hhi, hlo, tm_), (4, 5, 6, 7, 0, 1, 2, 3))
        tx2 = []
        for m in range(4):
            tx, tq = residual(m, m, tps[m], tx1)
            tx2.append(tx)
        for m in range(4, 8):
            b = m
            tp = project("wo2", m, 128, b, (hhi, hlo, tm_))
            if m == 7:
                chs = group([("gt", 0, 128, 0), ("up", 0, 128, 1), ("gt", 1, 128, 2)])
            tx, tq = residual(b, m, tp, tx1)
            tx2.append(tx)
        f6 = fence()
        hs.close()
        ga_.close()
        k2.close()

        ff = ExitStack()
        ahi = sb(ff, "ahi", [128, FFB, S], F32R)
        alo = sb(ff, "alo", [128, FFB, S], F32R)
        hs = ExitStack()
        hhi = sb(hs, "hhi4", [128, NB, S], F32R)
        hlo = sb(hs, "hlo4", [128, NB, S], F32R)
        te, tm = rsqrt_rows(7, D, eps_c, rsb[:, :], square_in.tok, 0.0, None, tx1[-1], *tqg.values(), more=tq[0])
        sqfree[tq[1]] = [tm]
        ssq_read[0] = [tm]
        th, reads = norm_split(lambda b: vc(V_FN + b), te, tx2, hhi, hlo, f6, None,
                               lambda: chs.extend(group([("up", 1, 128, 3)])))
        h3 = (hhi, hlo, th)
        preload(SILU)
        tps = project_group(chs, h3, hi=norm_split.hi)
        sfree = [[th[-1]], [th[-1]]]
        tact = []
        for j in range(FFB):
            i = j % 2
            b0, b1 = 2 * (j % 4), 2 * (j % 4) + 1
            tp = tps[2 * j] if j < 2 else project("gt", j, 128, b0, h3)
            s_ = tmpf[:, i, :]
            ts = A(lambda e, s_=s_, b0=b0: e.activation(s_, PB[b0][:, :], ACT.Silu), tp, *sfree[i])
            free[b0] = [ts]
            tp = tps[2 * j + 1] if j < 2 else project("up", j, 128, b1, h3)
            t1 = V(lambda e, s_=s_, b1=b1: e.tensor_tensor(s_, s_, PB[b1][:, :], ALU.mult), ts, tp)
            free[b1] = [t1]
            tl = split(s_, ahi[:, j, :], alo[:, j, :], t1, *f6)
            sfree[i] = [tl]
            tact.append(tl)
        f7 = fence()
        hs.close()
        pl = ExitStack()
        hhi = sb(pl, "hhi5", [128, NB, S], F32R)
        hlo = sb(pl, "hlo5", [128, NB, S], F32R)
        plr = sb(pl, "plr", [128, 4, S])
        tPL = [GDMA(f"pl{m}", plr[:, m, :], ple[128 * m:128 * m + 128, :], t_ple, *f7) for m in range(4)]
        tx3 = []
        for m in range(8):
            b = 4 + m % 2
            for q in range(3):
                tp = project("dn", 3 * m + q, 128, b, (ahi, alo, tact), kbs=range(8 * q, min(8 * q + 8, FFB)),
                             start=q == 0, stop=q == 2)
            if m == 0:
                preload(EXPLN)
            if m == 7:
                chs = group([("pg", i, 128, i) for i in range(3)])
            tx, tq = residual(b, m, tp, tx2)
            tx3.append(tx)

        te, tm = rsqrt_rows(7, D, eps_c, rsb[:, :], square_in.tok, 0.0, None, reads[-1], more=tq[0])
        sqfree[tq[1]] = [tm]
        ssq_read[0] = [tm]
        th, reads = norm_split(lambda b: vc(V_PN + b), te, tx3, hhi, hlo, f7, None,
                               lambda: chs.extend(group([("pg", 3, 128, 3)])))
        preload(SILU)
        tps = project_group(chs, (hhi, hlo, th), hi=norm_split.hi)
        tx4 = []
        sfree = [[th[-1]], [th[-1]]]
        tq = None

        def embed(m):
            b, i = m, m % 2
            s_ = tmpf[:, i, :]
            t1 = A(lambda e: e.activation(s_, PB[b][:, :], ACT.Tanh, scale=0.5), tps[m], *sfree[i])
            free[b] = [t1]
            t1 = V(lambda e: e.scalar_tensor_tensor(s_, s_, 1.0, plr[:, m % 4, :], ALU.add, ALU.mult), t1, tPL[m])
            if m < 4:
                tPL.append(DMA(f"pl{m + 4}", plr[:, m, :], ple[128 * m + 512:128 * m + 640, :], t1))
            tx = V(lambda e: e.tensor_tensor(xT[:, m, :], xT[:, m, :], s_, ALU.add), t1, tx3[m])
            sfree[i] = [tx]
            tx4.append(tx)
            return last_square(xT[:, m, :], tx) if m == 7 else \
                square_in(xT[:, m, :], m == 0, tx, *(ssq_read[0] if m == 0 else []))

        for m in range(4):
            embed(m)
            tps.append(project("pg", 4 + m, 128, 4 + m, (hhi, hlo, th)))
        for m in range(4, 8):
            tq = embed(m)
        for m in range(2):
            tx4[m] = A(lambda e, m=m: e.activation(xT[:, m, :], xT[:, m, :], ACT.Copy, scale=vc(V_LN + m)), tx4[m])
        preload(EXPLN)
        te, tm = rsqrt_rows(7, D, eps_c, rsb[:, :], square_in.tok, 0.0, None, reads[-1], more=tq[0])
        sqfree[tq[1]] = [tm]
        t_out = []
        for m in (0, 2, 3, 4, 1, 5, 6, 7):
            if m < 2:
                t1 = G(lambda e, m=m: e.tensor_tensor(xT[:, m, :], xT[:, m, :], rsb[:, :], ALU.mult), te, tx4[m])
                t_out.append(DMA(f"o{m}", out_d[m * 128:m * 128 + 128, :], xT[:, m, :], t1))
                continue
            t1 = V(lambda e, m=m: e.scalar_tensor_tensor(xT[:, m, :], xT[:, m, :], vc(V_LN + m), rsb[:, :],
                                                         ALU.mult, ALU.mult), te, tx4[m])
            t_out.append(DMA(f"o{m}", out_d[m * 128:m * 128 + 128, :], xT[:, m, :], t1))
        assert st.next == len(PLAN)
        pl.close()
        ff.close()

        emit(t_out)

def constants():
    i = np.arange(128)
    ii, jj = i[:, None], i[None, :]
    eye = np.eye(128, dtype=np.float32)
    cst = np.zeros((128, NCST), np.float32)
    cst[:, O_IDENT:O_IDENT + 128] = eye
    cst[:, O_NIDENT:O_NIDENT + 128] = -eye
    cst[:, O_ONES:O_ONES + 128] = 1
    cst[:, O_NONES:O_NONES + 128] = -1
    cst[:, O_TRI:O_TRI + 128] = np.where(ii >= jj, -1, 0)
    inv = np.float32(10000.0) ** (-np.arange(0, 32, 2, dtype=np.float32) / np.float32(32))
    cst[:, O_COL] = inv[i % 16]
    cst[:, O_COL + 1] = np.where(i % 32 < 16, -1, 1)
    cst[:, O_COL + 2] = np.where(i < 32, 1, -1)
    rc = np.zeros((128, NRC), np.float32)
    rc[:, R_MC:R_MC + 128] = np.where(jj <= ii, 0, NEG)
    rc[:, R_MS:R_MS + 128] = np.where(ii < jj, 0, NEG)
    rc[:, R_MG:R_MG + 128] = np.where((ii // 64 == jj // 64) & (jj >= ii), 0, NEG)
    gc = np.zeros((128, NGC), np.float32)
    for lv in range(1, 6):
        s = 1 << lv
        lower = (ii // (2 * s) == jj // (2 * s)) & (ii % (2 * s) >= s) & (jj % (2 * s) < s)
        gc[:, G_LM + 128 * (lv - 1):G_LM + 128 * lv] = lower
    gc[:, G_LT:G_LT + 128] = (ii // 2 == jj // 2) & (jj % 2 == 1) & (ii % 2 == 0)
    rm = np.ones((96, 512), np.float32)
    rm[0:64, ::64] = 0
    return cst, rc, gc, rm


def blocks_of(w, cols, k0=0, kb=None):
    kb = w.shape[0] // 128 - k0 if kb is None else kb
    part = w[128 * k0:128 * (k0 + kb), cols]
    return np.ascontiguousarray(part.reshape(kb, 128, -1).transpose(1, 0, 2)).reshape(-1)


def weights(a):
    w_in, w_in2 = a["w_in"][0], a["w_in_2"][0]
    at = np.cumsum([0, 512, 512, 512, 512, 384, 256, 32, 512, 1024, 1024])
    base = dict(zip(("sbq", "sbk", "sbv", "sz", "cq", "ckv", "kr", "mz", "ga", "gb"), at))
    at2 = np.cumsum([0, 1536, 512, 4, 4, 512, 512, 512, 8])
    base2 = dict(zip(("gqkv", "gz", "g_a", "g_b", "fq", "fk", "fv", "ff"), at2))
    kr = np.zeros((1024, 96), np.float32)
    kr[:, 64:96] = w_in[:, base["kr"]:base["kr"] + 32]
    small = np.zeros((1024, 96), np.float32)
    small[:, 0:4] = w_in2[:, base2["g_a"]:base2["g_a"] + 4]
    small[:, 32:36] = w_in2[:, base2["g_b"]:base2["g_b"] + 4]
    small[:, 64:72] = w_in2[:, base2["ff"]:base2["ff"] + 8]
    ukv = a["w_ukv"][0].reshape(256, 8, 128)
    uk = np.ascontiguousarray(ukv[:, :, 0:64]).reshape(256, 512)
    uv = np.ascontiguousarray(ukv[:, :, 64:128]).reshape(256, 512)
    ada = np.ascontiguousarray(a["w_ada"][0].T)
    every = slice(None)
    out = []
    for name, i, kb, n in chunks():
        c = slice(128 * i, 128 * i + 128)
        if name == "ada":
            out.append(ada[c, :].reshape(-1))
        elif name == "kr":
            out.append(blocks_of(kr, every))
        elif name == "small":
            out.append(blocks_of(small, every))
        elif name in ("sbv", "fv"):
            w, b = (w_in, base["sbv"]) if name == "sbv" else (w_in2, base2["fv"])
            out.append(blocks_of(w, slice(b, b + 512), 2 * i, 2))
        elif name in base:
            out.append(blocks_of(w_in, slice(base[name] + 128 * i, base[name] + 128 * i + 128)))
        elif name in base2:
            out.append(blocks_of(w_in2, slice(base2[name] + 128 * i, base2[name] + 128 * i + 128)))
        elif name == "uq":
            out.append(blocks_of(a["w_uq"][0], slice(288 * i, 288 * i + n)))
        elif name == "uk":
            out.append(blocks_of(uk, every))
        elif name == "uv":
            out.append(blocks_of(uv, every))
        elif name in ("wa", "wb"):
            out.append(blocks_of(a["w_branch_" + name[1]][0], slice(256 * i, 256 * i + 256)))
        elif name == "wo":
            out.append(blocks_of(a["w_out"][0], c))
        elif name == "wo2":
            out.append(blocks_of(a["w_out_2"][0], c))
        elif name == "gt":
            out.append(blocks_of(a["w_gate_up_2"][0], c))
        elif name == "up":
            out.append(blocks_of(a["w_gate_up_2"][0], slice(128 * (FFB + i), 128 * (FFB + i) + 128)))
        elif name == "dn":
            m, q = i // 3, i % 3
            out.append(blocks_of(a["w_down_2"][0], slice(128 * m, 128 * m + 128), 8 * q, kb))
        elif name == "pp":
            out.append(blocks_of(a["w_ple_proj_2"][0], slice(512 * i, 512 * i + 512)))
        elif name == "pg":
            out.append(blocks_of(a["w_ple_gate_2"][0], c))
        assert out[-1].size == 128 * kb * n, (name, i)
    return np.concatenate(out)


def vectors(a):
    v = np.zeros((128, NVEC), np.float32)

    def put(at, x):
        n = x.size // 128
        v[:, at:at + n] = x.reshape(n, 128).T

    put(V_NG, a["norm_gain"])
    put(V_BA, a["b_ada"])
    put(V_AN, a["attn_norm_w_2"])
    put(V_FN, a["ffn_norm_w_2"])
    put(V_PN, a["ple_norm_w_2"])
    put(V_LN, a["final_norm_w_2"])
    put(V_QN, a["q_norm_gain"])
    put(V_KN, a["kv_norm_gain"])
    put(V_GN, a["gdn_norm_w_2"])
    put(V_N1, a["final_norm_gain"])
    v[:, V_CV:V_CV + 48] = a["conv_w_2"][0].reshape(4, 12, 128).transpose(2, 1, 0).reshape(128, 48)
    v[0:4, V_DT] = a["dt_bias_2"][0]
    v[64:72, V_FB] = a["fox_f_bias_2"][0]
    v[0:4, V_AL] = a["a_log_2"][0]
    return v


def layout(inputs):
    a = {k: np.asarray(v) for k, v in inputs.items()}
    cst, rc, gc, rm = constants()
    return {
        "w_all": weights(a), "cst_d": cst, "rc_d": rc, "gc_d": gc, "rm_d": rm, "vec_d": vectors(a),
        "x_d": np.ascontiguousarray(a["x"][0].T), "c_d": np.ascontiguousarray(a["c"]),
        "pos_d": np.ascontiguousarray(a["positions"]),
        "ada_d": np.ascontiguousarray(a["w_ada"][0].T[0:2048]), "p_d": np.ascontiguousarray(a["p_2"][0, 0].T),
    }


def kernel(**inputs):
    import concourse.bacc as bacc
    from concourse.bass_utils import run_bass_kernel_spmd

    nc = bacc.Bacc("TRN2", target_bir_lowering=False, num_devices=1)
    arrays = layout(inputs)
    args = [nc.dram_tensor(n, x.shape, mybir.dt.from_np(x.dtype), kind="ExternalInput").ap() for n, x in arrays.items()]
    out = nc.dram_tensor("out_d", (D, S), F32, kind="ExternalOutput").ap()
    build(nc, *args, out)
    r = run_bass_kernel_spmd(nc, [arrays], core_ids=[0])
    return np.ascontiguousarray(r.results[0]["out_d"].T).reshape(1, S, D)
```
